# Optimizing a Trainium2 kernel written in Bass

```python
import math
import jax, jax.numpy as jnp
from jax import lax
import numpy as np

D_MODEL = 1024
BATCH = 1
SEQ = 1024
DEPTH = 2

N_EVEN = (DEPTH + 1) // 2
N_ODD = DEPTH // 2
HEAD_DIM = 64
EPS = 1e-6

A_WIDTH = D_MODEL // 2
A_EXPAND = 128
A_HEADS = A_WIDTH // A_EXPAND
A_HEAD_V = A_WIDTH // A_HEADS
A_CHUNK = 32

B_WIDTH = D_MODEL - A_WIDTH
B_HEADS = B_WIDTH // HEAD_DIM
DILATED_PATTERNS = ((128, 1), (512, 4), (2048, 16))
B_QBLOCK = 128
EVEN_IN = 4 * A_WIDTH + 3 * B_WIDTH

C_HEADS = D_MODEL // HEAD_DIM
C_KV_HEADS = 4
C_GROUP = C_HEADS // C_KV_HEADS
C_KV_WIDTH = C_KV_HEADS * HEAD_DIM
CMP_LEN = 32
CMP_STRIDE = 16
CMP_HIDDEN = 2 * HEAD_DIM
SLC_BLOCK = 64
SLC_TOPN = 8
SLC_QBLOCK = 32
WIN = 512
WIN_QBLOCK = 128
ODD_IN = D_MODEL + 6 * C_KV_WIDTH + 3 * C_HEADS

D_FF = -(-8 * D_MODEL // (3 * 256)) * 256

kernel_name = 'hybrid_hgrn2_dilated_nsa_trunk'

def rms_norm(x, g):
    xf = x.astype(jnp.float32)
    y = xf * lax.rsqrt(jnp.mean(xf * xf, axis=-1, keepdims=True) + EPS)
    return (y * g.astype(jnp.float32)).astype(x.dtype)

def alibi_slopes(n):
    return 2.0 ** (-8.0 * jnp.arange(1, n + 1, dtype=jnp.float32) / n)

def hgrn2(q, f_logit, v, gate, lb, o_gain):
    Bn, S, _ = q.shape
    f32 = jnp.float32
    f = lb + (1.0 - lb) * jax.nn.sigmoid(f_logit.astype(f32))
    log_f = jnp.log(f)
    k = 1.0 - f
    q = jax.nn.silu(q.astype(f32))
    v = v.astype(f32)
    n_chunk = S // A_CHUNK

    def chunks(t, d):
        return t.reshape(Bn, n_chunk, A_CHUNK, A_HEADS, d).transpose(1, 0, 3, 2, 4)

    qc, kc, lc = chunks(q, A_EXPAND), chunks(k, A_EXPAND), chunks(log_f, A_EXPAND)
    vc = chunks(v, A_HEAD_V)
    causal = jnp.tril(jnp.ones((A_CHUNK, A_CHUNK), dtype=bool))[:, :, None]

    def step(state, inp):
        qb, kb, vb, lf = inp
        b = jnp.cumsum(lf, axis=-2)
        b_last = b[..., -1:, :]
        diff = b[..., :, None, :] - b[..., None, :, :]
        decay = jnp.exp(jnp.where(causal, diff, -jnp.inf))
        scores = jnp.einsum('bhtk,bhsk,bhtsk->bhts', qb, kb, decay)
        out = (jnp.einsum('bhts,bhsv->bhtv', scores, vb)
               + jnp.einsum('bhtk,bhkv->bhtv', qb * jnp.exp(b), state))
        new_state = (jnp.exp(b_last)[..., 0, :, None] * state
                     + jnp.einsum('bhsk,bhsv->bhkv', kb * jnp.exp(b_last - b), vb))
        return new_state, out

    state0 = jnp.zeros((Bn, A_HEADS, A_EXPAND, A_HEAD_V), f32)
    _, o = lax.scan(step, state0, (qc, kc, vc, lc))
    o = o.transpose(1, 0, 3, 2, 4).reshape(Bn, S, A_HEADS, A_HEAD_V)
    o = o * lax.rsqrt(jnp.mean(o * o, axis=-1, keepdims=True) + EPS)
    return o.reshape(Bn, S, A_WIDTH) * o_gain.astype(f32) * jax.nn.silu(gate.astype(f32))

def dilated_branch(q, k, v, window, dilation, slopes):
    Bn, H, S, dh = q.shape
    L = S // dilation
    w = window // dilation
    qb = min(B_QBLOCK, L)
    nb = L // qb

    def sub(t):
        return t.reshape(Bn, H, L, dilation, dh).transpose(0, 1, 3, 2, 4)

    pad = ((0, 0), (0, 0), (0, 0), (w, 0), (0, 0))
    kp = jnp.pad(sub(k), pad)
    vp = jnp.pad(sub(v), pad)
    kidx = jnp.arange(nb)[:, None] * qb + jnp.arange(qb + w)[None, :]
    k_band = kp[:, :, :, kidx]
    v_band = vp[:, :, :, kidx]
    q_blk = sub(q).reshape(Bn, H, dilation, nb, qb, dh)
    j = jnp.arange(qb)[:, None] - jnp.arange(qb + w)[None, :] + w
    valid = (j >= 0) & (j <= w) & (kidx[:, None, :] >= w)
    s = (jnp.einsum('bhrnqd,bhrnkd->bhrnqk', q_blk, k_band) * dh ** -0.5
         - slopes[:, None, None, None, None] * (j * dilation).astype(jnp.float32))
    s = jnp.where(valid, s, -jnp.inf)
    m = jnp.max(s, axis=-1, keepdims=True)
    e = jnp.exp(s - m)
    l = jnp.sum(e, axis=-1, keepdims=True)
    o = jnp.einsum('bhrnqk,bhrnkd->bhrnqd', e, v_band) / l
    lse = (m + jnp.log(l))[..., 0]
    o = o.reshape(Bn, H, dilation, L, dh).transpose(0, 1, 3, 2, 4).reshape(Bn, H, S, dh)
    lse = lse.reshape(Bn, H, dilation, L).transpose(0, 1, 3, 2).reshape(Bn, H, S)
    return o, lse

def hybrid_mixer(h, w_in, lb, o_gain, q_gain, k_gain, w_out):
    Bn, S, _ = h.shape
    dt = h.dtype
    proj = h @ w_in
    split_at = [A_WIDTH * i for i in range(1, 5)] + [4 * A_WIDTH + B_WIDTH * i for i in range(1, 3)]
    a_q, a_f, a_i, a_g, b_q, b_k, b_v = jnp.split(proj, split_at, axis=-1)
    a_out = hgrn2(a_q, a_f, a_i, a_g, lb, o_gain)

    def heads(t):
        return t.reshape(Bn, S, B_HEADS, HEAD_DIM).transpose(0, 2, 1, 3).astype(jnp.float32)

    q = rms_norm(heads(b_q), q_gain)
    k = rms_norm(heads(b_k), k_gain)
    v = heads(b_v)
    slopes = alibi_slopes(B_HEADS)
    outs, lses = zip(*[dilated_branch(q, k, v, win, dil, slopes) for (win, dil) in DILATED_PATTERNS])
    wts = jax.nn.softmax(jnp.stack(lses), axis=0)
    b_out = jnp.einsum('nbhs,nbhsd->bshd', wts, jnp.stack(outs)).reshape(Bn, S, B_WIDTH)
    mixed = jnp.concatenate([a_out, b_out], axis=-1).astype(dt)
    return mixed @ w_out

def nsa_mixer(h, w_in, q_gain, k_gain, cmp_pe, cmp_w1, cmp_w2, w_out):
    Bn, S, _ = h.shape
    dt = h.dtype
    f32 = jnp.float32
    scale = HEAD_DIM ** -0.5
    proj = h @ w_in
    q, kc, vc, ks, vs, kw, vw, g = jnp.split(
        proj, [D_MODEL + C_KV_WIDTH * i for i in range(7)], axis=-1)
    q = rms_norm(q.reshape(Bn, S, C_KV_HEADS, C_GROUP, HEAD_DIM)
                 .transpose(0, 2, 3, 1, 4).astype(f32), q_gain)

    def kv_heads(t):
        return t.reshape(Bn, S, C_KV_HEADS, HEAD_DIM).transpose(0, 2, 1, 3).astype(f32)

    kc, vc, ks, vs, kw, vw = (kv_heads(t) for t in (kc, vc, ks, vs, kw, vw))
    ks = rms_norm(ks, k_gain[1])
    kw = rms_norm(kw, k_gain[2])
    gates = jax.nn.sigmoid(g.astype(f32)).reshape(Bn, S, 3, C_KV_HEADS, C_GROUP).transpose(2, 0, 3, 4, 1)[..., None]
    slopes = alibi_slopes(C_HEADS).reshape(C_KV_HEADS, C_GROUP)
    pos = jnp.arange(S)

    n_cmp = (S - CMP_LEN) // CMP_STRIDE + 1
    cidx = jnp.arange(n_cmp)[:, None] * CMP_STRIDE + jnp.arange(CMP_LEN)[None, :]

    def compress(t, pe, w1, w2):
        blocks = t[:, :, cidx] + pe.astype(f32)
        blocks = blocks.reshape(Bn, C_KV_HEADS, n_cmp, CMP_LEN * HEAD_DIM)
        return jax.nn.silu(blocks @ w1.astype(f32)) @ w2.astype(f32)

    k_cmp = rms_norm(compress(kc, cmp_pe[0], cmp_w1[0], cmp_w2[0]), k_gain[0])
    v_cmp = compress(vc, cmp_pe[1], cmp_w1[1], cmp_w2[1])
    dist_c = (pos[:, None] - cidx[:, -1][None, :]).astype(f32)
    s_c = (jnp.einsum('bgjtd,bgnd->bgjtn', q, k_cmp) * scale
           - slopes[None, :, :, None, None] * dist_c)
    s_c = jnp.where(dist_c >= 0, s_c, -jnp.inf)
    m_c = jnp.max(s_c, axis=-1, keepdims=True)
    e_c = jnp.exp(s_c - jnp.where(jnp.isfinite(m_c), m_c, 0.0))
    l_c = jnp.sum(e_c, axis=-1, keepdims=True)
    p_c = e_c / jnp.where(l_c > 0, l_c, 1.0)
    o_cmp = jnp.einsum('bgjtn,bgnd->bgjtd', p_c, v_cmp)

    n_slc = S // SLC_BLOCK
    blk = jnp.arange(n_slc)
    c_start = cidx[:, 0]
    overlap = ((c_start[:, None] < (blk[None, :] + 1) * SLC_BLOCK)
               & (c_start[:, None] + CMP_LEN > blk[None, :] * SLC_BLOCK)).astype(f32)
    importance = jnp.einsum('bgjtn,nm->bgtm', p_c, overlap)
    cur = (pos // SLC_BLOCK)[:, None]
    forced = (blk[None, :] == 0) | (blk[None, :] == cur) | (blk[None, :] == cur - 1)
    score = jnp.where(blk[None, :] > cur, -jnp.inf, jnp.where(forced, jnp.inf, importance))
    n_top = min(SLC_TOPN, n_slc)
    top_s, top_i = lax.top_k(score, n_top)
    top_ok = top_s > -jnp.inf
    k_blocks = ks.reshape(Bn, C_KV_HEADS, n_slc, SLC_BLOCK, HEAD_DIM)
    v_blocks = vs.reshape(Bn, C_KV_HEADS, n_slc, SLC_BLOCK, HEAD_DIM)
    gather = jax.vmap(jax.vmap(lambda tb, idx: tb[idx]))
    n_sel_keys = n_top * SLC_BLOCK

    def sel_block(args):
        qb, ib, okb, tb = args
        kg = gather(k_blocks, ib).reshape(Bn, C_KV_HEADS, SLC_QBLOCK, n_sel_keys, HEAD_DIM)
        vg = gather(v_blocks, ib).reshape(Bn, C_KV_HEADS, SLC_QBLOCK, n_sel_keys, HEAD_DIM)
        kpos = (ib[..., None] * SLC_BLOCK + jnp.arange(SLC_BLOCK)).reshape(Bn, C_KV_HEADS, SLC_QBLOCK, n_sel_keys)
        ok = jnp.broadcast_to(okb[..., None], ib.shape + (SLC_BLOCK,)).reshape(Bn, C_KV_HEADS, SLC_QBLOCK, n_sel_keys)
        dist = tb[:, None] - kpos
        valid = (dist >= 0) & ok
        s = (jnp.einsum('bgjqd,bgqmd->bgjqm', qb, kg) * scale
             - slopes[None, :, :, None, None] * dist[:, :, None].astype(f32))
        s = jnp.where(valid[:, :, None], s, -jnp.inf)
        return jnp.einsum('bgjqm,bgqmd->bgjqd', jax.nn.softmax(s, axis=-1), vg)

    n_qb = S // SLC_QBLOCK
    q_r = q.reshape(Bn, C_KV_HEADS, C_GROUP, n_qb, SLC_QBLOCK, HEAD_DIM).transpose(3, 0, 1, 2, 4, 5)
    i_r = top_i.reshape(Bn, C_KV_HEADS, n_qb, SLC_QBLOCK, n_top).transpose(2, 0, 1, 3, 4)
    ok_r = top_ok.reshape(Bn, C_KV_HEADS, n_qb, SLC_QBLOCK, n_top).transpose(2, 0, 1, 3, 4)
    t_r = pos.reshape(n_qb, SLC_QBLOCK)
    o_slc = lax.map(sel_block, (q_r, i_r, ok_r, t_r)).transpose(1, 2, 3, 0, 4, 5).reshape(
        Bn, C_KV_HEADS, C_GROUP, S, HEAD_DIM)

    pad = ((0, 0), (0, 0), (WIN, 0), (0, 0))
    kw_p = jnp.pad(kw, pad)
    vw_p = jnp.pad(vw, pad)
    band = jnp.arange(WIN_QBLOCK + WIN)

    def win_block(args):
        qb, start = args
        kb = lax.dynamic_slice_in_dim(kw_p, start, WIN_QBLOCK + WIN, axis=2)
        vb = lax.dynamic_slice_in_dim(vw_p, start, WIN_QBLOCK + WIN, axis=2)
        qpos = start + jnp.arange(WIN_QBLOCK)
        kpos = start - WIN + band
        dist = qpos[:, None] - kpos[None, :]
        valid = (dist >= 0) & (dist < WIN) & (kpos[None, :] >= 0)
        s = (jnp.einsum('bgjqd,bgkd->bgjqk', qb, kb) * scale
             - slopes[None, :, :, None, None] * dist.astype(f32))
        s = jnp.where(valid, s, -jnp.inf)
        return jnp.einsum('bgjqk,bgkd->bgjqd', jax.nn.softmax(s, axis=-1), vb)

    n_wb = S // WIN_QBLOCK
    q_w = q.reshape(Bn, C_KV_HEADS, C_GROUP, n_wb, WIN_QBLOCK, HEAD_DIM).transpose(3, 0, 1, 2, 4, 5)
    starts = jnp.arange(n_wb) * WIN_QBLOCK
    o_win = lax.map(win_block, (q_w, starts)).transpose(1, 2, 3, 0, 4, 5).reshape(
        Bn, C_KV_HEADS, C_GROUP, S, HEAD_DIM)

    o = gates[0] * o_cmp + gates[1] * o_slc + gates[2] * o_win
    o = o.transpose(0, 3, 1, 2, 4).reshape(Bn, S, D_MODEL).astype(dt)
    return o @ w_out

def swiglu(h, w_gate, w_up, w_down):
    return (jax.nn.silu(h @ w_gate) * (h @ w_up)) @ w_down

def setup_inputs(seed: int = 0) -> dict:
    key = jax.random.key(seed)
    ks = jax.random.split(key, 20)

    def nrm(k, shape, scale):
        return jax.random.normal(k, shape, jnp.float32) * scale

    def gain(k, shape):
        return 1.0 + 0.02 * jax.random.normal(k, shape, jnp.float32)

    return {
        'x': nrm(ks[0], (BATCH, SEQ, D_MODEL), 1.0),
        'attn_norm': gain(ks[1], (DEPTH, D_MODEL)),
        'ffn_norm': gain(ks[2], (DEPTH, D_MODEL)),
        'hy_w_in': nrm(ks[3], (N_EVEN, D_MODEL, EVEN_IN), D_MODEL ** -0.5),
        'hy_lb_logits': nrm(ks[4], (N_EVEN, A_WIDTH), 0.1),
        'hy_o_gain': gain(ks[5], (N_EVEN, A_WIDTH)),
        'hy_q_gain': gain(ks[6], (N_EVEN, HEAD_DIM)),
        'hy_k_gain': gain(ks[7], (N_EVEN, HEAD_DIM)),
        'hy_w_out': nrm(ks[8], (N_EVEN, D_MODEL, D_MODEL), D_MODEL ** -0.5),
        'nsa_w_in': nrm(ks[9], (N_ODD, D_MODEL, ODD_IN), D_MODEL ** -0.5),
        'nsa_q_gain': gain(ks[10], (N_ODD, HEAD_DIM)),
        'nsa_k_gain': gain(ks[11], (N_ODD, 3, HEAD_DIM)),
        'nsa_cmp_pe': nrm(ks[12], (N_ODD, 2, CMP_LEN, HEAD_DIM), 0.1),
        'nsa_cmp_w1': nrm(ks[13], (N_ODD, 2, CMP_LEN * HEAD_DIM, CMP_HIDDEN), (CMP_LEN * HEAD_DIM) ** -0.5),
        'nsa_cmp_w2': nrm(ks[14], (N_ODD, 2, CMP_HIDDEN, HEAD_DIM), CMP_HIDDEN ** -0.5),
        'nsa_w_out': nrm(ks[15], (N_ODD, D_MODEL, D_MODEL), D_MODEL ** -0.5),
        'ffn_w_gate': nrm(ks[16], (DEPTH, D_MODEL, D_FF), D_MODEL ** -0.5),
        'ffn_w_up': nrm(ks[17], (DEPTH, D_MODEL, D_FF), D_MODEL ** -0.5),
        'ffn_w_down': nrm(ks[18], (DEPTH, D_FF, D_MODEL), D_FF ** -0.5),
    }

def reference(x, attn_norm, ffn_norm, hy_w_in, hy_lb_logits, hy_o_gain, hy_q_gain, hy_k_gain, hy_w_out,
              nsa_w_in, nsa_q_gain, nsa_k_gain, nsa_cmp_pe, nsa_cmp_w1, nsa_cmp_w2, nsa_w_out,
              ffn_w_gate, ffn_w_up, ffn_w_down):
    p_lb = jax.nn.softmax(hy_lb_logits.astype(jnp.float32), axis=0)
    lower_bounds = jnp.cumsum(p_lb, axis=0) - p_lb[0]
    for layer in range(DEPTH):
        h = rms_norm(x, attn_norm[layer])
        i = layer // 2
        if layer % 2 == 0:
            x = x + hybrid_mixer(h, hy_w_in[i], lower_bounds[i], hy_o_gain[i], hy_q_gain[i],
                                 hy_k_gain[i], hy_w_out[i])
        else:
            x = x + nsa_mixer(h, nsa_w_in[i], nsa_q_gain[i], nsa_k_gain[i], nsa_cmp_pe[i],
                              nsa_cmp_w1[i], nsa_cmp_w2[i], nsa_w_out[i])
        h = rms_norm(x, ffn_norm[layer])
        x = x + swiglu(h, ffn_w_gate[layer], ffn_w_up[layer], ffn_w_down[layer])
    return x


_drawn_inputs = setup_inputs


def setup_inputs(seed=0):
    import zlib

    import numpy as np

    out = dict(_drawn_inputs(seed))
    spreads = {}
    factors = {'attn_norm': 3.107,
     'ffn_norm': 2.864,
     'hy_o_gain': 5.926,
     'hy_q_gain': 8.0,
     'hy_k_gain': 8.0,
     'nsa_q_gain': 8.0,
     'nsa_k_gain': 8.0}
    for name, (base, spread) in spreads.items():
        noise = np.random.default_rng([zlib.crc32(name.encode()), seed]).standard_normal(out[name].shape)
        drawn = base * np.exp(spread * noise) if base else spread * noise
        out[name] = __import__('jax').numpy.asarray(drawn.astype(out[name].dtype))
    for name, factor in factors.items():
        out[name] = (out[name] * factor).astype(out[name].dtype)
    return out
```

```python
import math
from contextlib import ExitStack

import concourse.bass as bass
import numpy as np
from concourse import mybir

F32 = mybir.dt.float32
I32 = mybir.dt.int32
ALU = mybir.AluOpType
ACT = mybir.ActivationFunctionType
AX = mybir.AxisListType

P = 128
SEQ = 1024
DM = 1024
TT = SEQ // P
KD = DM // P
HD = 64
HA = HD + 2
EPS = 1e-6
NEG = -1e30
BANK = 512

A_WIDTH = DM // 2
A_HEADS = 4
B_HEADS = 8
EVEN_IN = 4 * A_WIDTH + 3 * (DM - A_WIDTH)

C_HEADS = 16
KV_HEADS = 4
GROUP = C_HEADS // KV_HEADS
KV_W = KV_HEADS * HD
ODD_IN = DM + 6 * KV_W + 3 * C_HEADS
CMP_LEN, CMP_STRIDE, CMP_HIDDEN = 32, 16, 2 * HD
N_CMP = (SEQ - CMP_LEN) // CMP_STRIDE + 1
CMP_PAD = 64
SLC = 64
N_SLC = SEQ // SLC
TOPN = 8
WIN = 512
D_FF = -(-8 * DM // (3 * 256)) * 256


class Stage:

    def __init__(self, nc, name):
        self.nc, self.name, self.ctx, self.sems = nc, name, ExitStack(), []

    def __enter__(self):
        self.ctx.__enter__()
        return self

    def __exit__(self, *e):
        done = self.ctx.__exit__(*e)
        if e[0] is None:
            self.nc.clear_and_free_semaphores(self.sems)
            self.nc.all_engine_barrier()
        return done

    def sb(self, name, shape, dt=F32):
        return self.ctx.enter_context(self.nc.sbuf_tensor(f"{self.name}_{name}", shape, dt))

    def ps(self, name, shape, dt=F32):
        return self.ctx.enter_context(self.nc.psum_tensor(f"{self.name}_{name}", shape, dt))

    def sem(self, name):
        self.sems.append(self.nc.alloc_semaphore(f"{self.name}_{name}"))
        return self.sems[-1]

    def block(self):
        return self.ctx.enter_context(self.nc.Block())


def bcast(ap, n):
    return ap.to_broadcast(list(ap.shape[:-1]) + [n])



def load_stage(nc, x, x_sb, ident):
    with Stage(nc, "load") as st:
        x_in, zeroed = st.sem("x_in"), st.sem("zeroed")
        block = st.block()

        @block.sync
        def _(sp):
            sp.dma_start(x_sb[:], x.rearrange("o (t p) d -> p (o t) d", p=P)).then_inc(x_in, 16)
            sp.wait_ge(x_in, 16)

        @block.gpsimd
        def _(pool):
            nc.gpsimd.memset(ident[:], 0.0).then_inc(zeroed, 1)
            pool.wait_ge(zeroed, 1)
            nc.gpsimd.affine_select(out=ident[:], in_=ident[:], compare_op=ALU.not_equal, fill=1.0, base=0,
                                    pattern=[[-1, P]], channel_multiplier=1)


def transpose_stage(nc, name, src, dst, gain_parts, ident, norm):
    with Stage(nc, name) as st:
        gain = st.sb("gain", [P, KD])
        sq = st.sb("sq", [P, 2, DM])
        h = st.sb("h", [P, 2, DM])
        ss = st.sb("ss", [P, TT])
        ms = st.sb("ms", [P, TT])
        root = st.sb("root", [P, TT])
        rstd = st.sb("rstd", [P, TT])
        tr = st.ps("tr", [P, 4, BANK])
        gain_in, gain_set = st.sem("gain_in"), st.sem("gain_set")
        ss_done, ms_done, root_done, rstd_done = (st.sem(n) for n in ("ss_done", "ms_done", "root_done", "rstd_done"))
        h_done, tr_done, out_done = st.sem("h_done"), st.sem("tr_done"), st.sem("out_done")
        n_gain = sum(g is not None for g, _, _ in gain_parts)
        block = st.block()

        @block.sync
        def _(sp):
            sp.wait_ge(gain_set, 1)
            with nc.allow_non_contiguous_dma(reason="a gain per partition"):
                for g, lo, hi in gain_parts:
                    if g is not None:
                        sp.dma_start(gain[:, lo:hi], g.rearrange("(k p) -> p k", p=P)).then_inc(gain_in, 16)

        @block.gpsimd
        def _(pool):
            nc.gpsimd.memset(gain[:], 1.0).then_inc(gain_set, 1)

        @block.scalar
        def _(act):
            if norm:
                for t in range(TT):
                    if t >= 2:
                        act.wait_ge(ss_done, t - 1)
                    nc.scalar.activation(sq[:, t % 2, :], src[:, t, :], ACT.Square,
                                         accum_out=ss[:, t:t + 1]).then_inc(ss_done, 1)
                act.wait_ge(ms_done, 1)
                nc.scalar.activation(root[:], ms[:], ACT.Sqrt).then_inc(root_done, 1)

        @block.vector
        def _(dve):
            if norm:
                dve.wait_ge(ss_done, TT)
                nc.vector.tensor_scalar(ms[:], ss[:], 1.0 / DM, EPS, ALU.mult, ALU.add).then_inc(ms_done, 1)
                dve.wait_ge(root_done, 1)
                nc.vector.reciprocal(rstd[:], root[:]).then_inc(rstd_done, 1)
                dve.wait_ge(rstd_done, 1)
            for t in range(TT + 1):
                if t < TT and norm:
                    if t >= 2:
                        dve.wait_ge(tr_done, 2 * (t - 1))
                    nc.vector.tensor_scalar(h[:, t % 2, :], src[:, t, :], rstd[:, t:t + 1], None,
                                            ALU.mult).then_inc(h_done, 1)
                if t == 1 and n_gain:
                    dve.wait_ge(gain_in, 16 * n_gain)
                if t == 1:
                    dve.wait_ge(gain_set, 1)
                for half in range(2 if t else 0):
                    n = 2 * (t - 1) + half
                    dve.wait_ge(tr_done, n + 1)
                    k0 = half * 4
                    nc.vector.tensor_tensor(
                        dst[:, k0:k0 + 4, (t - 1) * P:t * P],
                        tr[:, n % 4, :].rearrange("p (k c) -> p k c", c=P),
                        bcast(gain[:, k0:k0 + 4].rearrange("p (k o) -> p k o", o=1), P),
                        ALU.mult).then_inc(out_done, 1)

        @block.tensor
        def _(pe):
            for t in range(TT):
                if norm:
                    pe.wait_ge(h_done, t + 1)
                for half in range(2):
                    n = 2 * t + half
                    if n >= 4:
                        pe.wait_ge(out_done, n - 3)
                    for k in range(4):
                        kk = half * 4 + k
                        rows = h[:, t % 2, :] if norm else src[:, t, :]
                        ins = nc.tensor.transpose(tr[:, n % 4, k * P:(k + 1) * P], rows[:, kk * P:(kk + 1) * P],
                                                  ident[:])
                    ins.then_inc(tr_done, 1)



def linear_stage(nc, name, lhsT, w, kt, width, cols, dst_dram=None, add_to=None):
    n_chunks = cols // width
    pairs, tail = divmod(n_chunks, 2)
    with Stage(nc, name) as st:
        wb = st.sb("w", [P, 2, kt, width])
        stage = st.sb("stage", [P, 2, TT, width]) if dst_dram is not None else None
        acc = st.ps("acc", [P, TT, BANK])
        w_in = [st.sem(f"w_in{s}") for s in range(2)]
        y_out = [st.sem(f"y_out{s}") for s in range(2)] if dst_dram is not None else None
        y_done = [st.sem("y_done_act"), st.sem("y_done_dve")]
        acc_done = st.sem("acc_done")
        wv = w.rearrange("(k p) n -> p k n", p=P)
        wc = wv[:, :, 0:n_chunks * width].rearrange("p k (c n) -> p k c n", n=width)
        by = (lambda t: t % 2) if dst_dram is not None else (lambda t: 1)
        each = (TT // 2, TT // 2) if dst_dram is not None else (0, TT)
        nth = (lambda t: t // 2) if dst_dram is not None else (lambda t: t)
        if dst_dram is not None:
            dv = dst_dram.rearrange("(t p) n -> p t n", p=P)
            dc = dv[:, :, 0:n_chunks * width].rearrange("p t (c n) -> p t c n", n=width)
        if add_to is not None:
            xc = add_to[:, :, :].rearrange("p t (c n) -> p t c n", n=width)
        block = st.block()

        def of_chunk(view, c, s):
            v = view[:, :, 0:2 * (view.shape[2] // 2), :].rearrange("p k (c s) n -> p k c s n", s=2)
            return v[:, :, bass.ds(c, 1), s, :].rearrange("p k o n -> p k (o n)")

        @block.sync
        def _(sp):
            for s in range(min(2, n_chunks)):
                sp.dma_start(wb[:, s, :, :], wc[:, :, s, :]).then_inc(w_in[s], 16)
            if pairs > 1:
                with sp.Fori(0, pairs - 1) as c:
                    for s in range(2):
                        sp.wait_ge(acc_done, c * (2 * TT) + (s + 1) * TT)
                        sp.dma_start(wb[:, s, :, :], of_chunk(wc[:, :, 2:, :], c, s)).then_inc(w_in[s], 16)
            if tail and pairs:
                sp.wait_ge(acc_done, (2 * pairs - 1) * TT)
                sp.dma_start(wb[:, 0, :, :], wc[:, :, n_chunks - 1, :]).then_inc(w_in[0], 16)

        @block.tensor
        def _(pe):
            def chunk(c, s, first):
                pe.wait_ge(w_in[s], (c + 1) * 16)
                for t in range(TT):
                    if not first:
                        pe.wait_ge(y_done[by(t)], (c * 2 + s) * each[by(t)] + nth(t) + 1 - each[by(t)])
                    for k in range(kt):
                        ins = nc.tensor.matmul(acc[:, t, 0:width], lhsT[:, k, t * P:(t + 1) * P], wb[:, s, k, :],
                                               start=k == 0, stop=k == kt - 1)
                    ins.then_inc(acc_done, 1)

            if pairs:
                chunk(0, 0, True)
                chunk(0, 1, False)
            if pairs > 1:
                with pe.Fori(1, pairs) as c:
                    chunk(c, 0, False)
                    chunk(c, 1, False)
            if tail:
                chunk(pairs, 0, pairs == 0)

        def take(eng, who, c, s, first):
            if dst_dram is not None and not first:
                eng.wait_ge(y_out[s], c * 16)
            for t in range(TT):
                if by(t) != who:
                    continue
                eng.wait_ge(acc_done, (c * 2 + s) * TT + t + 1)
                if add_to is not None:
                    xs = of_chunk(xc[:, t:t + 1, :, :], c, s).rearrange("p o n -> p (o n)")
                    nc.vector.tensor_tensor(xs, acc[:, t, 0:width], xs, ALU.add).then_inc(y_done[who], 1)
                elif who == 0:
                    nc.scalar.activation(stage[:, s, t, :], acc[:, t, 0:width], ACT.Copy).then_inc(y_done[0], 1)
                else:
                    nc.vector.tensor_copy(stage[:, s, t, :], acc[:, t, 0:width]).then_inc(y_done[1], 1)

        def all_chunks(eng, step):
            if pairs:
                step(0, 0, True)
                step(0, 1, True)
            if pairs > 1:
                with eng.Fori(1, pairs) as c:
                    step(c, 0, False)
                    step(c, 1, False)
            if tail:
                step(pairs, 0, pairs == 0)

        @block.scalar
        def _(act):
            if dst_dram is not None:
                all_chunks(act, lambda c, s, first: take(act, 0, c, s, first))

        @block.vector
        def _(dve):
            all_chunks(dve, lambda c, s, first: take(dve, 1, c, s, first))

        @block.gpsimd
        def _(pool):
            if dst_dram is None:
                return

            def store(c, s, first):
                for who in range(2):
                    pool.wait_ge(y_done[who], (c * 2 + s + 1) * each[who])
                dst = dc[:, :, n_chunks - 1, :] if isinstance(c, int) and 2 * c + s == n_chunks - 1 else of_chunk(dc, c, s)
                pool.dma_start(dst, stage[:, s, :, :]).then_inc(y_out[s], 16)

            all_chunks(pool, store)
            for s in range(min(2, n_chunks)):
                pool.wait_ge(y_out[s], 16 * (pairs + (tail if s == 0 else 0)))


def ffn_stage(nc, name, hT, w_gate, w_up, actT):
    NF = D_FF // P
    HALF = SEQ // 2
    with Stage(nc, name) as st:
        wg = st.sb("wg", [P, 2, KD, P])
        wu = st.sb("wu", [P, 2, KD, P])
        sg = st.sb("sg", [P, 4, HALF])
        acc = st.ps("acc", [P, 2, 2, 2, BANK])
        w_in = [st.sem(f"w_in{s}") for s in range(2)]
        gate_done, up_done, silu_done, act_done = (st.sem(n) for n in ("gate_done", "up_done", "silu_done", "act_done"))
        gv = w_gate.rearrange("(k p) (c s n) -> p k c s n", p=P, s=2, n=P)
        uv = w_up.rearrange("(k p) (c s n) -> p k c s n", p=P, s=2, n=P)
        av = actT[:, :, :].rearrange("p (c s) n -> p c s n", s=2)
        block = st.block()

        @block.sync
        def _(sp):
            for s in range(2):
                sp.dma_start(wg[:, s, :, :], gv[:, :, 0, s, :]).then_inc(w_in[s], 16)
                sp.dma_start(wu[:, s, :, :], uv[:, :, 0, s, :]).then_inc(w_in[s], 16)
            with sp.Fori(0, NF // 2 - 1) as c:
                for s in range(2):
                    sp.wait_ge(up_done, c * 4 + 2 * (s + 1))
                    for wb, v in ((wg, gv), (wu, uv)):
                        sp.dma_start(wb[:, s, :, :],
                                     v[:, :, 1:, s, :][:, :, bass.ds(c, 1), :].rearrange("p k o n -> p k (o n)"))\
                            .then_inc(w_in[s], 16)

        @block.tensor
        def _(pe):
            def tile(c, s, first):
                pe.wait_ge(w_in[s], (c + 1) * 32)
                for half in range(2):
                    if not first:
                        pe.wait_ge(act_done, c * 4 + 2 * s + half + 1 - 4)
                    for which, wb, done in ((0, wg, gate_done), (1, wu, up_done)):
                        for k in range(KD):
                            ins = nc.tensor.matmul(acc[:, s, half, which, :], wb[:, s, k, :],
                                                   hT[:, k, half * HALF:(half + 1) * HALF], start=k == 0, stop=k == KD - 1)
                        ins.then_inc(done, 1)

            tile(0, 0, True)
            tile(0, 1, True)
            with pe.Fori(1, NF // 2) as c:
                tile(c, 0, False)
                tile(c, 1, False)

        @block.scalar
        def _(act):
            def tile(c, s, first):
                for half in range(2):
                    act.wait_ge(gate_done, c * 4 + 2 * s + half + 1)
                    if not first:
                        act.wait_ge(act_done, c * 4 + 2 * s + half + 1 - 4)
                    nc.scalar.activation(sg[:, 2 * s + half, :], acc[:, s, half, 0, :], ACT.Silu).then_inc(silu_done, 1)

            tile(0, 0, True)
            tile(0, 1, True)
            with act.Fori(1, NF // 2) as c:
                tile(c, 0, False)
                tile(c, 1, False)

        @block.vector
        def _(dve):
            with dve.Fori(0, NF // 2) as c:
                for s in range(2):
                    for half in range(2):
                        n = 2 * s + half
                        dve.wait_ge(up_done, c * 4 + n + 1)
                        dve.wait_ge(silu_done, c * 4 + n + 1)
                        nc.vector.tensor_tensor(
                            av[:, bass.ds(c, 1), s, half * HALF:(half + 1) * HALF].rearrange("p o n -> p (o n)"),
                            acc[:, s, half, 1, :], sg[:, n, :], ALU.mult).then_inc(act_done, 1)



def hgrn_stage(nc, proj, lb_logits, mixed, ident):
    HEADS, V, D8 = A_HEADS, A_WIDTH // A_HEADS, 8
    LEVELS = (64, 32, 16, 8)
    NL = len(LEVELS)
    BLK = SEQ // D8
    CB = P // D8
    width = [D8 - s for s in range(D8)]
    off = [BLK * sum(width[:s]) for s in range(D8 + 1)]
    TINY = 2.0 ** -64
    with Stage(nc, "hg") as st:
        qf = st.sb("qf", [P, 2, 2, TT, P])
        v = st.sb("v", [P, 2, TT, V])
        lb0 = st.sb("lb0", [P, HEADS])
        lbs = st.sb("lbs", [P, 6, HEADS])
        f = st.sb("f", [P, SEQ])
        fc = st.sb("fc", [P, SEQ])
        q = st.sb("q", [P, SEQ])
        k = st.sb("k", [P, SEQ])
        b = st.sb("b", [P, SEQ])
        reset = st.sb("reset", [P, SEQ])
        qb = st.sb("qb", [P, SEQ])
        decay = st.sb("decay", [P, TT])
        kl = st.sb("kl", [P, SEQ])
        lev = st.sb("lev", [P, NL, SEQ])
        near = st.sb("near", [P, off[D8]])
        pick = st.sb("pick", [P, D8, P])
        m_lev = st.sb("m_lev", [P, NL, P])
        m_near = st.sb("m_near", [P, P])
        sm = st.sb("sm", [P, 2, NL + 1, P])
        kt = st.sb("kt", [P, 2, P])
        state = st.sb("state", [P, 2, V])
        ps_tr = st.ps("ps_tr", [P, 2, BANK])
        ps_l = st.ps("ps_l", [P, 2, BANK])
        ps_n = st.ps("ps_n", [P, 1, BANK])
        ps_kb = st.ps("ps_k", [P, 1, BANK])
        ps_ub = st.ps("ps_u", [P, 1, BANK])
        ps_o = st.ps("ps_o", [P, 1, BANK])
        ps_k, ps_u = ps_kb[:, 0, 0:P], ps_ub[:, 0, 0:V]
        qf_in = [st.sem(f"qf_in{x}") for x in range(2)]
        v_in = [st.sem(f"v_in{x}") for x in range(2)]
        lb_in, lb_exp, lb_step, setup = st.sem("lb_in"), st.sem("lb_exp"), st.sem("lb_step"), st.sem("setup")
        tr_done, sig_done, f_done, q_done, k_done, lf_done, b_done = (
            st.sem(n) for n in ("tr_done", "sig_done", "f_done", "q_done", "k_done", "lf_done", "b_done"))
        diff_done, exp_done, g_done, near_k = st.sem("diff_done"), st.sem("exp_done"), st.sem("g_done"), st.sem("near_k")
        a_done, m_done, kt_done, o_done, u_done, state_done, o_taken = (
            st.sem(n) for n in ("a_done", "m_done", "kt_done", "o_done", "u_done", "state_done", "o_taken"))
        cols = lambda c0: proj[:, c0:c0 + A_WIDTH].rearrange("(t p) (i x v) -> p t i x v", p=P, x=2, v=V)
        q_cols, f_cols, v_cols = cols(0), cols(A_WIDTH), cols(2 * A_WIDTH)
        DIFFS = 1 + NL + 1
        EXPS = 1 + DIFFS
        PRODUCTS = 2 + NL + 1
        block = st.block()

        def halves(ap, h):
            w = ap.rearrange("p (n x h) -> p n x h", x=2, h=h)
            return w[:, :, 0, :], w[:, :, 1, :]

        def near_of(ap, s):
            w = ap.rearrange("p (n c) -> p n c", c=D8)
            return w[:, :, s:], w[:, :, s:s + 1].to_broadcast([P, BLK, width[s]])

        @block.sync
        def _(sp):
            with nc.allow_non_contiguous_dma(reason="a bound per partition"):
                sp.dma_start(lb0[:], lb_logits.rearrange("o (h k) -> k (o h)", k=P)).then_inc(lb_in, 16)

            def load(it, x):
                for n, src in enumerate((f_cols, q_cols)):
                    sp.dma_start(qf[:, x, n, :, :], src[:, :, bass.ds(it, 1), x, :].rearrange("p t o v -> p t (o v)")).then_inc(qf_in[x], 16)
                sp.dma_start(v[:, x, :, :], v_cols[:, :, bass.ds(it, 1), x, :].rearrange("p t o v -> p t (o v)")).then_inc(v_in[x], 16)

            for x in range(2):
                load(0, x)
            with sp.Fori(1, HEADS // 2) as it:
                for x in range(2):
                    sp.wait_ge(u_done, it * (2 * TT) + (x + 1) * TT - 2 * TT)
                    load(it, x)

        @block.gpsimd
        def _(pool):
            nc.gpsimd.memset(reset[:], 1.0).then_inc(setup, 1)
            nc.gpsimd.memset(pick[:], 0.0).then_inc(setup, 1)
            nc.gpsimd.memset(m_lev[:], 0.0).then_inc(setup, 1)
            nc.gpsimd.memset(m_near[:], 1.0).then_inc(setup, 1)
            pool.wait_ge(setup, 4)
            nc.gpsimd.memset(reset[:].rearrange("p (c t) -> p c t", t=P)[:, :, 0], 0.0)
            for s in range(D8):
                nc.gpsimd.memset(pick[:, s, :].rearrange("p (n c) -> p n c", c=D8)[:, :, s], 1.0)
            for n, h in enumerate(LEVELS):
                nc.gpsimd.memset(halves(m_lev[:, n, :], h)[1], 1.0)
            ins = nc.gpsimd.memset(state[:], 0.0)
            ins.then_inc(setup, 1)
            pool.wait_ge(setup, 5)
            for n, h in enumerate(LEVELS):
                right = halves(m_lev[:, n, :], h)[1]
                nc.gpsimd.affine_select(out=right, in_=right, compare_op=ALU.is_ge, fill=0.0, base=0,
                                        pattern=[[-2 * h, P // (2 * h)], [0, h]], channel_multiplier=1).then_inc(setup, 1)
            near_m = m_near[:].rearrange("p (n c) -> p n c", c=D8)
            nc.gpsimd.affine_select(out=near_m, in_=near_m, compare_op=ALU.is_ge, fill=0.0, base=0,
                                    pattern=[[-D8, CB], [0, D8]], channel_multiplier=1).then_inc(setup, 1)
            pool.wait_ge(setup, 6 + NL)
            for n, h in enumerate(LEVELS):
                right = halves(m_lev[:, n, :], h)[1]
                nc.gpsimd.affine_select(out=right, in_=right, compare_op=ALU.is_ge, fill=0.0, base=h - 1,
                                        pattern=[[2 * h, P // (2 * h)], [0, h]], channel_multiplier=-1).then_inc(setup, 1)
            nc.gpsimd.affine_select(out=near_m, in_=near_m, compare_op=ALU.is_ge, fill=0.0, base=D8 - 1,
                                    pattern=[[D8, CB], [0, D8]], channel_multiplier=-1).then_inc(setup, 1)

        @block.tensor
        def _(pe):
            with pe.Fori(0, HEADS // 2) as it:
                for x in range(2):
                    head = it * 2 + x
                    pe.wait_ge(qf_in[x], (it + 1) * 32)
                    for n in range(2):
                        if n:
                            pe.wait_ge(sig_done, head * 2 + 1)
                        elif x:
                            pe.wait_ge(q_done, head)
                        for t in range(TT):
                            ins = nc.tensor.transpose(ps_tr[:, t // 4, (t % 4) * P:(t % 4 + 1) * P], qf[:, x, n, t, :], ident[:])
                        ins.then_inc(tr_done, 1)

                    def scores(c):
                        if c >= 2:
                            pe.wait_ge(m_done, head * TT + c - 1)
                        for n in range(NL):
                            g = lev[:, n, c * P:(c + 1) * P]
                            nc.tensor.matmul(ps_l[:, c % 2, n * P:(n + 1) * P], g, g, start=True, stop=True)
                        if c:
                            pe.wait_ge(m_done, head * TT + c)
                        for s in range(D8):
                            pairs = near[:, off[s]:off[s + 1]].rearrange("p (n c) -> p n c", c=width[s])[:, c * CB:(c + 1) * CB, :]
                            nc.tensor.matmul(ps_n[:, 0, 0:P].rearrange("p (n c) -> p n c", c=D8)[:, :, s:], pick[:, s, :], pairs,
                                             start=s == 0, stop=s == D8 - 1, skip_group_check=True)
                        if c:
                            pe.wait_ge(kt_done, head * TT + c)
                        nc.tensor.transpose(ps_k, kl[:, c * P:(c + 1) * P], ident[:]).then_inc(a_done, 1)

                    def outputs(c):
                        pe.wait_ge(m_done, head * TT + c + 1)
                        if c:
                            pe.wait_ge(o_taken, head * TT + c)
                            pe.wait_ge(state_done, head * (TT - 1) + c)
                        for n in range(NL + 1):
                            ins = nc.tensor.matmul(ps_o[:, 0, 0:V], sm[:, c % 2, n, :], v[:, x, c, :], start=n == 0,
                                                   stop=c == 0 and n == NL)
                        if c:
                            ins = nc.tensor.matmul(ps_o[:, 0, 0:V], qb[:, c * P:(c + 1) * P], state[:, c % 2, :], start=False, stop=True)
                        ins.then_inc(o_done, 1)
                        pe.wait_ge(kt_done, head * TT + c + 1)
                        nc.tensor.matmul(ps_u, kt[:, c % 2, :], v[:, x, c, :], start=True, stop=True).then_inc(u_done, 1)

                    pe.wait_ge(v_in[x], (it + 1) * 16)
                    pe.wait_ge(setup, 7 + 2 * NL)
                    pe.wait_ge(g_done, (head + 1) * PRODUCTS)
                    scores(0)
                    for c in range(TT):
                        if c + 1 < TT:
                            scores(c + 1)
                        outputs(c)

        @block.scalar
        def _(act):
            act.wait_ge(lb_step, 1)
            nc.scalar.activation(lbs[:, 1, :], lbs[:, 0, :], ACT.Exp).then_inc(lb_exp, 1)
            with act.Fori(0, HEADS // 2) as it:
                for x in range(2):
                    head = it * 2 + x
                    flat = ps_tr[:, :, :].rearrange("p a b -> p (a b)")
                    act.wait_ge(tr_done, head * 2 + 1)
                    nc.scalar.activation(f[:], flat, ACT.Sigmoid).then_inc(sig_done, 1)
                    act.wait_ge(tr_done, head * 2 + 2)
                    nc.scalar.activation(q[:], flat, ACT.Sigmoid).then_inc(sig_done, 1)
                    act.wait_ge(f_done, head * 2 + 2)
                    nc.scalar.activation(fc[:], fc[:], ACT.Ln).then_inc(lf_done, 1)
                    act.wait_ge(b_done, head + 1)
                    nc.scalar.activation(decay[:], b[:].rearrange("p (c t) -> p c t", t=P)[:, :, P - 1], ACT.Exp)
                    nc.scalar.activation(qb[:], b[:], ACT.Exp).then_inc(exp_done, 1)
                    act.wait_ge(diff_done, head * DIFFS + 1)
                    nc.scalar.activation(kl[:], kl[:], ACT.Exp).then_inc(exp_done, 1)
                    for n in range(NL):
                        act.wait_ge(diff_done, head * DIFFS + 2 + n)
                        nc.scalar.activation(lev[:, n, :], lev[:, n, :], ACT.Exp).then_inc(exp_done, 1)
                    act.wait_ge(diff_done, head * DIFFS + 2 + NL)
                    nc.scalar.activation(near[:], near[:], ACT.Exp).then_inc(exp_done, 1)
                    dst = mixed[:, :, 0:A_WIDTH].rearrange("p t (i x v) -> p t i x v", x=2, v=V)
                    for c in range(TT + 1):
                        if c < TT:
                            act.wait_ge(a_done, head * TT + c + 1)
                            if c >= 2:
                                act.wait_ge(u_done, head * TT + c - 1)
                            nc.scalar.activation(kt[:, c % 2, :], ps_k, ACT.Copy).then_inc(kt_done, 1)
                        if c:
                            act.wait_ge(o_done, head * TT + c)
                            nc.scalar.activation(dst[:, c - 1, bass.ds(it, 1), x, :].rearrange("p o v -> p (o v)"),
                                                 ps_o[:, 0, 0:V], ACT.Copy).then_inc(o_taken, 1)

        @block.vector
        def _(dve):
            dve.wait_ge(lb_in, 16)
            nc.vector.tensor_tensor(lbs[:, 0, :], lb0[:], lb0[:], ALU.subtract).then_inc(lb_step, 1)
            dve.wait_ge(lb_exp, 1)
            nc.vector.reciprocal(lbs[:, 2, :], lbs[:, 1, :]).then_inc(lb_step, 1)
            dve.wait_ge(lb_step, 2)
            nc.vector.tensor_tensor(lbs[:, 3, :], lbs[:, 1, :], lbs[:, 2, :], ALU.mult).then_inc(lb_step, 1)
            dve.wait_ge(lb_step, 3)
            nc.vector.tensor_tensor(lbs[:, 4, :], lbs[:, 3, :], lbs[:, 3, :], ALU.subtract).then_inc(lb_step, 1)
            dve.wait_ge(lb_step, 4)
            nc.vector.tensor_scalar(lbs[:, 5, :], lbs[:, 4, :], -1.0, 1.0, ALU.mult, ALU.add).then_inc(lb_step, 1)
            dve.wait_ge(lb_step, 5)
            dve.wait_ge(setup, 7 + 2 * NL)
            with dve.Fori(0, HEADS // 2) as it:
                for x in range(2):
                    head = it * 2 + x
                    flat = ps_tr[:, :, :].rearrange("p a b -> p (a b)")
                    lb = lbs[:, 4, :].rearrange("p (i x) -> p i x", x=2)[:, bass.ds(it, 1), x]
                    one_lb = lbs[:, 5, :].rearrange("p (i x) -> p i x", x=2)[:, bass.ds(it, 1), x]
                    dve.wait_ge(sig_done, head * 2 + 1)
                    nc.vector.tensor_scalar(f[:], f[:], one_lb, lb, ALU.mult, ALU.add).then_inc(f_done, 1)
                    dve.wait_ge(f_done, head * 2 + 1)
                    nc.vector.tensor_scalar(fc[:], f[:], TINY, None, ALU.max).then_inc(f_done, 1)
                    nc.vector.tensor_scalar(k[:], f[:], -1.0, 1.0, ALU.mult, ALU.add).then_inc(k_done, 1)
                    dve.wait_ge(sig_done, head * 2 + 2)
                    nc.vector.tensor_tensor(q[:], flat, q[:], ALU.mult).then_inc(q_done, 1)
                    dve.wait_ge(lf_done, head + 1)
                    nc.vector.tensor_tensor_scan(b[:], reset[:], fc[:], 0.0, ALU.mult, ALU.add).then_inc(b_done, 1)
                    dve.wait_ge(b_done, head + 1)
                    b3 = b[:].rearrange("p (c t) -> p c t", t=P)
                    nc.vector.tensor_tensor(kl[:].rearrange("p (c t) -> p c t", t=P), b3[:, :, P - 1:P].to_broadcast([P, TT, P]), b3,
                                            ALU.subtract).then_inc(diff_done, 1)
                    for n, h in enumerate(LEVELS):
                        left, right = halves(b[:], h)
                        to_left, to_right = halves(lev[:, n, :], h)
                        middle = left[:, :, h - 1:h].to_broadcast([P, SEQ // (2 * h), h])
                        nc.vector.tensor_tensor(to_left, middle, left, ALU.subtract)
                        nc.vector.tensor_tensor(to_right, right, middle, ALU.subtract).then_inc(diff_done, 1)
                    for s in range(D8):
                        to = near[:, off[s]:off[s + 1]].rearrange("p (n c) -> p n c", c=width[s])
                        behind, key = near_of(b[:], s)
                        ins = nc.vector.tensor_tensor(to, behind, key, ALU.subtract)
                    ins.then_inc(diff_done, 1)
                    dve.wait_ge(exp_done, head * EXPS + 1)
                    dve.wait_ge(k_done, head + 1)
                    nc.vector.tensor_tensor(qb[:], qb[:], q[:], ALU.mult).then_inc(g_done, 1)
                    dve.wait_ge(exp_done, head * EXPS + 2)
                    nc.vector.tensor_tensor(kl[:], kl[:], k[:], ALU.mult).then_inc(g_done, 1)
                    for n, h in enumerate(LEVELS):
                        to_left, to_right = halves(lev[:, n, :], h)
                        dve.wait_ge(exp_done, head * EXPS + 3 + n)
                        nc.vector.tensor_tensor(to_left, to_left, halves(k[:], h)[0], ALU.mult)
                        nc.vector.tensor_tensor(to_right, to_right, halves(q[:], h)[1], ALU.mult).then_inc(g_done, 1)
                    dve.wait_ge(exp_done, head * EXPS + EXPS)
                    for s in range(D8):
                        to = near[:, off[s]:off[s + 1]].rearrange("p (n c) -> p n c", c=width[s])
                        ins = nc.vector.tensor_tensor(to, to, near_of(k[:], s)[1], ALU.mult)
                    ins.then_inc(near_k, 1)
                    dve.wait_ge(near_k, head + 1)
                    for s in range(D8):
                        to = near[:, off[s]:off[s + 1]].rearrange("p (n c) -> p n c", c=width[s])
                        ins = nc.vector.tensor_tensor(to, to, near_of(q[:], s)[0], ALU.mult)
                    ins.then_inc(g_done, 1)

                    def masks(c):
                        dve.wait_ge(a_done, head * TT + c + 1)
                        if c >= 2:
                            dve.wait_ge(o_done, head * TT + c - 1)
                        nc.vector.tensor_tensor(sm[:, c % 2, 0:NL, :], ps_l[:, c % 2, :].rearrange("p (n t) -> p n t", t=P),
                                                m_lev[:], ALU.mult)
                        nc.vector.tensor_tensor(sm[:, c % 2, NL, :], ps_n[:, 0, 0:P], m_near[:], ALU.mult).then_inc(m_done, 1)

                    masks(0)
                    for c in range(TT):
                        if c + 1 < TT:
                            masks(c + 1)
                            dve.wait_ge(u_done, head * TT + c + 1)
                            if c == 0:
                                nc.vector.tensor_copy(state[:, 1, :], ps_u).then_inc(state_done, 1)
                            else:
                                dve.wait_ge(state_done, head * (TT - 1) + c)
                                nc.vector.scalar_tensor_tensor(state[:, (c + 1) % 2, :], state[:, c % 2, :], decay[:, c:c + 1], ps_u,
                                                               ALU.mult, ALU.add).then_inc(state_done, 1)
    hgrn_out_stage(nc, proj, mixed)


def hgrn_out_stage(nc, proj, mixed):
    HEADS, V = A_HEADS, A_WIDTH // A_HEADS
    with Stage(nc, "hgo") as st:
        g = st.sb("g", [P, TT, A_WIDTH])
        sg = st.sb("sg", [P, TT, A_WIDTH])
        sq = st.sb("sq", [P, TT, A_WIDTH])
        ss = st.sb("ss", [P, TT, HEADS])
        ms = st.sb("ms", [P, TT, HEADS])
        root = st.sb("root", [P, TT, HEADS])
        rstd = st.sb("rstd", [P, TT, HEADS])
        g_in, sg_done, sq_done, norm, silu_done = (st.sem(n) for n in ("g_in", "sg_done", "sq_done", "norm", "silu_done"))
        block = st.block()
        o = mixed[:, :, 0:A_WIDTH]

        @block.sync
        def _(sp):
            sp.dma_start(g[:], proj[:, 3 * A_WIDTH:4 * A_WIDTH].rearrange("(t p) n -> p t n", p=P)).then_inc(g_in, 16)

        @block.scalar
        def _(act):
            nc.scalar.activation(sq[:], o, ACT.Square).then_inc(sq_done, 1)
            act.wait_ge(g_in, 16)
            nc.scalar.activation(sg[:], g[:], ACT.Sigmoid).then_inc(sg_done, 1)
            act.wait_ge(norm, 2)
            nc.scalar.activation(root[:], ms[:], ACT.Sqrt).then_inc(norm, 1)

        @block.vector
        def _(dve):
            dve.wait_ge(sq_done, 1)
            nc.vector.tensor_reduce(ss[:].rearrange("p t h -> p (t h)"), sq[:].rearrange("p t (h v) -> p (t h) v", v=V), AX.X, ALU.add)\
                .then_inc(norm, 1)
            dve.wait_ge(norm, 1)
            nc.vector.tensor_scalar(ms[:], ss[:], 1.0 / V, EPS, ALU.mult, ALU.add).then_inc(norm, 1)
            dve.wait_ge(sg_done, 1)
            nc.vector.tensor_tensor(sg[:], sg[:], g[:], ALU.mult).then_inc(silu_done, 1)
            dve.wait_ge(norm, 3)
            nc.vector.reciprocal(rstd[:], root[:]).then_inc(norm, 1)
            dve.wait_ge(norm, 4)
            o4 = o.rearrange("p t (h v) -> p t h v", v=V)
            nc.vector.tensor_tensor(o4, o4, rstd[:].rearrange("p t (h x) -> p t h x", x=1).to_broadcast([P, TT, HEADS, V]), ALU.mult)\
                .then_inc(norm, 1)
            dve.wait_ge(norm, 5)
            dve.wait_ge(silu_done, 1)
            nc.vector.tensor_tensor(o, o, sg[:], ALU.mult)



def heads_stage(nc, name, src, dst, quads, ident):
    Q = 4
    with Stage(nc, name) as st:
        raw = st.sb("raw", [P, 2, TT, Q, HD])
        sq = st.sb("sq", [P, TT, Q, HD])
        tok = st.sb("tok", [P, 2, TT, Q, HA])
        outT = st.sb("outT", [HA, 2, Q, SEQ])
        ss = st.sb("ss", [P, TT * Q])
        ms = st.sb("ms", [P, TT * Q])
        root = st.sb("root", [P, TT * Q])
        rstd = st.sb("rstd", [P, TT * Q])
        pos_i = st.sb("pos_i", [P, TT], I32)
        pos = st.sb("pos", [P, TT])
        gains = st.sb("gains", [HA, len(quads)])
        gsc = st.sb("gsc", [HA, len(quads)])
        tr = st.ps("tr", [HA, TT, BANK])
        raw_in = [st.sem(f"raw_in{s}") for s in range(2)]
        outT_out = [st.sem(f"outT_out{s}") for s in range(2)]
        gain_in, setup, gsc_done = st.sem("gain_in"), st.sem("setup"), st.sem("gsc_done")
        sq_done, ss_done, ms_done, root_done, rstd_done = (
            st.sem(n) for n in ("sq_done", "ss_done", "ms_done", "root_done", "rstd_done"))
        aug_done, tok_done, tr_done = st.sem("aug_done"), st.sem("tok_done"), st.sem("tr_done")
        taken = [st.sem("taken_act"), st.sem("taken_dve")]
        normed = [n for n, q in enumerate(quads) if q[2] is not None]
        sv = src.rearrange("(t p) n -> p t n", p=P)
        block = st.block()

        @block.sync
        def _(sp):
            sp.wait_ge(setup, 1)
            with nc.allow_non_contiguous_dma(reason="a gain per partition"):
                for n in normed:
                    sp.dma_start(gains[0:HD, n:n + 1], quads[n][2].rearrange("(d o) -> d o", o=1)).then_inc(gain_in, 16)
            for n, (col, *_) in enumerate(quads):
                if n >= 2:
                    sp.wait_ge(tok_done, n - 1)
                sp.dma_start(raw[:, n % 2, :, :, :],
                             sv[:, :, col:col + Q * HD].rearrange("p t (h d) -> p t h d", d=HD)).then_inc(raw_in[n % 2], 16)

        @block.gpsimd
        def _(pool):
            nc.gpsimd.memset(gains[:], 1.0).then_inc(setup, 1)
            nc.gpsimd.iota(pos_i[:], pattern=[[P, TT]], base=0, channel_multiplier=1).then_inc(setup, 1)
            pool.wait_ge(setup, 2)
            nc.gpsimd.tensor_copy(pos[:], pos_i[:]).then_inc(setup, 1)
            pool.wait_ge(setup, 3)
            for n, (_, _, _, _, slopes) in enumerate(quads):
                s = n % 2
                if n >= 2:
                    pool.wait_ge(tr_done, (n - 1) * TT)
                for h in range(Q):
                    for r, ap in ((HD, tok[:, s, :, h, HD:HD + 1]), (HD + 1, tok[:, s, :, h, HD + 1:HA])):
                        ap = ap.rearrange("p t o -> p (t o)")
                        if slopes is not None and r == HD:
                            ins = nc.gpsimd.memset(ap, slopes[h])
                        elif slopes is not None:
                            ins = nc.gpsimd.tensor_scalar(ap, pos[:], -slopes[h], 1.0, ALU.mult, ALU.mult)
                        elif r == HD:
                            ins = nc.gpsimd.tensor_copy(ap, pos[:])
                        else:
                            ins = nc.gpsimd.memset(ap, 1.0)
                ins.then_inc(aug_done, 1)

            for n, (_, h0, *_) in enumerate(quads):
                for who in range(2):
                    pool.wait_ge(taken[who], (n + 1) * (TT // 2))
                pool.dma_start(dst[h0:h0 + Q, :, :].rearrange("h r t -> r h t"), outT[:, n % 2, :, :])\
                    .then_inc(outT_out[n % 2], 16)
            for s in range(2):
                pool.wait_ge(outT_out[s], 16 * ((len(quads) + 1 - s) // 2))

        def take(eng, who, n):
            if n >= 2:
                eng.wait_ge(outT_out[n % 2], 16 * (n // 2))
            if n == 0:
                eng.wait_ge(gsc_done, 1)
            for t in range(who, TT, 2):
                eng.wait_ge(tr_done, n * TT + t + 1)
                to, of = outT[:, n % 2, :, t * P:(t + 1) * P], tr[:, t, :].rearrange("r (h c) -> r h c", c=P)
                if who == 0:
                    nc.scalar.activation(to, of, ACT.Copy, scale=gsc[:, n:n + 1]).then_inc(taken[0], 1)
                else:
                    nc.vector.tensor_scalar(to, of, gsc[:, n:n + 1], None, ALU.mult).then_inc(taken[1], 1)

        @block.scalar
        def _(act):
            for n in range(len(quads) + 1):
                if n < len(quads) and n in normed:
                    i = normed.index(n)
                    act.wait_ge(raw_in[n % 2], 16 * (n // 2 + 1))
                    if i:
                        act.wait_ge(ss_done, i)
                    nc.scalar.activation(sq[:], raw[:, n % 2, :, :, :], ACT.Square).then_inc(sq_done, 1)
                    act.wait_ge(ms_done, i + 1)
                    nc.scalar.activation(root[:], ms[:], ACT.Sqrt).then_inc(root_done, 1)
                if n:
                    take(act, 0, n - 1)

        @block.vector
        def _(dve):
            dve.wait_ge(gain_in, 16 * len(normed))
            for n, q in enumerate(quads):
                ins = nc.vector.tensor_scalar(gsc[0:HD, n:n + 1], gains[0:HD, n:n + 1], q[3], None, ALU.mult)
            nc.vector.tensor_copy(gsc[HD:HA, :], gains[HD:HA, :]).then_inc(gsc_done, 1)
            for n in range(len(quads) + 1):
                if n < len(quads):
                    s = n % 2
                    dve.wait_ge(raw_in[s], 16 * (n // 2 + 1))
                    if n in normed:
                        i = normed.index(n)
                        dve.wait_ge(sq_done, i + 1)
                        nc.vector.tensor_reduce(ss[:], sq[:].rearrange("p t h d -> p (t h) d"), AX.X, ALU.add)\
                            .then_inc(ss_done, 1)
                        dve.wait_ge(ss_done, i + 1)
                        nc.vector.tensor_scalar(ms[:], ss[:], 1.0 / HD, EPS, ALU.mult, ALU.add).then_inc(ms_done, 1)
                        dve.wait_ge(root_done, i + 1)
                        nc.vector.reciprocal(rstd[:], root[:]).then_inc(rstd_done, 1)
                        dve.wait_ge(rstd_done, i + 1)
                    if n >= 2:
                        dve.wait_ge(tr_done, (n - 1) * TT)
                    if n in normed:
                        nc.vector.tensor_tensor(
                            tok[:, s, :, :, 0:HD].rearrange("p t h d -> p (t h) d"),
                            raw[:, s, :, :, :].rearrange("p t h d -> p (t h) d"),
                            bcast(rstd[:].rearrange("p (a o) -> p a o", o=1), HD), ALU.mult).then_inc(tok_done, 1)
                    else:
                        nc.vector.tensor_copy(tok[:, s, :, :, 0:HD].rearrange("p t h d -> p (t h) d"),
                                              raw[:, s, :, :, :].rearrange("p t h d -> p (t h) d")).then_inc(tok_done, 1)
                if n:
                    take(dve, 1, n - 1)

        @block.tensor
        def _(pe):
            for n in range(len(quads)):
                pe.wait_ge(tok_done, n + 1)
                pe.wait_ge(aug_done, n + 1)
                for t in range(TT):
                    if n:
                        pe.wait_ge(taken[t % 2], (n - 1) * (TT // 2) + t // 2 + 1)
                    for h in range(Q):
                        ins = nc.tensor.transpose(tr[:, t, h * P:(h + 1) * P], tok[:, n % 2, t, h, :], ident[:])
                    ins.then_inc(tr_done, 1)


def attention_stage(nc, name, n_heads, qT, branches, mixed, col0, ident, gates=None, sel=None):
    NB = len(branches)
    ROUNDS = n_heads // 2
    U = NB * TT
    units = [(hh, br, i, min(i + 1, branches[br][4])) for hh in range(2) for br in range(NB) for i in range(TT)]
    N = len(units)
    chunks = []
    of_unit = []
    for n, (_, _, _, nk) in enumerate(units):
        of_unit.append(range(len(chunks), len(chunks) + -(-nk // 4)))
        chunks += [(n, j, min(4, nk - j)) for j in range(0, nk, 4)]
    C = len(chunks)
    nth = [c // 2 for c in range(C)]
    per = [(C + 1) // 2, C // 2]
    selected = [n for n, (_, br, i, _) in enumerate(units) if branches[br][6] and i >= TOPN * SLC // P]
    loads = 1 + 2 * NB
    with Stage(nc, name) as st:
        q = st.sb("q", [HA, 2, SEQ])
        k = st.sb("k", [HA, 2, NB, SEQ])
        v = st.sb("v", [P, 2, NB, TT, HD])
        sb = st.sb("s", [P, 2, SEQ])
        pr = st.sb("p", [P, 2, SEQ])
        pt = st.sb("pt", [P, 4, BANK])
        nm = st.sb("nm", [P, N])
        rowsum = st.sb("rowsum", [P, N])
        rl = st.sb("rl", [P, 2 * NB, TT])
        sc = st.sb("sc", [P, 2 * NB, TT])
        o_sb = st.sb("o", [P, TT, HD])
        mask = st.sb("mask", [P, 2, SEQ]) if sel is not None else None
        ps_s = st.ps("ps_s", [P, 2, 2 * BANK])
        ps_t = st.ps("ps_t", [P, 2, BANK])
        ps_o = st.ps("ps_o", [P, 2, BANK])
        in_sem = [st.sem(f"in{s}") for s in range(2)]
        s_done, neg_done, e_done, t_done, pv_done, o_free, step, mask_done, mask_free = (
            st.sem(x) for x in ("s_done", "neg_done", "e_done", "t_done", "pv_done", "o_free", "step", "mask_done", "mask_free"))
        pt_done = [st.sem("pt_done_dve"), st.sem("pt_done_act")]
        qv = qT.rearrange("(i s) r t -> i s r t", s=2)
        kvs = []
        for kT, vd, group, *_ in branches:
            vv = vd.rearrange("(t p) (g d) -> p t g d", p=P, d=HD)
            kvs.append((kT, vv, group))
        bank_of = lambda hh, br: (hh * NB + br) % 2
        evacs = 2 * NB
        block = st.block()

        @block.sync
        def _(sp):
            def load(it, s):
                sp.dma_start(q[:, s, :], qv[bass.ds(it, 1), s, :, :].rearrange("o r t -> (o r) t")).then_inc(in_sem[s], 16)
                for b, (kT, vv, group) in enumerate(kvs):
                    if group == 1:
                        ks = kT.rearrange("(i s) r t -> i s r t", s=2)[bass.ds(it, 1), s, :, :]
                        vs = vv.rearrange("p t (i s) d -> p t i s d", s=2)[:, :, bass.ds(it, 1), s, :]
                    else:
                        g = it // (group // 2)
                        ks, vs = kT[bass.ds(g, 1), :, :], vv[:, :, bass.ds(g, 1), :]
                    sp.dma_start(k[:, s, b, :], ks.rearrange("o r t -> (o r) t")).then_inc(in_sem[s], 16)
                    sp.dma_start(v[:, s, b, :, :], vs.rearrange("p t o d -> p t (o d)")).then_inc(in_sem[s], 16)

            for s in range(2):
                load(0, s)
            with sp.Fori(1, ROUNDS) as it:
                for s in range(2):
                    sp.wait_ge(pv_done, it * N + (s + 1) * U - N)
                    load(it, s)

        @block.tensor
        def _(pe):
            with pe.Fori(0, ROUNDS) as it:
                def scores(n):
                    hh, br, i, nk = units[n]
                    if n % U == 0:
                        pe.wait_ge(in_sem[hh], (it + 1) * (16 * loads))
                    if n >= 2:
                        pe.wait_ge(neg_done, it * N + n - 1)
                    k0 = (i + 1 - nk) * P
                    for j in range(0, nk * P, BANK):
                        w = min(BANK, nk * P - j)
                        ins = nc.tensor.matmul(ps_s[:, n % 2, j:j + w], q[:, hh, i * P:(i + 1) * P],
                                               k[:, hh, br, k0 + j:k0 + j + w], start=True, stop=True)
                    ins.then_inc(s_done, 1)

                def transposes(n):
                    pe.wait_ge(e_done, it * N + n + 1)
                    for c in of_unit[n]:
                        _, j0, w = chunks[c]
                        if c >= 2:
                            pe.wait_ge(pt_done[c % 2], it * per[c % 2] + nth[c])
                        for j in range(w):
                            ins = nc.tensor.transpose(ps_t[:, c % 2, j * P:(j + 1) * P],
                                                      pr[:, n % 2, (j0 + j) * P:(j0 + j + 1) * P], ident[:])
                        ins.then_inc(t_done, 1)

                def values(n):
                    hh, br, i, nk = units[n]
                    if i == 0:
                        pe.wait_ge(o_free, it * evacs + hh * NB + br + 1)
                    for c in of_unit[n]:
                        _, j0, w = chunks[c]
                        pe.wait_ge(pt_done[c % 2], it * per[c % 2] + nth[c] + 1)
                        for j in range(j0, j0 + w):
                            ins = nc.tensor.matmul(ps_o[:, bank_of(hh, br), i * HD:(i + 1) * HD],
                                                   pt[:, c % 4, (j - j0) * P:(j - j0 + 1) * P],
                                                   v[:, hh, br, i + 1 - nk + j, :], start=j == 0, stop=j == nk - 1)
                    ins.then_inc(pv_done, 1)

                scores(0)
                scores(1)
                for n in range(N):
                    transposes(n)
                    if n:
                        values(n - 1)
                    if n + 2 < N:
                        scores(n + 2)
                values(N - 1)

        def copies(eng, who, it, n):
            for c in of_unit[n]:
                if c % 2 != who:
                    continue
                eng.wait_ge(t_done, it * C + c + 1)
                if c >= 4:
                    eng.wait_ge(pv_done, it * N + chunks[c - 4][0] + 1)
                w = chunks[c][2] * P
                if who:
                    nc.scalar.activation(pt[:, c % 4, 0:w], ps_t[:, c % 2, 0:w], ACT.Copy).then_inc(pt_done[1], 1)
                else:
                    nc.vector.tensor_copy(pt[:, c % 4, 0:w], ps_t[:, c % 2, 0:w]).then_inc(pt_done[0], 1)

        @block.scalar
        def _(act):
            with act.Fori(0, ROUNDS) as it:
                def exps(n):
                    w = units[n][3] * P
                    act.wait_ge(neg_done, it * N + n + 1)
                    if n >= 2:
                        act.wait_ge(t_done, it * C + of_unit[n - 2][-1] + 1)
                    nc.scalar.activation(pr[:, n % 2, 0:w], sb[:, n % 2, 0:w], ACT.Exp, bias=nm[:, n:n + 1],
                                         scale=-1.0, accum_out=rowsum[:, n:n + 1]).then_inc(e_done, 1)

                exps(0)
                exps(1)
                for n in range(N):
                    copies(act, 1, it, n)
                    if n + 2 < N:
                        exps(n + 2)

        @block.vector
        def _(dve):
            nc.vector.memset(o_sb[:], 0.0).then_inc(o_free, 2)
            with dve.Fori(0, ROUNDS) as it:
                def negate(n):
                    hh, br, i, nk = units[n]
                    w = nk * P
                    dve.wait_ge(s_done, it * N + n + 1)
                    if n >= 2:
                        dve.wait_ge(e_done, it * N + n - 1)
                    if n in selected:
                        m = selected.index(n)
                        dve.wait_ge(mask_done, it * len(selected) + m + 1)
                        bias = mask[:, m % 2, 0:w]
                    else:
                        bias = branches[br][3][:, SEQ - w:SEQ]
                    nc.vector.nop(nofuse=True)
                    ins = nc.vector.tensor_tensor_reduce(out=sb[:, n % 2, 0:w], in0=ps_s[:, n % 2, 0:w], in1=bias,
                                                         scale=-1.0, scalar=3e38, op0=ALU.add, op1=ALU.min,
                                                         accum_out=nm[:, n:n + 1])
                    ins.then_inc(neg_done, 1)

                def output(hh, br):
                    b = hh * NB + br
                    n0 = hh * U + br * TT
                    links = 1 if gates is None else 2
                    done = (it * evacs + b) * links
                    dst = mixed[:, :, col0:col0 + n_heads * HD].rearrange("p t (i s d) -> p t i s d", s=2, d=HD)
                    dst = dst[:, :, bass.ds(it, 1), hh, :].rearrange("p t o d -> p t (o d)")
                    bank = ps_o[:, bank_of(hh, br), :].rearrange("p (t d) -> p t d", d=HD)
                    dve.wait_ge(pv_done, it * N + n0 + TT)
                    nc.vector.reciprocal(rl[:, b, :], rowsum[:, n0:n0 + TT]).then_inc(step, 1)
                    dve.wait_ge(step, done + 1)
                    if gates is None:
                        nc.vector.tensor_tensor(dst, bank, bcast(rl[:, b, :].rearrange("p (t o) -> p t o", o=1), HD),
                                                ALU.mult).then_inc(o_free, 1)
                        return
                    g = gates[:, :, branches[br][5]:branches[br][5] + n_heads].rearrange("p t (i s) -> p t i s", s=2)
                    nc.vector.tensor_tensor(sc[:, b, :], rl[:, b, :],
                                            g[:, :, bass.ds(it, 1), hh].rearrange("p t o -> p (t o)"),
                                            ALU.mult).then_inc(step, 1)
                    dve.wait_ge(step, done + 2)
                    nc.vector.tensor_tensor(o_sb[:], bank, bcast(sc[:, b, :].rearrange("p (t o) -> p t o", o=1), HD),
                                            ALU.mult).then_inc(o_free, 1)
                    dve.wait_ge(o_free, it * evacs + b + 3)
                    nc.vector.tensor_tensor(dst, o_sb[:], dst, ALU.add)

                negate(0)
                negate(1)
                for n in range(N):
                    copies(dve, 0, it, n)
                    if n + 2 < N:
                        negate(n + 2)
                    if n % TT == 1 and n > TT:
                        output(units[n - TT][0], units[n - TT][1])
                output(1, NB - 1)

        @block.gpsimd
        def _(pool):
            if sel is None:
                return
            bias = branches[0][3]
            with pool.Fori(0, ROUNDS) as it:
                for m, n in enumerate(selected):
                    _, _, i, nk = units[n]
                    w = nk * P
                    if m >= 2:
                        pool.wait_ge(neg_done, it * N + selected[m - 2] + 1)
                    else:
                        pool.wait_ge(s_done, it * N + 1)
                    picked = sel[:, bass.ds(it // (GROUP // 2), 1), i, 0:w // SLC].rearrange("p o (m x) -> p (o m) x", x=1)
                    pool.nop(nofuse=True)
                    nc.gpsimd.tensor_tensor(mask[:, m % 2, 0:w].rearrange("p (m c) -> p m c", c=SLC),
                                            bias[:, SEQ - w:SEQ].rearrange("p (m c) -> p m c", c=SLC),
                                            bcast(picked, SLC), ALU.add).then_inc(mask_done, 1)



def compress_stage(nc, kvT, pe, w1, w2, k_gain, gate_cols, kcT, vc, gates, ident):
    G = KV_HEADS
    NW = N_CMP
    with Stage(nc, "cmp") as st:
        t_in = st.sb("t_in", [HD, 2, G, SEQ])
        w1s = st.sb("w1s", [HD, 2, CMP_LEN, CMP_HIDDEN])
        w2s = st.sb("w2s", [CMP_HIDDEN, 2, HD])
        pes = st.sb("pes", [2 * CMP_LEN, HD])
        peT = st.sb("peT", [HD, 2 * CMP_LEN])
        gain = st.sb("gain", [HA, 1])
        g_raw = st.sb("g_raw", [P, TT, 3 * C_HEADS])
        pb = st.sb("pb", [CMP_HIDDEN, 2])
        hid = st.sb("hid", [CMP_HIDDEN, 2, G * NW])
        sq = st.sb("sq", [NW, G, HD])
        ss = st.sb("ss", [NW, G])
        ms = st.sb("ms", [NW, G])
        root = st.sb("root", [NW, G])
        rstd = st.sb("rstd", [NW, G])
        pos_i = st.sb("pos_i", [CMP_PAD, 1], I32)
        ktok = st.sb("ktok", [CMP_PAD, G, HA])
        ps_h = st.ps("ps_h", [CMP_HIDDEN, 2, BANK])
        ps_b = st.ps("ps_b", [CMP_HIDDEN, 2, BANK])
        ps_c = st.ps("ps_c", [CMP_PAD, 2, BANK])
        ps_t = st.ps("ps_t", [P, 1, BANK])
        pe_in, in_sem, g_in, gain_in = st.sem("pe_in"), st.sem("in"), st.sem("g_in"), st.sem("gain_in")
        peT_ready, peT_done, bias_ready, pb_done, hid_ready, hid_done, c_ready = (
            st.sem(x) for x in ("peT_ready", "peT_done", "bias_ready", "pb_done", "hid_ready", "hid_done", "c_ready"))
        norm, sq_done, ktok_set, ktok_done, tr_ready, gain_set = (
            st.sem(x) for x in ("norm", "sq_done", "ktok_set", "ktok_done", "tr_ready", "gain_set"))
        block = st.block()

        @block.sync
        def _(sp):
            sp.dma_start(pes[:], pe.rearrange("v l d -> (v l) d")).then_inc(pe_in, 16)
            for v in range(2):
                sp.dma_start(w1s[:, v, :, :], w1[v, :, :].rearrange("(l d) h -> d l h", d=HD)).then_inc(in_sem, 16)
                sp.dma_start(w2s[:, v, :], w2[v, :, :]).then_inc(in_sem, 16)
                sp.dma_start(t_in[:, v, :, :], kvT[v * G:(v + 1) * G, 0:HD, :].rearrange("g r t -> r g t")).then_inc(in_sem, 16)
            sp.dma_start(g_raw[:], gate_cols.rearrange("(t p) n -> p t n", p=P)).then_inc(g_in, 16)
            sp.wait_ge(gain_set, 1)
            with nc.allow_non_contiguous_dma(reason="a gain per partition"):
                sp.dma_start(gain[0:HD, :], k_gain.rearrange("(d o) -> d o", o=1)).then_inc(gain_in, 16)

        @block.gpsimd
        def _(pool):
            nc.gpsimd.memset(gain[:], 1.0).then_inc(gain_set, 1)
            nc.gpsimd.iota(pos_i[:], pattern=[[0, 1]], base=CMP_LEN - 1, channel_multiplier=CMP_STRIDE).then_inc(ktok_set, 1)
            nc.gpsimd.memset(ktok[:], 0.0).then_inc(ktok_set, 1)
            nc.gpsimd.memset(vc[:], 0.0).then_inc(ktok_set, 1)
            pool.wait_ge(ktok_set, 3)
            for g in range(G):
                nc.gpsimd.tensor_copy(ktok[:, g, HD:HD + 1], pos_i[:])
                ins = nc.gpsimd.memset(ktok[:, g, HD + 1:HA], 1.0)
            ins.then_inc(ktok_set, 1)

        @block.tensor
        def _(te):
            te.wait_ge(pe_in, 16)
            nc.tensor.transpose(ps_t[0:HD, 0, 0:2 * CMP_LEN], pes[:], ident[0:2 * CMP_LEN, 0:2 * CMP_LEN]).then_inc(peT_ready, 1)
            te.wait_ge(in_sem, 16 * 6)
            te.wait_ge(peT_done, 1)
            for v in range(2):
                for l in range(CMP_LEN):
                    ins = nc.tensor.matmul(ps_b[:, v, 0:1], w1s[:, v, l, :], peT[:, v * CMP_LEN + l:v * CMP_LEN + l + 1],
                                           start=l == 0, stop=l == CMP_LEN - 1)
                ins.then_inc(bias_ready, 1)
            for v in range(2):
                for l in range(CMP_LEN):
                    windows = t_in[:, v, :, l:l + CMP_STRIDE * (NW - 1) + 1:CMP_STRIDE]
                    ins = nc.tensor.matmul(ps_h[:, v, 0:G * NW].rearrange("p (g n) -> p g n", n=NW), w1s[:, v, l, :],
                                           windows, start=l == 0, stop=l == CMP_LEN - 1)
                ins.then_inc(hid_ready, 1)
            for v in range(2):
                te.wait_ge(hid_done, v + 1)
                for g in range(G):
                    ins = nc.tensor.matmul(ps_c[0:NW, v, g * HD:(g + 1) * HD], hid[:, v, g * NW:(g + 1) * NW], w2s[:, v, :],
                                           start=True, stop=True)
                ins.then_inc(c_ready, 1)
            te.wait_ge(ktok_done, 1)
            for g in range(G):
                ins = nc.tensor.transpose(ps_t[0:HA, 0, g * CMP_PAD:(g + 1) * CMP_PAD], ktok[:, g, :], ident[0:CMP_PAD, 0:CMP_PAD])
            ins.then_inc(tr_ready, 1)

        @block.scalar
        def _(act):
            act.wait_ge(bias_ready, 2)
            nc.scalar.activation(pb[:], ps_b[:, :, 0:1].rearrange("p v o -> p (v o)"), ACT.Copy).then_inc(pb_done, 1)
            act.wait_ge(pb_done, 1)
            for v in range(2):
                act.wait_ge(hid_ready, v + 1)
                nc.scalar.activation(hid[:, v, :], ps_h[:, v, 0:G * NW], ACT.Silu, bias=pb[:, v:v + 1]).then_inc(hid_done, 1)
            act.wait_ge(c_ready, 1)
            nc.scalar.activation(sq[:], ps_c[0:NW, 0, 0:G * HD].rearrange("p (g d) -> p g d", d=HD), ACT.Square)\
                .then_inc(sq_done, 1)
            act.wait_ge(norm, 2)
            nc.scalar.activation(root[:], ms[:], ACT.Sqrt).then_inc(norm, 1)
            act.wait_ge(g_in, 16)
            nc.scalar.activation(gates[:], g_raw[:], ACT.Sigmoid)

        @block.vector
        def _(dve):
            dve.wait_ge(peT_ready, 1)
            nc.vector.tensor_copy(peT[:], ps_t[0:HD, 0, 0:2 * CMP_LEN]).then_inc(peT_done, 1)
            dve.wait_ge(sq_done, 1)
            nc.vector.tensor_reduce(ss[:], sq[:], AX.X, ALU.add).then_inc(norm, 1)
            dve.wait_ge(norm, 1)
            nc.vector.tensor_scalar(ms[:], ss[:], 1.0 / HD, EPS, ALU.mult, ALU.add).then_inc(norm, 1)
            dve.wait_ge(norm, 3)
            nc.vector.reciprocal(rstd[:], root[:]).then_inc(norm, 1)
            dve.wait_ge(norm, 4)
            dve.wait_ge(ktok_set, 4)
            nc.vector.tensor_tensor(ktok[0:NW, :, 0:HD], ps_c[0:NW, 0, 0:G * HD].rearrange("p (g d) -> p g d", d=HD),
                                    bcast(rstd[:].rearrange("p (g o) -> p g o", o=1), HD), ALU.mult).then_inc(ktok_done, 1)
            dve.wait_ge(c_ready, 2)
            nc.vector.tensor_copy(vc[0:NW, :, :], ps_c[0:NW, 1, 0:G * HD].rearrange("p (g d) -> p g d", d=HD))
            dve.wait_ge(tr_ready, 1)
            dve.wait_ge(gain_in, 16)
            nc.vector.tensor_scalar(kcT[:], ps_t[0:HA, 0, 0:G * CMP_PAD].rearrange("p (g n) -> p g n", n=CMP_PAD),
                                    gain[:, 0:1], None, ALU.mult)


def select_stage(nc, qT, kcT, vc, gates, sel, mixed, ident):
    J = GROUP
    N = 2 * TT
    ROUNDS = KV_HEADS // 2
    FIRST = TOPN * SLC // P
    PICKED = 3e38
    FORCED = 1e30
    with Stage(nc, "sel") as st:
        q = st.sb("q", [HA, 2, J, SEQ])
        cmask = st.sb("cmask", [P, TT, CMP_PAD])
        force = st.sb("force", [P, TT, N_SLC])
        alive = st.sb("alive", [P, TT])
        s = st.sb("s", [P, 2, J, CMP_PAD])
        e = st.sb("e", [P, 2, J, CMP_PAD])
        pn = st.sb("pn", [P, 2, J, CMP_PAD])
        pt = st.sb("pt", [CMP_PAD, 2, J, P])
        nm = st.sb("nm", [P, 2, J])
        rowsum = st.sb("rowsum", [P, 2, J])
        rl = st.sb("rl", [P, 2, J])
        rla = st.sb("rla", [P, 2, J])
        both = st.sb("both", [P, 1 + CMP_PAD])
        quad = st.sb("quad", [P, N_SLC])
        imp = st.sb("imp", [P, N_SLC])
        score = st.sb("score", [P, N_SLC])
        top = st.sb("top", [P, 8])
        marked = st.sb("marked", [P, N_SLC])
        ps_s = st.ps("ps_s", [P, 2, BANK])
        ps_t = st.ps("ps_t", [CMP_PAD, 2, BANK])
        ps_o = st.ps("ps_o", [P, 2, BANK])
        in_sem = [st.sem(f"in{x}") for x in range(2)]
        setup, s_done, neg_done, e_done, pn_done, t_done, pt_done, o_done, o_taken, link, sel_link = (
            st.sem(x) for x in ("setup", "s_done", "neg_done", "e_done", "pn_done", "t_done", "pt_done", "o_done",
                                "o_taken", "link", "sel_link"))
        masked, force_set = st.sem("masked"), st.sem("force_set")
        picks = [n for n in range(N) if n % TT >= FIRST]
        qv = qT.rearrange("(i s j) r t -> i s r j t", s=2, j=J)
        block = st.block()

        @block.sync
        def _(sp):
            def load(it, x):
                for j in range(J):
                    sp.dma_start(q[:, x, j, :], qv[bass.ds(it, 1), x, :, j, :].rearrange("o r t -> (o r) t")).then_inc(in_sem[x], 16)

            for x in range(2):
                load(0, x)
            with sp.Fori(1, ROUNDS) as it:
                for x in range(2):
                    sp.wait_ge(s_done, it * N + (x + 1) * TT - N)
                    load(it, x)

        @block.gpsimd
        def _(pool):
            nc.gpsimd.memset(cmask[:], 0.0).then_inc(setup, 1)
            nc.gpsimd.memset(alive[:], 1.0).then_inc(setup, 1)
            nc.gpsimd.memset(both[:], 0.0).then_inc(setup, 1)
            nc.gpsimd.memset(sel[:], 0.0).then_inc(setup, 1)
            pool.wait_ge(setup, 4)
            nc.gpsimd.affine_select(out=cmask[:], in_=cmask[:], compare_op=ALU.is_ge, fill=NEG, base=-(CMP_LEN - 1),
                                    pattern=[[P, TT], [-CMP_STRIDE, CMP_PAD]], channel_multiplier=1).then_inc(setup, 1)
            nc.gpsimd.affine_select(out=alive[:], in_=alive[:], compare_op=ALU.is_ge, fill=0.0, base=-(CMP_LEN - 1),
                                    pattern=[[P, TT]], channel_multiplier=1).then_inc(setup, 1)

        @block.tensor
        def _(pe):
            with pe.Fori(0, ROUNDS) as it:
                def scores(n):
                    x, i = divmod(n, TT)
                    if i == 0:
                        pe.wait_ge(in_sem[x], (it + 1) * (16 * J))
                    if n >= 2:
                        pe.wait_ge(masked, it * N + n - 1)
                    for j in range(J):
                        ins = nc.tensor.matmul(ps_s[:, n % 2, j * CMP_PAD:(j + 1) * CMP_PAD], q[:, x, j, i * P:(i + 1) * P],
                                               kview(it, x), start=True, stop=True)
                    ins.then_inc(s_done, 1)

                def transposes(n):
                    pe.wait_ge(pn_done, it * N + n + 1)
                    if n >= 2:
                        pe.wait_ge(pt_done, it * N + n - 1)
                    pe.nop(nofuse=True)
                    for j in range(J):
                        ins = nc.tensor.transpose(ps_t[:, n % 2, j * P:(j + 1) * P], pn[:, n % 2, j, :], ident[:])
                    ins.then_inc(t_done, 1)

                def values(n):
                    x, i = divmod(n, TT)
                    pe.wait_ge(pt_done, it * N + n + 1)
                    if n >= 2:
                        pe.wait_ge(o_taken, it * N + n - 1)
                    pe.nop(nofuse=True)
                    for j in range(J):
                        ins = nc.tensor.matmul(ps_o[:, n % 2, j * HD:(j + 1) * HD], pt[:, n % 2, j, :], vview(it, x),
                                               start=True, stop=True)
                    ins.then_inc(o_done, 1)

                def kview(it, x):
                    return kcT[:, :, :].rearrange("p (i s) n -> p i s n", s=2)[:, bass.ds(it, 1), x, :].rearrange("p o n -> p (o n)")

                def vview(it, x):
                    return vc[:, :, :].rearrange("p (i s) n -> p i s n", s=2)[:, bass.ds(it, 1), x, :].rearrange("p o n -> p (o n)")

                scores(0)
                scores(1)
                for n in range(N):
                    transposes(n)
                    if n:
                        values(n - 1)
                    if n + 2 < N:
                        scores(n + 2)
                values(N - 1)

        @block.scalar
        def _(act):
            with act.Fori(0, ROUNDS) as it:
                for n in range(N + 1):
                    if n < N:
                        act.wait_ge(neg_done, it * N + n + 1)
                        for j in range(J):
                            ins = nc.scalar.activation(e[:, n % 2, j, :], s[:, n % 2, j, :], ACT.Exp,
                                                       bias=nm[:, n % 2, j:j + 1], accum_out=rowsum[:, n % 2, j:j + 1])
                        ins.then_inc(e_done, 1)
                    if n:
                        m = n - 1
                        act.wait_ge(t_done, it * N + m + 1)
                        if m >= 2:
                            act.wait_ge(o_done, it * N + m - 1)
                        nc.scalar.activation(pt[:, m % 2, :, :], ps_t[:, m % 2, :].rearrange("p (j c) -> p j c", c=P), ACT.Copy)\
                            .then_inc(pt_done, 1)

        @block.vector
        def _(dve):
            nc.vector.memset(force[:], 0.0).then_inc(force_set, 1)
            dve.wait_ge(force_set, 1)
            for i in range(FIRST, TT):
                for half in range(2):
                    cur = 2 * i + half
                    rows = slice(half * SLC, (half + 1) * SLC)
                    nc.vector.memset(force[rows, i, 0:1], FORCED)
                    ins = nc.vector.memset(force[rows, i, cur - 1:cur + 1], FORCED)
                    if cur + 1 < N_SLC:
                        ins = nc.vector.memset(force[rows, i, cur + 1:N_SLC], NEG)
            ins.then_inc(force_set, 1)
            dve.wait_ge(force_set, 2)
            dve.wait_ge(setup, 6)
            with dve.Fori(0, ROUNDS) as it:
                def negate(n):
                    i = n % TT
                    dve.wait_ge(s_done, it * N + n + 1)
                    nc.vector.tensor_tensor(s[:, n % 2, :, :], ps_s[:, n % 2, 0:J * CMP_PAD].rearrange("p (j c) -> p j c", c=CMP_PAD),
                                            cmask[:, i:i + 1, :].to_broadcast([P, J, CMP_PAD]), ALU.add).then_inc(masked, 1)
                    dve.wait_ge(masked, it * N + n + 1)
                    nc.vector.tensor_reduce(nm[:, n % 2, :], s[:, n % 2, :, :], AX.X, ALU.max, negate=True).then_inc(neg_done, 1)

                def normalize(n):
                    i = n % TT
                    dve.wait_ge(e_done, it * N + n + 1)
                    nc.vector.reciprocal(rl[:, n % 2, :], rowsum[:, n % 2, :]).then_inc(link, 1)
                    dve.wait_ge(link, it * (2 * N) + 2 * n + 1)
                    nc.vector.tensor_scalar(rla[:, n % 2, :], rl[:, n % 2, :], alive[:, i:i + 1], None, ALU.mult).then_inc(link, 1)
                    dve.wait_ge(link, it * (2 * N) + 2 * n + 2)
                    if n >= 2:
                        dve.wait_ge(t_done, it * N + n - 1)
                    nc.vector.tensor_tensor(pn[:, n % 2, :, :], e[:, n % 2, :, :],
                                            bcast(rla[:, n % 2, :].rearrange("p (j o) -> p j o", o=1), CMP_PAD),
                                            ALU.mult).then_inc(pn_done, 1)

                def pick(n):
                    i = n % TT
                    m = picks.index(n)
                    at = it * (7 * len(picks)) + 7 * m
                    dve.wait_ge(pn_done, it * N + n + 1)
                    nc.vector.tensor_reduce(both[:, 1:], pn[:, n % 2, :, :].rearrange("p j n -> p n j"), AX.X, ALU.add).then_inc(sel_link, 1)
                    dve.wait_ge(sel_link, at + 1)
                    nc.vector.tensor_reduce(quad[:], both[:, 1:].rearrange("p (m w) -> p m w", w=SLC // CMP_STRIDE), AX.X, ALU.add)\
                        .then_inc(sel_link, 1)
                    dve.wait_ge(sel_link, at + 2)
                    nc.vector.tensor_tensor(imp[:], quad[:], both[:, 0:CMP_PAD:SLC // CMP_STRIDE], ALU.add).then_inc(sel_link, 1)
                    dve.wait_ge(sel_link, at + 3)
                    nc.vector.tensor_tensor(score[:], imp[:], force[:, i, :], ALU.add).then_inc(sel_link, 1)
                    dve.wait_ge(sel_link, at + 4)
                    nc.vector.nop(nofuse=True)
                    nc.vector.max(top[:], score[:]).then_inc(sel_link, 1)
                    dve.wait_ge(sel_link, at + 5)
                    nc.vector.nop(nofuse=True)
                    nc.vector.match_replace(marked[:], top[:], score[:], PICKED).then_inc(sel_link, 1)
                    dve.wait_ge(sel_link, at + 6)
                    nc.vector.tensor_scalar(sel[:, :, i, :].rearrange("p (i s) n -> p i s n", s=2)[:, bass.ds(it, 1), n // TT, :]
                                            .rearrange("p o n -> p (o n)"), marked[:], PICKED, NEG, ALU.not_equal, ALU.mult)\
                        .then_inc(sel_link, 1)

                def output(n):
                    x, i = divmod(n, TT)
                    dve.wait_ge(o_done, it * N + n + 1)
                    dst = mixed[:, i, :].rearrange("p (i s j d) -> p i s j d", s=2, j=J, d=HD)[:, bass.ds(it, 1), x, :, :]
                    g = gates[:, i, 0:C_HEADS].rearrange("p (i s j) -> p i s j", s=2, j=J)[:, bass.ds(it, 1), x, :]
                    nc.vector.tensor_tensor(dst.rearrange("p o j d -> p (o j) d"),
                                            ps_o[:, n % 2, 0:J * HD].rearrange("p (j d) -> p j d", d=HD),
                                            bcast(g.rearrange("p o (j x) -> p (o j) x", x=1), HD), ALU.mult).then_inc(o_taken, 1)

                negate(0)
                negate(1)
                for n in range(N):
                    normalize(n)
                    if n in picks:
                        pick(n)
                    if n:
                        output(n - 1)
                    if n + 2 < N:
                        negate(n + 2)
                output(N - 1)


def dilated_bias_stage(nc, bias):
    reach = ((128, 1), (512, 4), (2048, 16))
    with Stage(nc, "dil") as st:
        d = st.sb("d", [P, SEQ], I32)
        r = st.sb("r", [P, SEQ], I32)
        df = st.sb("df", [P, SEQ])
        a = st.sb("a", [P, SEQ])
        b = st.sb("b", [P, SEQ])
        c = st.sb("c", [P, SEQ])
        step, iota_done = st.sem("step"), st.sem("iota_done")
        block = st.block()

        @block.gpsimd
        def _(pool):
            nc.gpsimd.iota(d[:], pattern=[[-1, SEQ]], base=SEQ - P, channel_multiplier=1).then_inc(iota_done, 1)
            pool.wait_ge(step, 15)
            nc.gpsimd.affine_select(out=bias[:], in_=a[:], compare_op=ALU.is_ge, fill=NEG, base=SEQ - P,
                                    pattern=[[-1, SEQ]], channel_multiplier=1)

        @block.vector
        def _(dve):
            dve.wait_ge(iota_done, 1)
            nc.vector.tensor_copy(df[:], d[:]).then_inc(step, 1)
            dve.wait_ge(step, 1)
            nc.vector.tensor_scalar(c[:], df[:], float(reach[0][0]), None, ALU.is_le).then_inc(step, 1)
            for n, (window, dilation) in enumerate(reach[1:]):
                at = 2 + 4 * n
                nc.vector.tensor_scalar(r[:], d[:], dilation - 1, None, ALU.bitwise_and).then_inc(step, 1)
                dve.wait_ge(step, at + 1)
                nc.vector.tensor_scalar(a[:], r[:], 0.0, None, ALU.is_equal).then_inc(step, 1)
                dve.wait_ge(step, at + 2)
                nc.vector.scalar_tensor_tensor(b[:], df[:], float(window), a[:], ALU.is_le, ALU.mult).then_inc(step, 1)
                dve.wait_ge(step, at + 3)
                nc.vector.tensor_tensor(c[:], c[:], b[:], ALU.add).then_inc(step, 1)
                dve.wait_ge(step, at + 4)
            nc.vector.tensor_scalar(a[:], c[:], 0.0, NEG, ALU.is_equal, ALU.mult).then_inc(step, 1)
            for n, count in enumerate((2, 3)):
                at = 11 + 2 * n
                nc.vector.tensor_scalar(b[:], c[:], float(count), math.log(count), ALU.is_equal, ALU.mult).then_inc(step, 1)
                dve.wait_ge(step, at + 1)
                nc.vector.tensor_tensor(a[:], a[:], b[:], ALU.add).then_inc(step, 1)
                dve.wait_ge(step, at + 2)


def distance_bias_stage(nc, causal, window):
    with Stage(nc, "dist") as st:
        step = st.sem("step")
        block = st.block()

        @block.gpsimd
        def _(pool):
            nc.gpsimd.memset(causal[:], 0.0).then_inc(step, 1)
            pool.wait_ge(step, 1)
            nc.gpsimd.affine_select(out=causal[:], in_=causal[:], compare_op=ALU.is_ge, fill=NEG, base=SEQ - P,
                                    pattern=[[-1, SEQ]], channel_multiplier=1).then_inc(step, 1)
            pool.wait_ge(step, 2)
            nc.gpsimd.affine_select(out=window[:], in_=causal[:], compare_op=ALU.is_ge, fill=NEG, base=WIN - 1 - (SEQ - P),
                                    pattern=[[1, SEQ]], channel_multiplier=-1)


def store_stage(nc, x_sb, out):
    with Stage(nc, "store") as st:
        x_out = st.sem("x_out")
        block = st.block()

        @block.sync
        def _(sp):
            sp.dma_start(out.rearrange("o (t p) d -> p (o t) d", p=P), x_sb[:]).then_inc(x_out, 16)
            sp.wait_ge(x_out, 16)


def trunk(nc, x, attn_norm, ffn_norm, hy_w_in, hy_lb_logits, hy_o_gain, hy_q_gain, hy_k_gain, hy_w_out, nsa_w_in,
          nsa_q_gain, nsa_k_gain, nsa_cmp_pe, nsa_cmp_w1, nsa_cmp_w2, nsa_w_out, ffn_w_gate, ffn_w_up, ffn_w_down, out):
    def slopes(n, first, count):
        return [2.0 ** (-8.0 * (h + 1) / n) for h in range(first, first + count)]

    def dram(name, shape):
        return nc.dram_tensor(name, shape, F32).ap()

    proj0 = dram("proj0", (SEQ, EVEN_IN))
    q0T, k0T = dram("q0T", (B_HEADS, HA, SEQ)), dram("k0T", (B_HEADS, HA, SEQ))
    proj1 = dram("proj1", (SEQ, ODD_IN))
    q1T = dram("q1T", (C_HEADS, HA, SEQ))
    kvT = dram("kvT", (4 * KV_HEADS, HA, SEQ))
    Q = 4 * HD

    with ExitStack() as whole:
        def sb(ctx, name, shape):
            return ctx.enter_context(nc.sbuf_tensor(name, shape, F32))

        x_sb = sb(whole, "x_sb", [P, TT, DM])
        ident = sb(whole, "ident", [P, P])
        load_stage(nc, x, x_sb, ident)

        def ffn(layer):
            with ExitStack() as c:
                actT = sb(c, f"actT{layer}", [P, D_FF // P, SEQ])
                with ExitStack() as c2:
                    hT = sb(c2, f"ffn_hT{layer}", [P, KD, SEQ])
                    transpose_stage(nc, f"fn{layer}", x_sb, hT, [(ffn_norm[layer, :], 0, KD)], ident, True)
                    ffn_stage(nc, f"up{layer}", hT, ffn_w_gate[layer, :, :], ffn_w_up[layer, :, :], actT)
                linear_stage(nc, f"down{layer}", actT, ffn_w_down[layer, :, :], D_FF // P, 256, DM, add_to=x_sb)

        with ExitStack() as c:
            hT = sb(c, "hT0", [P, KD, SEQ])
            transpose_stage(nc, "an0", x_sb, hT, [(attn_norm[0, :], 0, KD)], ident, True)
            linear_stage(nc, "in0", hT, hy_w_in[0, :, :], KD, BANK, EVEN_IN, dst_dram=proj0)
        with ExitStack() as c:
            mixed = sb(c, "mixed0", [P, TT, DM])
            hgrn_stage(nc, proj0, hy_lb_logits, mixed, ident)
            with ExitStack() as c2:
                bias = sb(c2, "bias0", [P, SEQ])
                dilated_bias_stage(nc, bias)
                at = 4 * A_WIDTH
                heads_stage(nc, "q0", proj0, q0T, [(at + Q * n, 4 * n, hy_q_gain[0, :], HD ** -0.5, slopes(B_HEADS, 4 * n, 4))
                                                   for n in range(2)], ident)
                at += B_HEADS * HD
                heads_stage(nc, "k0", proj0, k0T, [(at + Q * n, 4 * n, hy_k_gain[0, :], 1.0, None) for n in range(2)], ident)
                at += B_HEADS * HD
                attention_stage(nc, "at0", B_HEADS, q0T, [(k0T, proj0[:, at:at + B_HEADS * HD], 1, bias, TT, 0, False)],
                                mixed, A_WIDTH, ident)
            hT = sb(c, "mT0", [P, KD, SEQ])
            transpose_stage(nc, "mt0", mixed, hT, [(hy_o_gain[0, :], 0, A_WIDTH // P), (None, A_WIDTH // P, KD)], ident, False)
            linear_stage(nc, "out0", hT, hy_w_out[0, :, :], KD, BANK, DM, add_to=x_sb)
        ffn(0)

        with ExitStack() as c:
            hT = sb(c, "hT1", [P, KD, SEQ])
            transpose_stage(nc, "an1", x_sb, hT, [(attn_norm[1, :], 0, KD)], ident, True)
            main = DM + 6 * KV_W
            linear_stage(nc, "in1", hT, nsa_w_in[0, :, 0:main], KD, BANK, main, dst_dram=proj1[:, 0:main])
            linear_stage(nc, "gate1", hT, nsa_w_in[0, :, main:ODD_IN], KD, 3 * C_HEADS, 3 * C_HEADS, dst_dram=proj1[:, main:ODD_IN])
        with ExitStack() as c:
            mixed = sb(c, "mixed1", [P, TT, DM])
            with ExitStack() as c2:
                gates = sb(c2, "gates", [P, TT, 3 * C_HEADS])
                kcT = sb(c2, "kcT", [HA, KV_HEADS, CMP_PAD])
                vc = sb(c2, "vc", [CMP_PAD, KV_HEADS, HD])
                sel = sb(c2, "sel", [P, KV_HEADS, TT, N_SLC])
                causal, window = sb(c2, "causal", [P, SEQ]), sb(c2, "window", [P, SEQ])
                distance_bias_stage(nc, causal, window)
                heads_stage(nc, "q1", proj1, q1T, [(Q * n, 4 * n, nsa_q_gain[0, :], HD ** -0.5, slopes(C_HEADS, 4 * n, 4))
                                                   for n in range(4)], ident)
                heads_stage(nc, "k1", proj1, kvT,
                            [(DM, 0, None, 1.0, None), (DM + KV_W, 4, None, 1.0, None),
                             (DM + 2 * KV_W, 8, nsa_k_gain[0, 1, :], 1.0, None),
                             (DM + 4 * KV_W, 12, nsa_k_gain[0, 2, :], 1.0, None)], ident)
                compress_stage(nc, kvT, nsa_cmp_pe[0, :, :, :], nsa_cmp_w1[0, :, :, :], nsa_cmp_w2[0, :, :, :],
                               nsa_k_gain[0, 0, :], proj1[:, main:ODD_IN], kcT, vc, gates, ident)
                select_stage(nc, q1T, kcT, vc, gates, sel, mixed, ident)
                vs, vw = DM + 3 * KV_W, DM + 5 * KV_W
                attention_stage(nc, "at1", C_HEADS, q1T,
                                [(kvT[8:12, :, :], proj1[:, vs:vs + KV_W], GROUP, causal, TT, C_HEADS, True),
                                 (kvT[12:16, :, :], proj1[:, vw:vw + KV_W], GROUP, window, WIN // P + 1, 2 * C_HEADS, False)],
                                mixed, 0, ident, gates=gates, sel=sel)
            hT = sb(c, "mT1", [P, KD, SEQ])
            transpose_stage(nc, "mt1", mixed, hT, [(None, 0, KD)], ident, False)
            linear_stage(nc, "out1", hT, nsa_w_out[0, :, :], KD, BANK, DM, add_to=x_sb)
        ffn(1)
        store_stage(nc, x_sb, out)


_INS = ["x", "attn_norm", "ffn_norm", "hy_w_in", "hy_lb_logits", "hy_o_gain", "hy_q_gain", "hy_k_gain", "hy_w_out",
        "nsa_w_in", "nsa_q_gain", "nsa_k_gain", "nsa_cmp_pe", "nsa_cmp_w1", "nsa_cmp_w2", "nsa_w_out",
        "ffn_w_gate", "ffn_w_up", "ffn_w_down"]


def kernel(**inputs):
    import concourse.bacc as _bacc
    from concourse.bass_utils import run_bass_kernel_spmd as _run

    nc = _bacc.Bacc("TRN2", target_bir_lowering=False, num_devices=1)
    arrays, args = {}, []
    for name in _INS:
        a = np.ascontiguousarray(inputs[name])
        arrays[f"in_{name}"] = a
        args.append(nc.dram_tensor(f"in_{name}", a.shape, mybir.dt.from_np(a.dtype), kind="ExternalInput").ap())
    args.append(nc.dram_tensor("out_x", (1, SEQ, DM), F32, kind="ExternalOutput").ap())
    trunk(nc, *args)
    return _run(nc, [arrays], core_ids=[0]).results[0]["out_x"]
```

```python
import math
from contextlib import ExitStack

import concourse.bass as bass
import numpy as np
from concourse import mybir

F32 = mybir.dt.float32
F32R = mybir.dt.float32r
I32 = mybir.dt.int32
ALU = mybir.AluOpType
ACT = mybir.ActivationFunctionType
AX = mybir.AxisListType

P = 128
SEQ = 1024
DM = 1024
TT = SEQ // P
KD = DM // P
HD = 64
HA = HD + 2
EPS = 1e-6
NEG = -1e30
BANK = 512

A_WIDTH = DM // 2
A_HEADS = 4
B_HEADS = 8
EVEN_IN = 4 * A_WIDTH + 3 * (DM - A_WIDTH)

C_HEADS = 16
KV_HEADS = 4
GROUP = C_HEADS // KV_HEADS
KV_W = KV_HEADS * HD
ODD_IN = DM + 6 * KV_W + 3 * C_HEADS
CMP_LEN, CMP_STRIDE, CMP_HIDDEN = 32, 16, 2 * HD
N_CMP = (SEQ - CMP_LEN) // CMP_STRIDE + 1
CMP_PAD = 64
SLC = 64
N_SLC = SEQ // SLC
TOPN = 8
WIN = 512
D_FF = -(-8 * DM // (3 * 256)) * 256


class Stage:

    def __init__(self, nc, name):
        self.nc, self.name, self.ctx, self.sems = nc, name, ExitStack(), []

    def __enter__(self):
        self.ctx.__enter__()
        return self

    def __exit__(self, *e):
        done = self.ctx.__exit__(*e)
        if e[0] is None:
            self.nc.clear_and_free_semaphores(self.sems)
            self.nc.all_engine_barrier()
        return done

    def sb(self, name, shape, dt=F32):
        return self.ctx.enter_context(self.nc.sbuf_tensor(f"{self.name}_{name}", shape, dt))

    def ps(self, name, shape, dt=F32):
        return self.ctx.enter_context(self.nc.psum_tensor(f"{self.name}_{name}", shape, dt))

    def sem(self, name):
        self.sems.append(self.nc.alloc_semaphore(f"{self.name}_{name}"))
        return self.sems[-1]

    def block(self):
        return self.ctx.enter_context(self.nc.Block())


def bcast(ap, n):
    return ap.to_broadcast(list(ap.shape[:-1]) + [n])



def load_stage(nc, x, x_sb, ident):
    with Stage(nc, "load") as st:
        x_in, zeroed = st.sem("x_in"), st.sem("zeroed")
        block = st.block()

        @block.sync
        def _(sp):
            sp.dma_start(x_sb[:], x.rearrange("o (t p) d -> p (o t) d", p=P)).then_inc(x_in, 16)
            sp.wait_ge(x_in, 16)

        @block.gpsimd
        def _(pool):
            nc.gpsimd.memset(ident[:], 0.0).then_inc(zeroed, 1)
            pool.wait_ge(zeroed, 1)
            nc.gpsimd.affine_select(out=ident[:], in_=ident[:], compare_op=ALU.not_equal, fill=1.0, base=0,
                                    pattern=[[-1, P]], channel_multiplier=1)


def transpose_stage(nc, name, src, dst, gains, ident, norm):
    dst_hi, dst_lo = dst
    scaled = norm or gains
    with Stage(nc, name) as st:
        gain = st.sb("gain", [P, DM]) if gains else None
        sq = st.sb("sq", [P, 2, DM]) if norm else None
        h = st.sb("h", [P, 2, DM]) if scaled else None
        ss = st.sb("ss", [P, TT])
        ms = st.sb("ms", [P, TT])
        root = st.sb("root", [P, TT])
        rstd = st.sb("rstd", [P, TT])
        tr = st.ps("tr", [P, 4, BANK])
        gain_in, gain_set = st.sem("gain_in"), st.sem("gain_set")
        ss_done, ms_done, root_done, rstd_done = (st.sem(n) for n in ("ss_done", "ms_done", "root_done", "rstd_done"))
        h_done, tr_done, hi_done, lo_done = (st.sem(n) for n in ("h_done", "tr_done", "hi_done", "lo_done"))
        block = st.block()

        @block.sync
        def _(sp):
            if gains:
                sp.wait_ge(gain_set, 1)
                for g, lo, hi in gains:
                    row = g.rearrange("(o d) -> o d", o=1)
                    sp.dma_start(gain[:, lo:hi], row.to_broadcast([P, hi - lo])).then_inc(gain_in, 16)

        @block.gpsimd
        def _(pool):
            if gains:
                nc.gpsimd.memset(gain[:], 1.0).then_inc(gain_set, 1)

        @block.scalar
        def _(act):
            if norm:
                for t in range(TT):
                    if t >= 2:
                        act.wait_ge(ss_done, t - 1)
                    nc.scalar.activation(sq[:, t % 2, :], src[:, t, :], ACT.Square,
                                         accum_out=ss[:, t:t + 1]).then_inc(ss_done, 1)
                act.wait_ge(ms_done, 1)
                nc.scalar.activation(root[:], ms[:], ACT.Sqrt).then_inc(root_done, 1)
            for m in range(2 * TT):
                t, k0 = m // 2, (m % 2) * 4
                act.wait_ge(tr_done, m + 1)
                nc.scalar.activation(dst_hi[:, k0:k0 + 4, t * P:(t + 1) * P],
                                     tr[:, m % 4, :].rearrange("p (k c) -> p k c", c=P), ACT.Copy).then_inc(hi_done, 1)

        @block.vector
        def _(dve):
            if norm:
                dve.wait_ge(ss_done, TT)
                nc.vector.tensor_scalar(ms[:], ss[:], 1.0 / DM, EPS, ALU.mult, ALU.add).then_inc(ms_done, 1)
                dve.wait_ge(root_done, 1)
                nc.vector.reciprocal(rstd[:], root[:]).then_inc(rstd_done, 1)
                dve.wait_ge(rstd_done, 1)
            if gains:
                dve.wait_ge(gain_in, 16 * len(gains))
            for t in range(TT + 1):
                if t < TT and scaled:
                    if t >= 2:
                        dve.wait_ge(tr_done, 2 * (t - 1))
                    if norm:
                        nc.vector.scalar_tensor_tensor(h[:, t % 2, :], src[:, t, :], rstd[:, t:t + 1], gain[:], ALU.mult,
                                                       ALU.mult).then_inc(h_done, 1)
                    else:
                        nc.vector.tensor_tensor(h[:, t % 2, :], src[:, t, :], gain[:], ALU.mult).then_inc(h_done, 1)
                for half in range(2 if t else 0):
                    m = 2 * (t - 1) + half
                    k0 = half * 4
                    dve.wait_ge(hi_done, m + 1)
                    nc.vector.tensor_tensor(dst_lo[:, k0:k0 + 4, (t - 1) * P:t * P],
                                            tr[:, m % 4, :].rearrange("p (k c) -> p k c", c=P),
                                            dst_hi[:, k0:k0 + 4, (t - 1) * P:t * P].bitcast(F32), ALU.subtract).then_inc(lo_done, 1)

        @block.tensor
        def _(pe):
            for t in range(TT):
                if scaled:
                    pe.wait_ge(h_done, t + 1)
                for half in range(2):
                    m = 2 * t + half
                    if m >= 4:
                        pe.wait_ge(lo_done, m - 3)
                    for k in range(4):
                        kk = half * 4 + k
                        rows = h[:, t % 2, :] if scaled else src[:, t, :]
                        ins = nc.tensor.transpose(tr[:, m % 4, k * P:(k + 1) * P], rows[:, kk * P:(kk + 1) * P],
                                                  ident[:])
                    ins.then_inc(tr_done, 1)




def linear_stage(nc, name, lhsT, w, groups, width, dst_dram=None, add_to=None):
    kt, NG, G = sum(groups), len(groups), max(groups)
    cols = w.shape[1]
    n_chunks = cols // width
    start = [sum(groups[:g]) for g in range(NG)]
    to_dram = dst_dram is not None
    with Stage(nc, name) as st:
        raw = st.sb("raw", [P, 2, G, width])
        w_hi = st.sb("w_hi", [P, 2, G, width], F32R)
        w_lo = st.sb("w_lo", [P, 2, G, width], F32R)
        out = st.sb("out", [P, TT, width]) if to_dram else None
        acc = st.ps("acc", [P, TT, BANK])
        w_in = [st.sem(f"w_in{s}") for s in range(2)]
        hi_done, lo_done, used, acc_done, acc_free, y_out = (
            st.sem(n) for n in ("hi_done", "lo_done", "used", "acc_done", "acc_free", "y_out"))
        wc = w.rearrange("(k p) (c n) -> p k c n", p=P, n=width)
        if to_dram:
            dc = dst_dram.rearrange("(t p) (c n) -> p t c n", p=P, n=width)
        else:
            xc = add_to[:, :, :].rearrange("p t (c n) -> p t c n", n=width)
        block = st.block()

        def all_chunks(eng, step):
            step(0, True, n_chunks == 1)
            if n_chunks > 2:
                with eng.Fori(1, n_chunks - 1) as c:
                    step(c, False, False)
            if n_chunks > 1:
                step(n_chunks - 1, False, True)

        def order(c, last):
            return [(c, g) for g in range(1, NG)] + ([] if last else [(c + 1, 0)])

        @block.sync
        def _(sp):
            def load(c, g, ahead=0):
                k0 = start[g]
                chunk = wc[:, k0:k0 + groups[g], ahead:, :][:, :, bass.ds(c, 1), :]
                sp.dma_start(raw[:, g % 2, 0:groups[g], :], chunk.rearrange("p k o n -> p k (o n)"))\
                    .then_inc(w_in[g % 2], 16)

            load(0, 0)
            load(0, 1)

            def chunk(c, first, last):
                for g in range(NG):
                    n = g + 2
                    if n >= NG and last:
                        break
                    sp.wait_ge(hi_done, c * NG + g + 1)
                    sp.wait_ge(lo_done, c * NG + g + 1)
                    load(c, n % NG, n // NG)

            all_chunks(sp, chunk)

        @block.scalar
        def _(act):
            def split(c, g, first):
                act.wait_ge(w_in[g % 2], c * (16 * (NG // 2)) + 16 * (g // 2 + 1))
                if g >= 2:
                    act.wait_ge(used, c * (NG - 1) + g - 1)
                elif not first and g == 1:
                    act.wait_ge(acc_done, c * TT)
                elif not first:
                    act.wait_ge(used, c * (NG - 1))
                nc.scalar.activation(w_hi[:, g % 2, 0:groups[g], :], raw[:, g % 2, 0:groups[g], :], ACT.Copy)\
                    .then_inc(hi_done, 1)

            def chunk(c, first, last):
                for cc, g in order(c, last):
                    split(cc, g, first and g > 0)
                if to_dram:
                    if not first:
                        act.wait_ge(y_out, c * 16)
                    for t in range(TT):
                        act.wait_ge(acc_done, c * TT + t + 1)
                        nc.scalar.activation(out[:, t, :], acc[:, t, 0:width], ACT.Copy).then_inc(acc_free, 1)

            split(0, 0, True)
            all_chunks(act, chunk)

        @block.vector
        def _(dve):
            def split(c, g):
                dve.wait_ge(hi_done, c * NG + g + 1)
                nc.vector.tensor_tensor(w_lo[:, g % 2, 0:groups[g], :], raw[:, g % 2, 0:groups[g], :],
                                        w_hi[:, g % 2, 0:groups[g], :].bitcast(F32), ALU.subtract).then_inc(lo_done, 1)

            def chunk(c, first, last):
                for cc, g in order(c, last):
                    split(cc, g)
                if not to_dram:
                    for t in range(TT):
                        dve.wait_ge(acc_done, c * TT + t + 1)
                        xs = xc[:, t, bass.ds(c, 1), :].rearrange("p o n -> p (o n)")
                        nc.vector.tensor_tensor(xs, acc[:, t, 0:width], xs, ALU.add).then_inc(acc_free, 1)

            split(0, 0)
            all_chunks(dve, chunk)

        @block.tensor
        def _(pe):
            def chunk(c, first, last):
                for g in range(NG):
                    pe.wait_ge(lo_done, c * NG + g + 1)
                    for k in range(start[g], start[g] + groups[g]):
                        for t in range(TT):
                            if k == 0 and not first:
                                pe.wait_ge(acc_free, c * TT + t + 1 - TT)
                            x_hi, x_lo = (x[:, k, t * P:(t + 1) * P] for x in lhsT)
                            r_hi, r_lo = (x[:, g % 2, k - start[g], :] for x in (w_hi, w_lo))
                            nc.tensor.matmul(acc[:, t, 0:width], x_hi, r_hi, start=k == 0, stop=False)
                            nc.tensor.matmul(acc[:, t, 0:width], x_hi, r_lo, start=False, stop=False)
                            ins = nc.tensor.matmul(acc[:, t, 0:width], x_lo, r_hi, start=False, stop=k == kt - 1)
                            if k == kt - 1:
                                ins.then_inc(acc_done, 1)
                    if g < NG - 1:
                        ins.then_inc(used, 1)

            all_chunks(pe, chunk)

        @block.gpsimd
        def _(pool):
            def store(c, first, last):
                pool.wait_ge(acc_free, (c + 1) * TT)
                pool.dma_start(dc[:, :, bass.ds(c, 1), :].rearrange("p t o n -> p t (o n)"), out[:]).then_inc(y_out, 16)

            if to_dram:
                all_chunks(pool, store)
                pool.wait_ge(y_out, 16 * n_chunks)


def ffn_stage(nc, name, hT, w_gate, w_up, actT):
    NF = w_gate.shape[1] // P
    HALF = SEQ // 2
    with Stage(nc, name) as st:
        raw = st.sb("raw", [P, 2, KD, P])
        w_hi = st.sb("w_hi", [P, 2, KD, P], F32R)
        w_lo = st.sb("w_lo", [P, 2, KD, P], F32R)
        sg = st.sb("sg", [P, 2, HALF])
        acc = st.ps("acc", [P, 2, 2, BANK])
        w_in = [st.sem("gate_in"), st.sem("up_in")]
        split_hi = [st.sem("gate_hi"), st.sem("up_hi")]
        split_lo = [st.sem("gate_lo"), st.sem("up_lo")]
        acc_done = [st.sem("gate_done"), st.sem("up_done")]
        silu_done, prod_done, act_hi, act_lo = (st.sem(n) for n in ("silu_done", "prod_done", "act_hi", "act_lo"))
        views = [w.rearrange("(k p) (c n) -> p k c n", p=P, n=P) for w in (w_gate, w_up)]
        a_hi, a_lo = actT
        block = st.block()

        def at(a, f, half):
            return a[:, bass.ds(f, 1), half * HALF:(half + 1) * HALF].rearrange("p o n -> p (o n)")

        @block.sync
        def _(sp):
            def load(f, m, ahead=0):
                sp.dma_start(raw[:, m, :, :], views[m][:, :, ahead:, :][:, :, bass.ds(f, 1), :]
                             .rearrange("p k o n -> p k (o n)")).then_inc(w_in[m], 16)

            for m in range(2):
                load(0, m)
            with sp.Fori(0, NF - 1) as f:
                for m in range(2):
                    sp.wait_ge(split_hi[m], f + 1)
                    sp.wait_ge(split_lo[m], f + 1)
                    load(f, m, 1)

        @block.tensor
        def _(pe):
            def tile(f, first):
                for m in range(2):
                    pe.wait_ge(split_lo[m], f + 1)
                    if not first:
                        pe.wait_ge((silu_done, prod_done)[m], f * 2)
                    for k in range(KD):
                        for w, h in ((w_hi, hT[0]), (w_hi, hT[1]), (w_lo, hT[0])):
                            for half in range(2):
                                end = k == KD - 1 and w is w_lo
                                ins = nc.tensor.matmul(acc[:, m, half, :], w[:, m, k, :],
                                                       h[:, k, half * HALF:(half + 1) * HALF],
                                                       start=k == 0 and w is w_hi and h is hT[0], stop=end)
                                if end:
                                    ins.then_inc(acc_done[m], 1)

            tile(0, True)
            with pe.Fori(1, NF) as f:
                tile(f, False)

        @block.scalar
        def _(act):
            def split(f, m, first=False):
                act.wait_ge(w_in[m], f * 16 + 16)
                if not first:
                    act.wait_ge(acc_done[m], f * 2)
                nc.scalar.activation(w_hi[:, m, :, :], raw[:, m, :, :], ACT.Copy).then_inc(split_hi[m], 1)

            def tile(f, first, last):
                if not last:
                    split(f + 1, 0)
                for half in range(2):
                    act.wait_ge(acc_done[0], f * 2 + half + 1)
                    if not first:
                        act.wait_ge(act_lo, f * 2 + half - 1)
                    nc.scalar.activation(sg[:, half, :], acc[:, 0, half, :], ACT.Silu).then_inc(silu_done, 1)
                if not last:
                    split(f + 1, 1)
                for half in range(2):
                    act.wait_ge(prod_done, f * 2 + half + 1)
                    nc.scalar.activation(at(a_hi, f, half), sg[:, half, :], ACT.Copy).then_inc(act_hi, 1)

            split(0, 0, True)
            split(0, 1, True)
            tile(0, True, False)
            with act.Fori(1, NF - 1) as f:
                tile(f, False, False)
            tile(NF - 1, False, True)

        @block.vector
        def _(dve):
            def split(f, m):
                dve.wait_ge(split_hi[m], f + 1)
                nc.vector.tensor_tensor(w_lo[:, m, :, :], raw[:, m, :, :], w_hi[:, m, :, :].bitcast(F32),
                                        ALU.subtract).then_inc(split_lo[m], 1)

            def tile(f, last):
                if not last:
                    split(f + 1, 0)
                    split(f + 1, 1)
                for half in range(2):
                    dve.wait_ge(acc_done[1], f * 2 + half + 1)
                    dve.wait_ge(silu_done, f * 2 + half + 1)
                    nc.vector.tensor_tensor(sg[:, half, :], acc[:, 1, half, :], sg[:, half, :], ALU.mult).then_inc(prod_done, 1)
                for half in range(2):
                    dve.wait_ge(act_hi, f * 2 + half + 1)
                    nc.vector.tensor_tensor(at(a_lo, f, half), sg[:, half, :], at(a_hi, f, half).bitcast(F32),
                                            ALU.subtract).then_inc(act_lo, 1)

            split(0, 0)
            split(0, 1)
            with dve.Fori(0, NF - 1) as f:
                tile(f, False)
            tile(NF - 1, True)



def hgrn_stage(nc, proj, lb_logits, mixed, ident):
    HEADS, V, D8 = A_HEADS, A_WIDTH // A_HEADS, 8
    LEVELS = (64, 32, 16, 8)
    NL = len(LEVELS)
    BLK = SEQ // D8
    CB = P // D8
    width = [D8 - s for s in range(D8)]
    off = [BLK * sum(width[:s]) for s in range(D8 + 1)]
    TINY = 2.0 ** -64
    with Stage(nc, "hg") as st:
        qf = st.sb("qf", [P, 2, 2, TT, P])
        v = st.sb("v", [P, 2, TT, V])
        lb0 = st.sb("lb0", [P, HEADS])
        lbs = st.sb("lbs", [P, 6, HEADS])
        f = st.sb("f", [P, SEQ])
        fc = st.sb("fc", [P, SEQ])
        q = st.sb("q", [P, SEQ])
        k = st.sb("k", [P, SEQ])
        b = st.sb("b", [P, SEQ])
        reset = st.sb("reset", [P, SEQ])
        qb = st.sb("qb", [P, SEQ])
        decay = st.sb("decay", [P, TT])
        kl = st.sb("kl", [P, SEQ])
        lev = st.sb("lev", [P, NL, SEQ])
        near = st.sb("near", [P, off[D8]])
        pick = st.sb("pick", [P, D8, P])
        m_lev = st.sb("m_lev", [P, NL, P])
        m_near = st.sb("m_near", [P, P])
        sm = st.sb("sm", [P, 2, NL + 1, P])
        kt = st.sb("kt", [P, 2, P])
        state = st.sb("state", [P, 2, V])
        ps_tr = st.ps("ps_tr", [P, 2, BANK])
        ps_l = st.ps("ps_l", [P, 2, BANK])
        ps_n = st.ps("ps_n", [P, 1, BANK])
        ps_kb = st.ps("ps_k", [P, 1, BANK])
        ps_ub = st.ps("ps_u", [P, 1, BANK])
        ps_o = st.ps("ps_o", [P, 1, BANK])
        ps_k, ps_u = ps_kb[:, 0, 0:P], ps_ub[:, 0, 0:V]
        qf_in = [st.sem(f"qf_in{x}") for x in range(2)]
        v_in = [st.sem(f"v_in{x}") for x in range(2)]
        lb_in, lb_exp, lb_step, setup = st.sem("lb_in"), st.sem("lb_exp"), st.sem("lb_step"), st.sem("setup")
        tr_done, sig_done, f_done, q_done, k_done, lf_done, b_done = (
            st.sem(n) for n in ("tr_done", "sig_done", "f_done", "q_done", "k_done", "lf_done", "b_done"))
        diff_done, exp_done, g_done, near_k = st.sem("diff_done"), st.sem("exp_done"), st.sem("g_done"), st.sem("near_k")
        a_done, m_done, kt_done, o_done, u_done, state_done, o_taken = (
            st.sem(n) for n in ("a_done", "m_done", "kt_done", "o_done", "u_done", "state_done", "o_taken"))
        cols = lambda c0: proj[:, c0:c0 + A_WIDTH].rearrange("(t p) (i x v) -> p t i x v", p=P, x=2, v=V)
        q_cols, f_cols, v_cols = cols(0), cols(A_WIDTH), cols(2 * A_WIDTH)
        DIFFS = 1 + NL + 1
        EXPS = 1 + DIFFS
        PRODUCTS = 2 + NL + 1
        block = st.block()

        def halves(ap, h):
            w = ap.rearrange("p (n x h) -> p n x h", x=2, h=h)
            return w[:, :, 0, :], w[:, :, 1, :]

        def near_of(ap, s):
            w = ap.rearrange("p (n c) -> p n c", c=D8)
            return w[:, :, s:], w[:, :, s:s + 1].to_broadcast([P, BLK, width[s]])

        @block.sync
        def _(sp):
            with nc.allow_non_contiguous_dma(reason="a bound per partition"):
                sp.dma_start(lb0[:], lb_logits.rearrange("o (h k) -> k (o h)", k=P)).then_inc(lb_in, 16)

            def load(it, x):
                for n, src in enumerate((f_cols, q_cols)):
                    sp.dma_start(qf[:, x, n, :, :], src[:, :, bass.ds(it, 1), x, :].rearrange("p t o v -> p t (o v)")).then_inc(qf_in[x], 16)
                sp.dma_start(v[:, x, :, :], v_cols[:, :, bass.ds(it, 1), x, :].rearrange("p t o v -> p t (o v)")).then_inc(v_in[x], 16)

            for x in range(2):
                load(0, x)
            with sp.Fori(1, HEADS // 2) as it:
                for x in range(2):
                    sp.wait_ge(u_done, it * (2 * TT) + (x + 1) * TT - 2 * TT)
                    load(it, x)

        @block.gpsimd
        def _(pool):
            nc.gpsimd.memset(reset[:], 1.0).then_inc(setup, 1)
            nc.gpsimd.memset(pick[:], 0.0).then_inc(setup, 1)
            nc.gpsimd.memset(m_lev[:], 0.0).then_inc(setup, 1)
            nc.gpsimd.memset(m_near[:], 1.0).then_inc(setup, 1)
            pool.wait_ge(setup, 4)
            nc.gpsimd.memset(reset[:].rearrange("p (c t) -> p c t", t=P)[:, :, 0], 0.0)
            for s in range(D8):
                nc.gpsimd.memset(pick[:, s, :].rearrange("p (n c) -> p n c", c=D8)[:, :, s], 1.0)
            for n, h in enumerate(LEVELS):
                nc.gpsimd.memset(halves(m_lev[:, n, :], h)[1], 1.0)
            ins = nc.gpsimd.memset(state[:], 0.0)
            ins.then_inc(setup, 1)
            pool.wait_ge(setup, 5)
            for n, h in enumerate(LEVELS):
                right = halves(m_lev[:, n, :], h)[1]
                nc.gpsimd.affine_select(out=right, in_=right, compare_op=ALU.is_ge, fill=0.0, base=0,
                                        pattern=[[-2 * h, P // (2 * h)], [0, h]], channel_multiplier=1).then_inc(setup, 1)
            near_m = m_near[:].rearrange("p (n c) -> p n c", c=D8)
            nc.gpsimd.affine_select(out=near_m, in_=near_m, compare_op=ALU.is_ge, fill=0.0, base=0,
                                    pattern=[[-D8, CB], [0, D8]], channel_multiplier=1).then_inc(setup, 1)
            pool.wait_ge(setup, 6 + NL)
            for n, h in enumerate(LEVELS):
                right = halves(m_lev[:, n, :], h)[1]
                nc.gpsimd.affine_select(out=right, in_=right, compare_op=ALU.is_ge, fill=0.0, base=h - 1,
                                        pattern=[[2 * h, P // (2 * h)], [0, h]], channel_multiplier=-1).then_inc(setup, 1)
            nc.gpsimd.affine_select(out=near_m, in_=near_m, compare_op=ALU.is_ge, fill=0.0, base=D8 - 1,
                                    pattern=[[D8, CB], [0, D8]], channel_multiplier=-1).then_inc(setup, 1)

        @block.tensor
        def _(pe):
            with pe.Fori(0, HEADS // 2) as it:
                for x in range(2):
                    head = it * 2 + x
                    pe.wait_ge(qf_in[x], (it + 1) * 32)
                    for n in range(2):
                        if n:
                            pe.wait_ge(sig_done, head * 2 + 1)
                        elif x:
                            pe.wait_ge(q_done, head)
                        for t in range(TT):
                            ins = nc.tensor.transpose(ps_tr[:, t // 4, (t % 4) * P:(t % 4 + 1) * P], qf[:, x, n, t, :], ident[:])
                        ins.then_inc(tr_done, 1)

                    def scores(c):
                        if c >= 2:
                            pe.wait_ge(m_done, head * TT + c - 1)
                        for n in range(NL):
                            g = lev[:, n, c * P:(c + 1) * P]
                            nc.tensor.matmul(ps_l[:, c % 2, n * P:(n + 1) * P], g, g, start=True, stop=True)
                        if c:
                            pe.wait_ge(m_done, head * TT + c)
                        for s in range(D8):
                            pairs = near[:, off[s]:off[s + 1]].rearrange("p (n c) -> p n c", c=width[s])[:, c * CB:(c + 1) * CB, :]
                            nc.tensor.matmul(ps_n[:, 0, 0:P].rearrange("p (n c) -> p n c", c=D8)[:, :, s:], pick[:, s, :], pairs,
                                             start=s == 0, stop=s == D8 - 1, skip_group_check=True)
                        if c:
                            pe.wait_ge(kt_done, head * TT + c)
                        nc.tensor.transpose(ps_k, kl[:, c * P:(c + 1) * P], ident[:]).then_inc(a_done, 1)

                    def outputs(c):
                        pe.wait_ge(m_done, head * TT + c + 1)
                        if c:
                            pe.wait_ge(o_taken, head * TT + c)
                            pe.wait_ge(state_done, head * (TT - 1) + c)
                        for n in range(NL + 1):
                            ins = nc.tensor.matmul(ps_o[:, 0, 0:V], sm[:, c % 2, n, :], v[:, x, c, :], start=n == 0,
                                                   stop=c == 0 and n == NL)
                        if c:
                            ins = nc.tensor.matmul(ps_o[:, 0, 0:V], qb[:, c * P:(c + 1) * P], state[:, c % 2, :], start=False, stop=True)
                        ins.then_inc(o_done, 1)
                        pe.wait_ge(kt_done, head * TT + c + 1)
                        nc.tensor.matmul(ps_u, kt[:, c % 2, :], v[:, x, c, :], start=True, stop=True).then_inc(u_done, 1)

                    pe.wait_ge(v_in[x], (it + 1) * 16)
                    pe.wait_ge(setup, 7 + 2 * NL)
                    pe.wait_ge(g_done, (head + 1) * PRODUCTS)
                    scores(0)
                    for c in range(TT):
                        if c + 1 < TT:
                            scores(c + 1)
                        outputs(c)

        @block.scalar
        def _(act):
            act.wait_ge(lb_step, 1)
            nc.scalar.activation(lbs[:, 1, :], lbs[:, 0, :], ACT.Exp).then_inc(lb_exp, 1)
            with act.Fori(0, HEADS // 2) as it:
                for x in range(2):
                    head = it * 2 + x
                    flat = ps_tr[:, :, :].rearrange("p a b -> p (a b)")
                    act.wait_ge(tr_done, head * 2 + 1)
                    nc.scalar.activation(f[:], flat, ACT.Sigmoid).then_inc(sig_done, 1)
                    act.wait_ge(tr_done, head * 2 + 2)
                    nc.scalar.activation(q[:], flat, ACT.Sigmoid).then_inc(sig_done, 1)
                    act.wait_ge(f_done, head * 2 + 2)
                    nc.scalar.activation(fc[:], fc[:], ACT.Ln).then_inc(lf_done, 1)
                    act.wait_ge(b_done, head + 1)
                    nc.scalar.activation(decay[:], b[:].rearrange("p (c t) -> p c t", t=P)[:, :, P - 1], ACT.Exp)
                    nc.scalar.activation(qb[:], b[:], ACT.Exp).then_inc(exp_done, 1)
                    act.wait_ge(diff_done, head * DIFFS + 1)
                    nc.scalar.activation(kl[:], kl[:], ACT.Exp).then_inc(exp_done, 1)
                    for n in range(NL):
                        act.wait_ge(diff_done, head * DIFFS + 2 + n)
                        nc.scalar.activation(lev[:, n, :], lev[:, n, :], ACT.Exp).then_inc(exp_done, 1)
                    act.wait_ge(diff_done, head * DIFFS + 2 + NL)
                    nc.scalar.activation(near[:], near[:], ACT.Exp).then_inc(exp_done, 1)
                    dst = mixed[:, :, 0:A_WIDTH].rearrange("p t (i x v) -> p t i x v", x=2, v=V)
                    for c in range(TT + 1):
                        if c < TT:
                            act.wait_ge(a_done, head * TT + c + 1)
                            if c >= 2:
                                act.wait_ge(u_done, head * TT + c - 1)
                            nc.scalar.activation(kt[:, c % 2, :], ps_k, ACT.Copy).then_inc(kt_done, 1)
                        if c:
                            act.wait_ge(o_done, head * TT + c)
                            nc.scalar.activation(dst[:, c - 1, bass.ds(it, 1), x, :].rearrange("p o v -> p (o v)"),
                                                 ps_o[:, 0, 0:V], ACT.Copy).then_inc(o_taken, 1)

        @block.vector
        def _(dve):
            dve.wait_ge(lb_in, 16)
            nc.vector.tensor_tensor(lbs[:, 0, :], lb0[:], lb0[:], ALU.subtract).then_inc(lb_step, 1)
            dve.wait_ge(lb_exp, 1)
            nc.vector.reciprocal(lbs[:, 2, :], lbs[:, 1, :]).then_inc(lb_step, 1)
            dve.wait_ge(lb_step, 2)
            nc.vector.tensor_tensor(lbs[:, 3, :], lbs[:, 1, :], lbs[:, 2, :], ALU.mult).then_inc(lb_step, 1)
            dve.wait_ge(lb_step, 3)
            nc.vector.tensor_tensor(lbs[:, 4, :], lbs[:, 3, :], lbs[:, 3, :], ALU.subtract).then_inc(lb_step, 1)
            dve.wait_ge(lb_step, 4)
            nc.vector.tensor_scalar(lbs[:, 5, :], lbs[:, 4, :], -1.0, 1.0, ALU.mult, ALU.add).then_inc(lb_step, 1)
            dve.wait_ge(lb_step, 5)
            dve.wait_ge(setup, 7 + 2 * NL)
            with dve.Fori(0, HEADS // 2) as it:
                for x in range(2):
                    head = it * 2 + x
                    flat = ps_tr[:, :, :].rearrange("p a b -> p (a b)")
                    lb = lbs[:, 4, :].rearrange("p (i x) -> p i x", x=2)[:, bass.ds(it, 1), x]
                    one_lb = lbs[:, 5, :].rearrange("p (i x) -> p i x", x=2)[:, bass.ds(it, 1), x]
                    dve.wait_ge(sig_done, head * 2 + 1)
                    nc.vector.tensor_scalar(f[:], f[:], one_lb, lb, ALU.mult, ALU.add).then_inc(f_done, 1)
                    dve.wait_ge(f_done, head * 2 + 1)
                    nc.vector.tensor_scalar(fc[:], f[:], TINY, None, ALU.max).then_inc(f_done, 1)
                    nc.vector.tensor_scalar(k[:], f[:], -1.0, 1.0, ALU.mult, ALU.add).then_inc(k_done, 1)
                    dve.wait_ge(sig_done, head * 2 + 2)
                    nc.vector.tensor_tensor(q[:], flat, q[:], ALU.mult).then_inc(q_done, 1)
                    dve.wait_ge(lf_done, head + 1)
                    nc.vector.tensor_tensor_scan(b[:], reset[:], fc[:], 0.0, ALU.mult, ALU.add).then_inc(b_done, 1)
                    dve.wait_ge(b_done, head + 1)
                    b3 = b[:].rearrange("p (c t) -> p c t", t=P)
                    nc.vector.tensor_tensor(kl[:].rearrange("p (c t) -> p c t", t=P), b3[:, :, P - 1:P].to_broadcast([P, TT, P]), b3,
                                            ALU.subtract).then_inc(diff_done, 1)
                    for n, h in enumerate(LEVELS):
                        left, right = halves(b[:], h)
                        to_left, to_right = halves(lev[:, n, :], h)
                        middle = left[:, :, h - 1:h].to_broadcast([P, SEQ // (2 * h), h])
                        nc.vector.tensor_tensor(to_left, middle, left, ALU.subtract)
                        nc.vector.tensor_tensor(to_right, right, middle, ALU.subtract).then_inc(diff_done, 1)
                    for s in range(D8):
                        to = near[:, off[s]:off[s + 1]].rearrange("p (n c) -> p n c", c=width[s])
                        behind, key = near_of(b[:], s)
                        ins = nc.vector.tensor_tensor(to, behind, key, ALU.subtract)
                    ins.then_inc(diff_done, 1)
                    dve.wait_ge(exp_done, head * EXPS + 1)
                    dve.wait_ge(k_done, head + 1)
                    nc.vector.tensor_tensor(qb[:], qb[:], q[:], ALU.mult).then_inc(g_done, 1)
                    dve.wait_ge(exp_done, head * EXPS + 2)
                    nc.vector.tensor_tensor(kl[:], kl[:], k[:], ALU.mult).then_inc(g_done, 1)
                    for n, h in enumerate(LEVELS):
                        to_left, to_right = halves(lev[:, n, :], h)
                        dve.wait_ge(exp_done, head * EXPS + 3 + n)
                        nc.vector.tensor_tensor(to_left, to_left, halves(k[:], h)[0], ALU.mult)
                        nc.vector.tensor_tensor(to_right, to_right, halves(q[:], h)[1], ALU.mult).then_inc(g_done, 1)
                    dve.wait_ge(exp_done, head * EXPS + EXPS)
                    for s in range(D8):
                        to = near[:, off[s]:off[s + 1]].rearrange("p (n c) -> p n c", c=width[s])
                        ins = nc.vector.tensor_tensor(to, to, near_of(k[:], s)[1], ALU.mult)
                    ins.then_inc(near_k, 1)
                    dve.wait_ge(near_k, head + 1)
                    for s in range(D8):
                        to = near[:, off[s]:off[s + 1]].rearrange("p (n c) -> p n c", c=width[s])
                        ins = nc.vector.tensor_tensor(to, to, near_of(q[:], s)[0], ALU.mult)
                    ins.then_inc(g_done, 1)

                    def masks(c):
                        dve.wait_ge(a_done, head * TT + c + 1)
                        if c >= 2:
                            dve.wait_ge(o_done, head * TT + c - 1)
                        nc.vector.tensor_tensor(sm[:, c % 2, 0:NL, :], ps_l[:, c % 2, :].rearrange("p (n t) -> p n t", t=P),
                                                m_lev[:], ALU.mult)
                        nc.vector.tensor_tensor(sm[:, c % 2, NL, :], ps_n[:, 0, 0:P], m_near[:], ALU.mult).then_inc(m_done, 1)

                    masks(0)
                    for c in range(TT):
                        if c + 1 < TT:
                            masks(c + 1)
                            dve.wait_ge(u_done, head * TT + c + 1)
                            if c == 0:
                                nc.vector.tensor_copy(state[:, 1, :], ps_u).then_inc(state_done, 1)
                            else:
                                dve.wait_ge(state_done, head * (TT - 1) + c)
                                nc.vector.scalar_tensor_tensor(state[:, (c + 1) % 2, :], state[:, c % 2, :], decay[:, c:c + 1], ps_u,
                                                               ALU.mult, ALU.add).then_inc(state_done, 1)
    hgrn_out_stage(nc, proj, mixed)


def hgrn_out_stage(nc, proj, mixed):
    HEADS, V = A_HEADS, A_WIDTH // A_HEADS
    with Stage(nc, "hgo") as st:
        g = st.sb("g", [P, TT, A_WIDTH])
        sg = st.sb("sg", [P, TT, A_WIDTH])
        sq = st.sb("sq", [P, TT, A_WIDTH])
        ss = st.sb("ss", [P, TT, HEADS])
        ms = st.sb("ms", [P, TT, HEADS])
        root = st.sb("root", [P, TT, HEADS])
        rstd = st.sb("rstd", [P, TT, HEADS])
        g_in, sg_done, sq_done, norm, silu_done = (st.sem(n) for n in ("g_in", "sg_done", "sq_done", "norm", "silu_done"))
        block = st.block()
        o = mixed[:, :, 0:A_WIDTH]

        @block.sync
        def _(sp):
            sp.dma_start(g[:], proj[:, 3 * A_WIDTH:4 * A_WIDTH].rearrange("(t p) n -> p t n", p=P)).then_inc(g_in, 16)

        @block.scalar
        def _(act):
            nc.scalar.activation(sq[:], o, ACT.Square).then_inc(sq_done, 1)
            act.wait_ge(g_in, 16)
            nc.scalar.activation(sg[:], g[:], ACT.Sigmoid).then_inc(sg_done, 1)
            act.wait_ge(norm, 2)
            nc.scalar.activation(root[:], ms[:], ACT.Sqrt).then_inc(norm, 1)

        @block.vector
        def _(dve):
            dve.wait_ge(sq_done, 1)
            nc.vector.tensor_reduce(ss[:].rearrange("p t h -> p (t h)"), sq[:].rearrange("p t (h v) -> p (t h) v", v=V), AX.X, ALU.add)\
                .then_inc(norm, 1)
            dve.wait_ge(norm, 1)
            nc.vector.tensor_scalar(ms[:], ss[:], 1.0 / V, EPS, ALU.mult, ALU.add).then_inc(norm, 1)
            dve.wait_ge(sg_done, 1)
            nc.vector.tensor_tensor(sg[:], sg[:], g[:], ALU.mult).then_inc(silu_done, 1)
            dve.wait_ge(norm, 3)
            nc.vector.reciprocal(rstd[:], root[:]).then_inc(norm, 1)
            dve.wait_ge(norm, 4)
            o4 = o.rearrange("p t (h v) -> p t h v", v=V)
            nc.vector.tensor_tensor(o4, o4, rstd[:].rearrange("p t (h x) -> p t h x", x=1).to_broadcast([P, TT, HEADS, V]), ALU.mult)\
                .then_inc(norm, 1)
            dve.wait_ge(norm, 5)
            dve.wait_ge(silu_done, 1)
            nc.vector.tensor_tensor(o, o, sg[:], ALU.mult)



def heads_stage(nc, name, src, dst, quads, ident):
    Q = 4
    with Stage(nc, name) as st:
        raw = st.sb("raw", [P, 2, TT, Q, HD])
        sq = st.sb("sq", [P, TT, Q, HD])
        tok = st.sb("tok", [P, 2, TT, Q, HA])
        outT = st.sb("outT", [HA, 2, Q, SEQ])
        ss = st.sb("ss", [P, TT * Q])
        ms = st.sb("ms", [P, TT * Q])
        root = st.sb("root", [P, TT * Q])
        rstd = st.sb("rstd", [P, TT * Q])
        pos_i = st.sb("pos_i", [P, TT], I32)
        pos = st.sb("pos", [P, TT])
        gains = st.sb("gains", [HA, len(quads)])
        gsc = st.sb("gsc", [HA, len(quads)])
        tr = st.ps("tr", [HA, TT, BANK])
        raw_in = [st.sem(f"raw_in{s}") for s in range(2)]
        outT_out = [st.sem(f"outT_out{s}") for s in range(2)]
        gain_in, setup, gsc_done = st.sem("gain_in"), st.sem("setup"), st.sem("gsc_done")
        sq_done, ss_done, ms_done, root_done, rstd_done = (
            st.sem(n) for n in ("sq_done", "ss_done", "ms_done", "root_done", "rstd_done"))
        aug_done, tok_done, tr_done = st.sem("aug_done"), st.sem("tok_done"), st.sem("tr_done")
        taken = [st.sem("taken_act"), st.sem("taken_dve")]
        normed = [n for n, q in enumerate(quads) if q[2] is not None]
        sv = src.rearrange("(t p) n -> p t n", p=P)
        block = st.block()

        @block.sync
        def _(sp):
            sp.wait_ge(setup, 1)
            with nc.allow_non_contiguous_dma(reason="a gain per partition"):
                for n in normed:
                    sp.dma_start(gains[0:HD, n:n + 1], quads[n][2].rearrange("(d o) -> d o", o=1)).then_inc(gain_in, 16)
            for n, (col, *_) in enumerate(quads):
                if n >= 2:
                    sp.wait_ge(tok_done, n - 1)
                sp.dma_start(raw[:, n % 2, :, :, :],
                             sv[:, :, col:col + Q * HD].rearrange("p t (h d) -> p t h d", d=HD)).then_inc(raw_in[n % 2], 16)

        @block.gpsimd
        def _(pool):
            nc.gpsimd.memset(gains[:], 1.0).then_inc(setup, 1)
            nc.gpsimd.iota(pos_i[:], pattern=[[P, TT]], base=0, channel_multiplier=1).then_inc(setup, 1)
            pool.wait_ge(setup, 2)
            nc.gpsimd.tensor_copy(pos[:], pos_i[:]).then_inc(setup, 1)
            pool.wait_ge(setup, 3)
            for n, (_, _, _, _, slopes) in enumerate(quads):
                s = n % 2
                if n >= 2:
                    pool.wait_ge(tr_done, (n - 1) * TT)
                for h in range(Q):
                    for r, ap in ((HD, tok[:, s, :, h, HD:HD + 1]), (HD + 1, tok[:, s, :, h, HD + 1:HA])):
                        ap = ap.rearrange("p t o -> p (t o)")
                        if slopes is not None and r == HD:
                            ins = nc.gpsimd.memset(ap, slopes[h])
                        elif slopes is not None:
                            ins = nc.gpsimd.tensor_scalar(ap, pos[:], -slopes[h], 1.0, ALU.mult, ALU.mult)
                        elif r == HD:
                            ins = nc.gpsimd.tensor_copy(ap, pos[:])
                        else:
                            ins = nc.gpsimd.memset(ap, 1.0)
                ins.then_inc(aug_done, 1)

            for n, (_, h0, *_) in enumerate(quads):
                for who in range(2):
                    pool.wait_ge(taken[who], (n + 1) * (TT // 2))
                pool.dma_start(dst[h0:h0 + Q, :, :].rearrange("h r t -> r h t"), outT[:, n % 2, :, :])\
                    .then_inc(outT_out[n % 2], 16)
            for s in range(2):
                pool.wait_ge(outT_out[s], 16 * ((len(quads) + 1 - s) // 2))

        def take(eng, who, n):
            if n >= 2:
                eng.wait_ge(outT_out[n % 2], 16 * (n // 2))
            if n == 0:
                eng.wait_ge(gsc_done, 1)
            for t in range(who, TT, 2):
                eng.wait_ge(tr_done, n * TT + t + 1)
                to, of = outT[:, n % 2, :, t * P:(t + 1) * P], tr[:, t, :].rearrange("r (h c) -> r h c", c=P)
                if who == 0:
                    nc.scalar.activation(to, of, ACT.Copy, scale=gsc[:, n:n + 1]).then_inc(taken[0], 1)
                else:
                    nc.vector.tensor_scalar(to, of, gsc[:, n:n + 1], None, ALU.mult).then_inc(taken[1], 1)

        @block.scalar
        def _(act):
            for n in range(len(quads) + 1):
                if n < len(quads) and n in normed:
                    i = normed.index(n)
                    act.wait_ge(raw_in[n % 2], 16 * (n // 2 + 1))
                    if i:
                        act.wait_ge(ss_done, i)
                    nc.scalar.activation(sq[:], raw[:, n % 2, :, :, :], ACT.Square).then_inc(sq_done, 1)
                    act.wait_ge(ms_done, i + 1)
                    nc.scalar.activation(root[:], ms[:], ACT.Sqrt).then_inc(root_done, 1)
                if n:
                    take(act, 0, n - 1)

        @block.vector
        def _(dve):
            dve.wait_ge(gain_in, 16 * len(normed))
            for n, q in enumerate(quads):
                ins = nc.vector.tensor_scalar(gsc[0:HD, n:n + 1], gains[0:HD, n:n + 1], q[3], None, ALU.mult)
            nc.vector.tensor_copy(gsc[HD:HA, :], gains[HD:HA, :]).then_inc(gsc_done, 1)
            for n in range(len(quads) + 1):
                if n < len(quads):
                    s = n % 2
                    dve.wait_ge(raw_in[s], 16 * (n // 2 + 1))
                    if n in normed:
                        i = normed.index(n)
                        dve.wait_ge(sq_done, i + 1)
                        nc.vector.tensor_reduce(ss[:], sq[:].rearrange("p t h d -> p (t h) d"), AX.X, ALU.add)\
                            .then_inc(ss_done, 1)
                        dve.wait_ge(ss_done, i + 1)
                        nc.vector.tensor_scalar(ms[:], ss[:], 1.0 / HD, EPS, ALU.mult, ALU.add).then_inc(ms_done, 1)
                        dve.wait_ge(root_done, i + 1)
                        nc.vector.reciprocal(rstd[:], root[:]).then_inc(rstd_done, 1)
                        dve.wait_ge(rstd_done, i + 1)
                    if n >= 2:
                        dve.wait_ge(tr_done, (n - 1) * TT)
                    if n in normed:
                        nc.vector.tensor_tensor(
                            tok[:, s, :, :, 0:HD].rearrange("p t h d -> p (t h) d"),
                            raw[:, s, :, :, :].rearrange("p t h d -> p (t h) d"),
                            bcast(rstd[:].rearrange("p (a o) -> p a o", o=1), HD), ALU.mult).then_inc(tok_done, 1)
                    else:
                        nc.vector.tensor_copy(tok[:, s, :, :, 0:HD].rearrange("p t h d -> p (t h) d"),
                                              raw[:, s, :, :, :].rearrange("p t h d -> p (t h) d")).then_inc(tok_done, 1)
                if n:
                    take(dve, 1, n - 1)

        @block.tensor
        def _(pe):
            for n in range(len(quads)):
                pe.wait_ge(tok_done, n + 1)
                pe.wait_ge(aug_done, n + 1)
                for t in range(TT):
                    if n:
                        pe.wait_ge(taken[t % 2], (n - 1) * (TT // 2) + t // 2 + 1)
                    for h in range(Q):
                        ins = nc.tensor.transpose(tr[:, t, h * P:(h + 1) * P], tok[:, n % 2, t, h, :], ident[:])
                    ins.then_inc(tr_done, 1)


def attention_stage(nc, name, n_heads, qT, branches, mixed, col0, ident, gates=None, sel=None):
    NB = len(branches)
    ROUNDS = n_heads // 2
    U = NB * TT
    units = [(hh, br, i, min(i + 1, branches[br][4])) for hh in range(2) for br in range(NB) for i in range(TT)]
    N = len(units)
    chunks = []
    of_unit = []
    for n, (_, _, _, nk) in enumerate(units):
        of_unit.append(range(len(chunks), len(chunks) + -(-nk // 4)))
        chunks += [(n, j, min(4, nk - j)) for j in range(0, nk, 4)]
    C = len(chunks)
    nth = [c // 2 for c in range(C)]
    per = [(C + 1) // 2, C // 2]
    selected = [n for n, (_, br, i, _) in enumerate(units) if branches[br][6] and i >= TOPN * SLC // P]
    loads = 1 + 2 * NB
    with Stage(nc, name) as st:
        q = st.sb("q", [HA, 2, SEQ])
        k = st.sb("k", [HA, 2, NB, SEQ])
        v = st.sb("v", [P, 2, NB, TT, HD])
        sb = st.sb("s", [P, 2, SEQ])
        pr = st.sb("p", [P, 2, SEQ])
        pt = st.sb("pt", [P, 4, BANK])
        nm = st.sb("nm", [P, N])
        rowsum = st.sb("rowsum", [P, N])
        rl = st.sb("rl", [P, 2 * NB, TT])
        sc = st.sb("sc", [P, 2 * NB, TT])
        o_sb = st.sb("o", [P, TT, HD])
        mask = st.sb("mask", [P, 2, SEQ]) if sel is not None else None
        ps_s = st.ps("ps_s", [P, 2, 2 * BANK])
        ps_t = st.ps("ps_t", [P, 2, BANK])
        ps_o = st.ps("ps_o", [P, 2, BANK])
        in_sem = [st.sem(f"in{s}") for s in range(2)]
        s_done, neg_done, e_done, t_done, pv_done, o_free, step, mask_done, mask_free = (
            st.sem(x) for x in ("s_done", "neg_done", "e_done", "t_done", "pv_done", "o_free", "step", "mask_done", "mask_free"))
        pt_done = [st.sem("pt_done_dve"), st.sem("pt_done_act")]
        qv = qT.rearrange("(i s) r t -> i s r t", s=2)
        kvs = []
        for kT, vd, group, *_ in branches:
            vv = vd.rearrange("(t p) (g d) -> p t g d", p=P, d=HD)
            kvs.append((kT, vv, group))
        bank_of = lambda hh, br: (hh * NB + br) % 2
        evacs = 2 * NB
        block = st.block()

        @block.sync
        def _(sp):
            def load(it, s):
                sp.dma_start(q[:, s, :], qv[bass.ds(it, 1), s, :, :].rearrange("o r t -> (o r) t")).then_inc(in_sem[s], 16)
                for b, (kT, vv, group) in enumerate(kvs):
                    if group == 1:
                        ks = kT.rearrange("(i s) r t -> i s r t", s=2)[bass.ds(it, 1), s, :, :]
                        vs = vv.rearrange("p t (i s) d -> p t i s d", s=2)[:, :, bass.ds(it, 1), s, :]
                    else:
                        g = it // (group // 2)
                        ks, vs = kT[bass.ds(g, 1), :, :], vv[:, :, bass.ds(g, 1), :]
                    sp.dma_start(k[:, s, b, :], ks.rearrange("o r t -> (o r) t")).then_inc(in_sem[s], 16)
                    sp.dma_start(v[:, s, b, :, :], vs.rearrange("p t o d -> p t (o d)")).then_inc(in_sem[s], 16)

            for s in range(2):
                load(0, s)
            with sp.Fori(1, ROUNDS) as it:
                for s in range(2):
                    sp.wait_ge(pv_done, it * N + (s + 1) * U - N)
                    load(it, s)

        @block.tensor
        def _(pe):
            with pe.Fori(0, ROUNDS) as it:
                def scores(n):
                    hh, br, i, nk = units[n]
                    if n % U == 0:
                        pe.wait_ge(in_sem[hh], (it + 1) * (16 * loads))
                    if n >= 2:
                        pe.wait_ge(neg_done, it * N + n - 1)
                    k0 = (i + 1 - nk) * P
                    for j in range(0, nk * P, BANK):
                        w = min(BANK, nk * P - j)
                        ins = nc.tensor.matmul(ps_s[:, n % 2, j:j + w], q[:, hh, i * P:(i + 1) * P],
                                               k[:, hh, br, k0 + j:k0 + j + w], start=True, stop=True)
                    ins.then_inc(s_done, 1)

                def transposes(n):
                    pe.wait_ge(e_done, it * N + n + 1)
                    for c in of_unit[n]:
                        _, j0, w = chunks[c]
                        if c >= 2:
                            pe.wait_ge(pt_done[c % 2], it * per[c % 2] + nth[c])
                        for j in range(w):
                            ins = nc.tensor.transpose(ps_t[:, c % 2, j * P:(j + 1) * P],
                                                      pr[:, n % 2, (j0 + j) * P:(j0 + j + 1) * P], ident[:])
                        ins.then_inc(t_done, 1)

                def values(n):
                    hh, br, i, nk = units[n]
                    if i == 0:
                        pe.wait_ge(o_free, it * evacs + hh * NB + br + 1)
                    for c in of_unit[n]:
                        _, j0, w = chunks[c]
                        pe.wait_ge(pt_done[c % 2], it * per[c % 2] + nth[c] + 1)
                        for j in range(j0, j0 + w):
                            ins = nc.tensor.matmul(ps_o[:, bank_of(hh, br), i * HD:(i + 1) * HD],
                                                   pt[:, c % 4, (j - j0) * P:(j - j0 + 1) * P],
                                                   v[:, hh, br, i + 1 - nk + j, :], start=j == 0, stop=j == nk - 1)
                    ins.then_inc(pv_done, 1)

                scores(0)
                scores(1)
                for n in range(N):
                    transposes(n)
                    if n:
                        values(n - 1)
                    if n + 2 < N:
                        scores(n + 2)
                values(N - 1)

        def copies(eng, who, it, n):
            for c in of_unit[n]:
                if c % 2 != who:
                    continue
                eng.wait_ge(t_done, it * C + c + 1)
                if c >= 4:
                    eng.wait_ge(pv_done, it * N + chunks[c - 4][0] + 1)
                w = chunks[c][2] * P
                if who:
                    nc.scalar.activation(pt[:, c % 4, 0:w], ps_t[:, c % 2, 0:w], ACT.Copy).then_inc(pt_done[1], 1)
                else:
                    nc.vector.tensor_copy(pt[:, c % 4, 0:w], ps_t[:, c % 2, 0:w]).then_inc(pt_done[0], 1)

        @block.scalar
        def _(act):
            with act.Fori(0, ROUNDS) as it:
                def exps(n):
                    w = units[n][3] * P
                    act.wait_ge(neg_done, it * N + n + 1)
                    if n >= 2:
                        act.wait_ge(t_done, it * C + of_unit[n - 2][-1] + 1)
                    nc.scalar.activation(pr[:, n % 2, 0:w], sb[:, n % 2, 0:w], ACT.Exp, bias=nm[:, n:n + 1],
                                         scale=-1.0, accum_out=rowsum[:, n:n + 1]).then_inc(e_done, 1)

                exps(0)
                exps(1)
                for n in range(N):
                    copies(act, 1, it, n)
                    if n + 2 < N:
                        exps(n + 2)

        @block.vector
        def _(dve):
            nc.vector.memset(o_sb[:], 0.0).then_inc(o_free, 2)
            with dve.Fori(0, ROUNDS) as it:
                def negate(n):
                    hh, br, i, nk = units[n]
                    w = nk * P
                    dve.wait_ge(s_done, it * N + n + 1)
                    if n >= 2:
                        dve.wait_ge(e_done, it * N + n - 1)
                    if n in selected:
                        m = selected.index(n)
                        dve.wait_ge(mask_done, it * len(selected) + m + 1)
                        bias = mask[:, m % 2, 0:w]
                    else:
                        bias = branches[br][3][:, SEQ - w:SEQ]
                    nc.vector.nop(nofuse=True)
                    ins = nc.vector.tensor_tensor_reduce(out=sb[:, n % 2, 0:w], in0=ps_s[:, n % 2, 0:w], in1=bias,
                                                         scale=-1.0, scalar=3e38, op0=ALU.add, op1=ALU.min,
                                                         accum_out=nm[:, n:n + 1])
                    ins.then_inc(neg_done, 1)

                def output(hh, br):
                    b = hh * NB + br
                    n0 = hh * U + br * TT
                    links = 1 if gates is None else 2
                    done = (it * evacs + b) * links
                    dst = mixed[:, :, col0:col0 + n_heads * HD].rearrange("p t (i s d) -> p t i s d", s=2, d=HD)
                    dst = dst[:, :, bass.ds(it, 1), hh, :].rearrange("p t o d -> p t (o d)")
                    bank = ps_o[:, bank_of(hh, br), :].rearrange("p (t d) -> p t d", d=HD)
                    dve.wait_ge(pv_done, it * N + n0 + TT)
                    nc.vector.reciprocal(rl[:, b, :], rowsum[:, n0:n0 + TT]).then_inc(step, 1)
                    dve.wait_ge(step, done + 1)
                    if gates is None:
                        nc.vector.tensor_tensor(dst, bank, bcast(rl[:, b, :].rearrange("p (t o) -> p t o", o=1), HD),
                                                ALU.mult).then_inc(o_free, 1)
                        return
                    g = gates[:, :, branches[br][5]:branches[br][5] + n_heads].rearrange("p t (i s) -> p t i s", s=2)
                    nc.vector.tensor_tensor(sc[:, b, :], rl[:, b, :],
                                            g[:, :, bass.ds(it, 1), hh].rearrange("p t o -> p (t o)"),
                                            ALU.mult).then_inc(step, 1)
                    dve.wait_ge(step, done + 2)
                    nc.vector.tensor_tensor(o_sb[:], bank, bcast(sc[:, b, :].rearrange("p (t o) -> p t o", o=1), HD),
                                            ALU.mult).then_inc(o_free, 1)
                    dve.wait_ge(o_free, it * evacs + b + 3)
                    nc.vector.tensor_tensor(dst, o_sb[:], dst, ALU.add)

                negate(0)
                negate(1)
                for n in range(N):
                    copies(dve, 0, it, n)
                    if n + 2 < N:
                        negate(n + 2)
                    if n % TT == 1 and n > TT:
                        output(units[n - TT][0], units[n - TT][1])
                output(1, NB - 1)

        @block.gpsimd
        def _(pool):
            if sel is None:
                return
            bias = branches[0][3]
            with pool.Fori(0, ROUNDS) as it:
                for m, n in enumerate(selected):
                    _, _, i, nk = units[n]
                    w = nk * P
                    if m >= 2:
                        pool.wait_ge(neg_done, it * N + selected[m - 2] + 1)
                    else:
                        pool.wait_ge(s_done, it * N + 1)
                    picked = sel[:, bass.ds(it // (GROUP // 2), 1), i, 0:w // SLC].rearrange("p o (m x) -> p (o m) x", x=1)
                    pool.nop(nofuse=True)
                    nc.gpsimd.tensor_tensor(mask[:, m % 2, 0:w].rearrange("p (m c) -> p m c", c=SLC),
                                            bias[:, SEQ - w:SEQ].rearrange("p (m c) -> p m c", c=SLC),
                                            bcast(picked, SLC), ALU.add).then_inc(mask_done, 1)



def compress_stage(nc, kvT, pe, w1, w2, k_gain, gate_cols, kcT, vc, gates, ident):
    G = KV_HEADS
    NW = N_CMP
    with Stage(nc, "cmp") as st:
        t_in = st.sb("t_in", [HD, 2, G, SEQ])
        w1s = st.sb("w1s", [HD, 2, CMP_LEN, CMP_HIDDEN])
        w2s = st.sb("w2s", [CMP_HIDDEN, 2, HD])
        pes = st.sb("pes", [2 * CMP_LEN, HD])
        peT = st.sb("peT", [HD, 2 * CMP_LEN])
        gain = st.sb("gain", [HA, 1])
        g_raw = st.sb("g_raw", [P, TT, 3 * C_HEADS])
        pb = st.sb("pb", [CMP_HIDDEN, 2])
        hid = st.sb("hid", [CMP_HIDDEN, 2, G * NW])
        sq = st.sb("sq", [NW, G, HD])
        ss = st.sb("ss", [NW, G])
        ms = st.sb("ms", [NW, G])
        root = st.sb("root", [NW, G])
        rstd = st.sb("rstd", [NW, G])
        pos_i = st.sb("pos_i", [CMP_PAD, 1], I32)
        ktok = st.sb("ktok", [CMP_PAD, G, HA])
        ps_h = st.ps("ps_h", [CMP_HIDDEN, 2, BANK])
        ps_b = st.ps("ps_b", [CMP_HIDDEN, 2, BANK])
        ps_c = st.ps("ps_c", [CMP_PAD, 2, BANK])
        ps_t = st.ps("ps_t", [P, 1, BANK])
        pe_in, in_sem, g_in, gain_in = st.sem("pe_in"), st.sem("in"), st.sem("g_in"), st.sem("gain_in")
        peT_ready, peT_done, bias_ready, pb_done, hid_ready, hid_done, c_ready = (
            st.sem(x) for x in ("peT_ready", "peT_done", "bias_ready", "pb_done", "hid_ready", "hid_done", "c_ready"))
        norm, sq_done, ktok_set, ktok_done, tr_ready, gain_set = (
            st.sem(x) for x in ("norm", "sq_done", "ktok_set", "ktok_done", "tr_ready", "gain_set"))
        block = st.block()

        @block.sync
        def _(sp):
            sp.dma_start(pes[:], pe.rearrange("v l d -> (v l) d")).then_inc(pe_in, 16)
            for v in range(2):
                sp.dma_start(w1s[:, v, :, :], w1[v, :, :].rearrange("(l d) h -> d l h", d=HD)).then_inc(in_sem, 16)
                sp.dma_start(w2s[:, v, :], w2[v, :, :]).then_inc(in_sem, 16)
                sp.dma_start(t_in[:, v, :, :], kvT[v * G:(v + 1) * G, 0:HD, :].rearrange("g r t -> r g t")).then_inc(in_sem, 16)
            sp.dma_start(g_raw[:], gate_cols.rearrange("(t p) n -> p t n", p=P)).then_inc(g_in, 16)
            sp.wait_ge(gain_set, 1)
            with nc.allow_non_contiguous_dma(reason="a gain per partition"):
                sp.dma_start(gain[0:HD, :], k_gain.rearrange("(d o) -> d o", o=1)).then_inc(gain_in, 16)

        @block.gpsimd
        def _(pool):
            nc.gpsimd.memset(gain[:], 1.0).then_inc(gain_set, 1)
            nc.gpsimd.iota(pos_i[:], pattern=[[0, 1]], base=CMP_LEN - 1, channel_multiplier=CMP_STRIDE).then_inc(ktok_set, 1)
            nc.gpsimd.memset(ktok[:], 0.0).then_inc(ktok_set, 1)
            nc.gpsimd.memset(vc[:], 0.0).then_inc(ktok_set, 1)
            pool.wait_ge(ktok_set, 3)
            for g in range(G):
                nc.gpsimd.tensor_copy(ktok[:, g, HD:HD + 1], pos_i[:])
                ins = nc.gpsimd.memset(ktok[:, g, HD + 1:HA], 1.0)
            ins.then_inc(ktok_set, 1)

        @block.tensor
        def _(te):
            te.wait_ge(pe_in, 16)
            nc.tensor.transpose(ps_t[0:HD, 0, 0:2 * CMP_LEN], pes[:], ident[0:2 * CMP_LEN, 0:2 * CMP_LEN]).then_inc(peT_ready, 1)
            te.wait_ge(in_sem, 16 * 6)
            te.wait_ge(peT_done, 1)
            for v in range(2):
                for l in range(CMP_LEN):
                    ins = nc.tensor.matmul(ps_b[:, v, 0:1], w1s[:, v, l, :], peT[:, v * CMP_LEN + l:v * CMP_LEN + l + 1],
                                           start=l == 0, stop=l == CMP_LEN - 1)
                ins.then_inc(bias_ready, 1)
            for v in range(2):
                for l in range(CMP_LEN):
                    windows = t_in[:, v, :, l:l + CMP_STRIDE * (NW - 1) + 1:CMP_STRIDE]
                    ins = nc.tensor.matmul(ps_h[:, v, 0:G * NW].rearrange("p (g n) -> p g n", n=NW), w1s[:, v, l, :],
                                           windows, start=l == 0, stop=l == CMP_LEN - 1)
                ins.then_inc(hid_ready, 1)
            for v in range(2):
                te.wait_ge(hid_done, v + 1)
                for g in range(G):
                    ins = nc.tensor.matmul(ps_c[0:NW, v, g * HD:(g + 1) * HD], hid[:, v, g * NW:(g + 1) * NW], w2s[:, v, :],
                                           start=True, stop=True)
                ins.then_inc(c_ready, 1)
            te.wait_ge(ktok_done, 1)
            for g in range(G):
                ins = nc.tensor.transpose(ps_t[0:HA, 0, g * CMP_PAD:(g + 1) * CMP_PAD], ktok[:, g, :], ident[0:CMP_PAD, 0:CMP_PAD])
            ins.then_inc(tr_ready, 1)

        @block.scalar
        def _(act):
            act.wait_ge(bias_ready, 2)
            nc.scalar.activation(pb[:], ps_b[:, :, 0:1].rearrange("p v o -> p (v o)"), ACT.Copy).then_inc(pb_done, 1)
            act.wait_ge(pb_done, 1)
            for v in range(2):
                act.wait_ge(hid_ready, v + 1)
                nc.scalar.activation(hid[:, v, :], ps_h[:, v, 0:G * NW], ACT.Silu, bias=pb[:, v:v + 1]).then_inc(hid_done, 1)
            act.wait_ge(c_ready, 1)
            nc.scalar.activation(sq[:], ps_c[0:NW, 0, 0:G * HD].rearrange("p (g d) -> p g d", d=HD), ACT.Square)\
                .then_inc(sq_done, 1)
            act.wait_ge(norm, 2)
            nc.scalar.activation(root[:], ms[:], ACT.Sqrt).then_inc(norm, 1)
            act.wait_ge(g_in, 16)
            nc.scalar.activation(gates[:], g_raw[:], ACT.Sigmoid)

        @block.vector
        def _(dve):
            dve.wait_ge(peT_ready, 1)
            nc.vector.tensor_copy(peT[:], ps_t[0:HD, 0, 0:2 * CMP_LEN]).then_inc(peT_done, 1)
            dve.wait_ge(sq_done, 1)
            nc.vector.tensor_reduce(ss[:], sq[:], AX.X, ALU.add).then_inc(norm, 1)
            dve.wait_ge(norm, 1)
            nc.vector.tensor_scalar(ms[:], ss[:], 1.0 / HD, EPS, ALU.mult, ALU.add).then_inc(norm, 1)
            dve.wait_ge(norm, 3)
            nc.vector.reciprocal(rstd[:], root[:]).then_inc(norm, 1)
            dve.wait_ge(norm, 4)
            dve.wait_ge(ktok_set, 4)
            nc.vector.tensor_tensor(ktok[0:NW, :, 0:HD], ps_c[0:NW, 0, 0:G * HD].rearrange("p (g d) -> p g d", d=HD),
                                    bcast(rstd[:].rearrange("p (g o) -> p g o", o=1), HD), ALU.mult).then_inc(ktok_done, 1)
            dve.wait_ge(c_ready, 2)
            nc.vector.tensor_copy(vc[0:NW, :, :], ps_c[0:NW, 1, 0:G * HD].rearrange("p (g d) -> p g d", d=HD))
            dve.wait_ge(tr_ready, 1)
            dve.wait_ge(gain_in, 16)
            nc.vector.tensor_scalar(kcT[:], ps_t[0:HA, 0, 0:G * CMP_PAD].rearrange("p (g n) -> p g n", n=CMP_PAD),
                                    gain[:, 0:1], None, ALU.mult)


def select_stage(nc, qT, kcT, vc, gates, sel, mixed, ident):
    J = GROUP
    N = 2 * TT
    ROUNDS = KV_HEADS // 2
    FIRST = TOPN * SLC // P
    PICKED = 3e38
    FORCED = 1e30
    with Stage(nc, "sel") as st:
        q = st.sb("q", [HA, 2, J, SEQ])
        cmask = st.sb("cmask", [P, TT, CMP_PAD])
        force = st.sb("force", [P, TT, N_SLC])
        alive = st.sb("alive", [P, TT])
        s = st.sb("s", [P, 2, J, CMP_PAD])
        e = st.sb("e", [P, 2, J, CMP_PAD])
        pn = st.sb("pn", [P, 2, J, CMP_PAD])
        pt = st.sb("pt", [CMP_PAD, 2, J, P])
        nm = st.sb("nm", [P, 2, J])
        rowsum = st.sb("rowsum", [P, 2, J])
        rl = st.sb("rl", [P, 2, J])
        rla = st.sb("rla", [P, 2, J])
        both = st.sb("both", [P, 1 + CMP_PAD])
        quad = st.sb("quad", [P, N_SLC])
        imp = st.sb("imp", [P, N_SLC])
        score = st.sb("score", [P, N_SLC])
        top = st.sb("top", [P, 8])
        marked = st.sb("marked", [P, N_SLC])
        ps_s = st.ps("ps_s", [P, 2, BANK])
        ps_t = st.ps("ps_t", [CMP_PAD, 2, BANK])
        ps_o = st.ps("ps_o", [P, 2, BANK])
        in_sem = [st.sem(f"in{x}") for x in range(2)]
        setup, s_done, neg_done, e_done, pn_done, t_done, pt_done, o_done, o_taken, link, sel_link = (
            st.sem(x) for x in ("setup", "s_done", "neg_done", "e_done", "pn_done", "t_done", "pt_done", "o_done",
                                "o_taken", "link", "sel_link"))
        masked, force_set = st.sem("masked"), st.sem("force_set")
        picks = [n for n in range(N) if n % TT >= FIRST]
        qv = qT.rearrange("(i s j) r t -> i s r j t", s=2, j=J)
        block = st.block()

        @block.sync
        def _(sp):
            def load(it, x):
                for j in range(J):
                    sp.dma_start(q[:, x, j, :], qv[bass.ds(it, 1), x, :, j, :].rearrange("o r t -> (o r) t")).then_inc(in_sem[x], 16)

            for x in range(2):
                load(0, x)
            with sp.Fori(1, ROUNDS) as it:
                for x in range(2):
                    sp.wait_ge(s_done, it * N + (x + 1) * TT - N)
                    load(it, x)

        @block.gpsimd
        def _(pool):
            nc.gpsimd.memset(cmask[:], 0.0).then_inc(setup, 1)
            nc.gpsimd.memset(alive[:], 1.0).then_inc(setup, 1)
            nc.gpsimd.memset(both[:], 0.0).then_inc(setup, 1)
            nc.gpsimd.memset(sel[:], 0.0).then_inc(setup, 1)
            pool.wait_ge(setup, 4)
            nc.gpsimd.affine_select(out=cmask[:], in_=cmask[:], compare_op=ALU.is_ge, fill=NEG, base=-(CMP_LEN - 1),
                                    pattern=[[P, TT], [-CMP_STRIDE, CMP_PAD]], channel_multiplier=1).then_inc(setup, 1)
            nc.gpsimd.affine_select(out=alive[:], in_=alive[:], compare_op=ALU.is_ge, fill=0.0, base=-(CMP_LEN - 1),
                                    pattern=[[P, TT]], channel_multiplier=1).then_inc(setup, 1)

        @block.tensor
        def _(pe):
            with pe.Fori(0, ROUNDS) as it:
                def scores(n):
                    x, i = divmod(n, TT)
                    if i == 0:
                        pe.wait_ge(in_sem[x], (it + 1) * (16 * J))
                    if n >= 2:
                        pe.wait_ge(masked, it * N + n - 1)
                    for j in range(J):
                        ins = nc.tensor.matmul(ps_s[:, n % 2, j * CMP_PAD:(j + 1) * CMP_PAD], q[:, x, j, i * P:(i + 1) * P],
                                               kview(it, x), start=True, stop=True)
                    ins.then_inc(s_done, 1)

                def transposes(n):
                    pe.wait_ge(pn_done, it * N + n + 1)
                    if n >= 2:
                        pe.wait_ge(pt_done, it * N + n - 1)
                    pe.nop(nofuse=True)
                    for j in range(J):
                        ins = nc.tensor.transpose(ps_t[:, n % 2, j * P:(j + 1) * P], pn[:, n % 2, j, :], ident[:])
                    ins.then_inc(t_done, 1)

                def values(n):
                    x, i = divmod(n, TT)
                    pe.wait_ge(pt_done, it * N + n + 1)
                    if n >= 2:
                        pe.wait_ge(o_taken, it * N + n - 1)
                    pe.nop(nofuse=True)
                    for j in range(J):
                        ins = nc.tensor.matmul(ps_o[:, n % 2, j * HD:(j + 1) * HD], pt[:, n % 2, j, :], vview(it, x),
                                               start=True, stop=True)
                    ins.then_inc(o_done, 1)

                def kview(it, x):
                    return kcT[:, :, :].rearrange("p (i s) n -> p i s n", s=2)[:, bass.ds(it, 1), x, :].rearrange("p o n -> p (o n)")

                def vview(it, x):
                    return vc[:, :, :].rearrange("p (i s) n -> p i s n", s=2)[:, bass.ds(it, 1), x, :].rearrange("p o n -> p (o n)")

                scores(0)
                scores(1)
                for n in range(N):
                    transposes(n)
                    if n:
                        values(n - 1)
                    if n + 2 < N:
                        scores(n + 2)
                values(N - 1)

        @block.scalar
        def _(act):
            with act.Fori(0, ROUNDS) as it:
                for n in range(N + 1):
                    if n < N:
                        act.wait_ge(neg_done, it * N + n + 1)
                        for j in range(J):
                            ins = nc.scalar.activation(e[:, n % 2, j, :], s[:, n % 2, j, :], ACT.Exp,
                                                       bias=nm[:, n % 2, j:j + 1], accum_out=rowsum[:, n % 2, j:j + 1])
                        ins.then_inc(e_done, 1)
                    if n:
                        m = n - 1
                        act.wait_ge(t_done, it * N + m + 1)
                        if m >= 2:
                            act.wait_ge(o_done, it * N + m - 1)
                        nc.scalar.activation(pt[:, m % 2, :, :], ps_t[:, m % 2, :].rearrange("p (j c) -> p j c", c=P), ACT.Copy)\
                            .then_inc(pt_done, 1)

        @block.vector
        def _(dve):
            nc.vector.memset(force[:], 0.0).then_inc(force_set, 1)
            dve.wait_ge(force_set, 1)
            for i in range(FIRST, TT):
                for half in range(2):
                    cur = 2 * i + half
                    rows = slice(half * SLC, (half + 1) * SLC)
                    nc.vector.memset(force[rows, i, 0:1], FORCED)
                    ins = nc.vector.memset(force[rows, i, cur - 1:cur + 1], FORCED)
                    if cur + 1 < N_SLC:
                        ins = nc.vector.memset(force[rows, i, cur + 1:N_SLC], NEG)
            ins.then_inc(force_set, 1)
            dve.wait_ge(force_set, 2)
            dve.wait_ge(setup, 6)
            with dve.Fori(0, ROUNDS) as it:
                def negate(n):
                    i = n % TT
                    dve.wait_ge(s_done, it * N + n + 1)
                    nc.vector.tensor_tensor(s[:, n % 2, :, :], ps_s[:, n % 2, 0:J * CMP_PAD].rearrange("p (j c) -> p j c", c=CMP_PAD),
                                            cmask[:, i:i + 1, :].to_broadcast([P, J, CMP_PAD]), ALU.add).then_inc(masked, 1)
                    dve.wait_ge(masked, it * N + n + 1)
                    nc.vector.tensor_reduce(nm[:, n % 2, :], s[:, n % 2, :, :], AX.X, ALU.max, negate=True).then_inc(neg_done, 1)

                def normalize(n):
                    i = n % TT
                    dve.wait_ge(e_done, it * N + n + 1)
                    nc.vector.reciprocal(rl[:, n % 2, :], rowsum[:, n % 2, :]).then_inc(link, 1)
                    dve.wait_ge(link, it * (2 * N) + 2 * n + 1)
                    nc.vector.tensor_scalar(rla[:, n % 2, :], rl[:, n % 2, :], alive[:, i:i + 1], None, ALU.mult).then_inc(link, 1)
                    dve.wait_ge(link, it * (2 * N) + 2 * n + 2)
                    if n >= 2:
                        dve.wait_ge(t_done, it * N + n - 1)
                    nc.vector.tensor_tensor(pn[:, n % 2, :, :], e[:, n % 2, :, :],
                                            bcast(rla[:, n % 2, :].rearrange("p (j o) -> p j o", o=1), CMP_PAD),
                                            ALU.mult).then_inc(pn_done, 1)

                def pick(n):
                    i = n % TT
                    m = picks.index(n)
                    at = it * (7 * len(picks)) + 7 * m
                    dve.wait_ge(pn_done, it * N + n + 1)
                    nc.vector.tensor_reduce(both[:, 1:], pn[:, n % 2, :, :].rearrange("p j n -> p n j"), AX.X, ALU.add).then_inc(sel_link, 1)
                    dve.wait_ge(sel_link, at + 1)
                    nc.vector.tensor_reduce(quad[:], both[:, 1:].rearrange("p (m w) -> p m w", w=SLC // CMP_STRIDE), AX.X, ALU.add)\
                        .then_inc(sel_link, 1)
                    dve.wait_ge(sel_link, at + 2)
                    nc.vector.tensor_tensor(imp[:], quad[:], both[:, 0:CMP_PAD:SLC // CMP_STRIDE], ALU.add).then_inc(sel_link, 1)
                    dve.wait_ge(sel_link, at + 3)
                    nc.vector.tensor_tensor(score[:], imp[:], force[:, i, :], ALU.add).then_inc(sel_link, 1)
                    dve.wait_ge(sel_link, at + 4)
                    nc.vector.nop(nofuse=True)
                    nc.vector.max(top[:], score[:]).then_inc(sel_link, 1)
                    dve.wait_ge(sel_link, at + 5)
                    nc.vector.nop(nofuse=True)
                    nc.vector.match_replace(marked[:], top[:], score[:], PICKED).then_inc(sel_link, 1)
                    dve.wait_ge(sel_link, at + 6)
                    nc.vector.tensor_scalar(sel[:, :, i, :].rearrange("p (i s) n -> p i s n", s=2)[:, bass.ds(it, 1), n // TT, :]
                                            .rearrange("p o n -> p (o n)"), marked[:], PICKED, NEG, ALU.not_equal, ALU.mult)\
                        .then_inc(sel_link, 1)

                def output(n):
                    x, i = divmod(n, TT)
                    dve.wait_ge(o_done, it * N + n + 1)
                    dst = mixed[:, i, :].rearrange("p (i s j d) -> p i s j d", s=2, j=J, d=HD)[:, bass.ds(it, 1), x, :, :]
                    g = gates[:, i, 0:C_HEADS].rearrange("p (i s j) -> p i s j", s=2, j=J)[:, bass.ds(it, 1), x, :]
                    nc.vector.tensor_tensor(dst.rearrange("p o j d -> p (o j) d"),
                                            ps_o[:, n % 2, 0:J * HD].rearrange("p (j d) -> p j d", d=HD),
                                            bcast(g.rearrange("p o (j x) -> p (o j) x", x=1), HD), ALU.mult).then_inc(o_taken, 1)

                negate(0)
                negate(1)
                for n in range(N):
                    normalize(n)
                    if n in picks:
                        pick(n)
                    if n:
                        output(n - 1)
                    if n + 2 < N:
                        negate(n + 2)
                output(N - 1)


def dilated_bias_stage(nc, bias):
    reach = ((128, 1), (512, 4), (2048, 16))
    with Stage(nc, "dil") as st:
        d = st.sb("d", [P, SEQ], I32)
        r = st.sb("r", [P, SEQ], I32)
        df = st.sb("df", [P, SEQ])
        a = st.sb("a", [P, SEQ])
        b = st.sb("b", [P, SEQ])
        c = st.sb("c", [P, SEQ])
        step, iota_done = st.sem("step"), st.sem("iota_done")
        block = st.block()

        @block.gpsimd
        def _(pool):
            nc.gpsimd.iota(d[:], pattern=[[-1, SEQ]], base=SEQ - P, channel_multiplier=1).then_inc(iota_done, 1)
            pool.wait_ge(step, 15)
            nc.gpsimd.affine_select(out=bias[:], in_=a[:], compare_op=ALU.is_ge, fill=NEG, base=SEQ - P,
                                    pattern=[[-1, SEQ]], channel_multiplier=1)

        @block.vector
        def _(dve):
            dve.wait_ge(iota_done, 1)
            nc.vector.tensor_copy(df[:], d[:]).then_inc(step, 1)
            dve.wait_ge(step, 1)
            nc.vector.tensor_scalar(c[:], df[:], float(reach[0][0]), None, ALU.is_le).then_inc(step, 1)
            for n, (window, dilation) in enumerate(reach[1:]):
                at = 2 + 4 * n
                nc.vector.tensor_scalar(r[:], d[:], dilation - 1, None, ALU.bitwise_and).then_inc(step, 1)
                dve.wait_ge(step, at + 1)
                nc.vector.tensor_scalar(a[:], r[:], 0.0, None, ALU.is_equal).then_inc(step, 1)
                dve.wait_ge(step, at + 2)
                nc.vector.scalar_tensor_tensor(b[:], df[:], float(window), a[:], ALU.is_le, ALU.mult).then_inc(step, 1)
                dve.wait_ge(step, at + 3)
                nc.vector.tensor_tensor(c[:], c[:], b[:], ALU.add).then_inc(step, 1)
                dve.wait_ge(step, at + 4)
            nc.vector.tensor_scalar(a[:], c[:], 0.0, NEG, ALU.is_equal, ALU.mult).then_inc(step, 1)
            for n, count in enumerate((2, 3)):
                at = 11 + 2 * n
                nc.vector.tensor_scalar(b[:], c[:], float(count), math.log(count), ALU.is_equal, ALU.mult).then_inc(step, 1)
                dve.wait_ge(step, at + 1)
                nc.vector.tensor_tensor(a[:], a[:], b[:], ALU.add).then_inc(step, 1)
                dve.wait_ge(step, at + 2)


def distance_bias_stage(nc, causal, window):
    with Stage(nc, "dist") as st:
        step = st.sem("step")
        block = st.block()

        @block.gpsimd
        def _(pool):
            nc.gpsimd.memset(causal[:], 0.0).then_inc(step, 1)
            pool.wait_ge(step, 1)
            nc.gpsimd.affine_select(out=causal[:], in_=causal[:], compare_op=ALU.is_ge, fill=NEG, base=SEQ - P,
                                    pattern=[[-1, SEQ]], channel_multiplier=1).then_inc(step, 1)
            pool.wait_ge(step, 2)
            nc.gpsimd.affine_select(out=window[:], in_=causal[:], compare_op=ALU.is_ge, fill=NEG, base=WIN - 1 - (SEQ - P),
                                    pattern=[[1, SEQ]], channel_multiplier=-1)


def store_stage(nc, x_sb, out):
    with Stage(nc, "store") as st:
        x_out = st.sem("x_out")
        block = st.block()

        @block.sync
        def _(sp):
            sp.dma_start(out.rearrange("o (t p) d -> p (o t) d", p=P), x_sb[:]).then_inc(x_out, 16)
            sp.wait_ge(x_out, 16)


def trunk(nc, x, attn_norm, ffn_norm, hy_w_in, hy_lb_logits, hy_o_gain, hy_q_gain, hy_k_gain, hy_w_out, nsa_w_in,
          nsa_q_gain, nsa_k_gain, nsa_cmp_pe, nsa_cmp_w1, nsa_cmp_w2, nsa_w_out, ffn_w_gate, ffn_w_up, ffn_w_down, out):
    def slopes(n, first, count):
        return [2.0 ** (-8.0 * (h + 1) / n) for h in range(first, first + count)]

    def dram(name, shape):
        return nc.dram_tensor(name, shape, F32).ap()

    proj0 = dram("proj0", (SEQ, EVEN_IN))
    q0T, k0T = dram("q0T", (B_HEADS, HA, SEQ)), dram("k0T", (B_HEADS, HA, SEQ))
    proj1 = dram("proj1", (SEQ, ODD_IN))
    q1T = dram("q1T", (C_HEADS, HA, SEQ))
    kvT = dram("kvT", (4 * KV_HEADS, HA, SEQ))
    Q = 4 * HD

    with ExitStack() as whole:
        def sb(ctx, name, shape):
            return ctx.enter_context(nc.sbuf_tensor(name, shape, F32))

        def parts(ctx, name, shape):
            return [ctx.enter_context(nc.sbuf_tensor(f"{name}_{part}", shape, F32R)) for part in ("hi", "lo")]

        x_sb = sb(whole, "x_sb", [P, TT, DM])
        ident = sb(whole, "ident", [P, P])
        load_stage(nc, x, x_sb, ident)

        def ffn(layer):
            with ExitStack() as c:
                hT = parts(c, f"ffn_hT{layer}", [P, KD, SEQ])
                transpose_stage(nc, f"fn{layer}", x_sb, hT, [(ffn_norm[layer, :], 0, DM)], ident, True)
                for n, (f0, groups) in enumerate(((0, (2, 2, 2, 2)), (8, (2, 2, 2, 2)), (16, (3, 3)))):
                    lo, hi = f0 * P, (f0 + sum(groups)) * P
                    with ExitStack() as c2:
                        actT = parts(c2, f"actT{layer}_{n}", [P, sum(groups), SEQ])
                        ffn_stage(nc, f"up{layer}_{n}", hT, ffn_w_gate[layer, :, lo:hi], ffn_w_up[layer, :, lo:hi], actT)
                        linear_stage(nc, f"down{layer}_{n}", actT, ffn_w_down[layer, lo:hi, :], groups, BANK, add_to=x_sb)

        with ExitStack() as c:
            hT = parts(c, "hT0", [P, KD, SEQ])
            transpose_stage(nc, "an0", x_sb, hT, [(attn_norm[0, :], 0, DM)], ident, True)
            linear_stage(nc, "in0", hT, hy_w_in[0, :, :], (4, 4), BANK, dst_dram=proj0)
        with ExitStack() as c:
            mixed = sb(c, "mixed0", [P, TT, DM])
            hgrn_stage(nc, proj0, hy_lb_logits, mixed, ident)
            with ExitStack() as c2:
                bias = sb(c2, "bias0", [P, SEQ])
                dilated_bias_stage(nc, bias)
                at = 4 * A_WIDTH
                heads_stage(nc, "q0", proj0, q0T, [(at + Q * n, 4 * n, hy_q_gain[0, :], HD ** -0.5, slopes(B_HEADS, 4 * n, 4))
                                                   for n in range(2)], ident)
                at += B_HEADS * HD
                heads_stage(nc, "k0", proj0, k0T, [(at + Q * n, 4 * n, hy_k_gain[0, :], 1.0, None) for n in range(2)], ident)
                at += B_HEADS * HD
                attention_stage(nc, "at0", B_HEADS, q0T, [(k0T, proj0[:, at:at + B_HEADS * HD], 1, bias, TT, 0, False)],
                                mixed, A_WIDTH, ident)
            mT = parts(c, "mT0", [P, KD, SEQ])
            transpose_stage(nc, "mt0", mixed, mT, [(hy_o_gain[0, :], 0, A_WIDTH)], ident, False)
            linear_stage(nc, "out0", mT, hy_w_out[0, :, :], (4, 4), BANK, add_to=x_sb)
        ffn(0)

        with ExitStack() as c:
            hT = parts(c, "hT1", [P, KD, SEQ])
            transpose_stage(nc, "an1", x_sb, hT, [(attn_norm[1, :], 0, DM)], ident, True)
            linear_stage(nc, "in1", hT, nsa_w_in[0, :, :], (4, 4), ODD_IN // 8, dst_dram=proj1)
        main = DM + 6 * KV_W
        with ExitStack() as c:
            mixed = sb(c, "mixed1", [P, TT, DM])
            with ExitStack() as c2:
                gates = sb(c2, "gates", [P, TT, 3 * C_HEADS])
                kcT = sb(c2, "kcT", [HA, KV_HEADS, CMP_PAD])
                vc = sb(c2, "vc", [CMP_PAD, KV_HEADS, HD])
                sel = sb(c2, "sel", [P, KV_HEADS, TT, N_SLC])
                causal, window = sb(c2, "causal", [P, SEQ]), sb(c2, "window", [P, SEQ])
                distance_bias_stage(nc, causal, window)
                heads_stage(nc, "q1", proj1, q1T, [(Q * n, 4 * n, nsa_q_gain[0, :], HD ** -0.5, slopes(C_HEADS, 4 * n, 4))
                                                   for n in range(4)], ident)
                heads_stage(nc, "k1", proj1, kvT,
                            [(DM, 0, None, 1.0, None), (DM + KV_W, 4, None, 1.0, None),
                             (DM + 2 * KV_W, 8, nsa_k_gain[0, 1, :], 1.0, None),
                             (DM + 4 * KV_W, 12, nsa_k_gain[0, 2, :], 1.0, None)], ident)
                compress_stage(nc, kvT, nsa_cmp_pe[0, :, :, :], nsa_cmp_w1[0, :, :, :], nsa_cmp_w2[0, :, :, :],
                               nsa_k_gain[0, 0, :], proj1[:, main:ODD_IN], kcT, vc, gates, ident)
                select_stage(nc, q1T, kcT, vc, gates, sel, mixed, ident)
                vs, vw = DM + 3 * KV_W, DM + 5 * KV_W
                attention_stage(nc, "at1", C_HEADS, q1T,
                                [(kvT[8:12, :, :], proj1[:, vs:vs + KV_W], GROUP, causal, TT, C_HEADS, True),
                                 (kvT[12:16, :, :], proj1[:, vw:vw + KV_W], GROUP, window, WIN // P + 1, 2 * C_HEADS, False)],
                                mixed, 0, ident, gates=gates, sel=sel)
            mT = parts(c, "mT1", [P, KD, SEQ])
            transpose_stage(nc, "mt1", mixed, mT, [], ident, False)
            linear_stage(nc, "out1", mT, nsa_w_out[0, :, :], (4, 4), BANK, add_to=x_sb)
        ffn(1)
        store_stage(nc, x_sb, out)


_INS = ["x", "attn_norm", "ffn_norm", "hy_w_in", "hy_lb_logits", "hy_o_gain", "hy_q_gain", "hy_k_gain", "hy_w_out",
        "nsa_w_in", "nsa_q_gain", "nsa_k_gain", "nsa_cmp_pe", "nsa_cmp_w1", "nsa_cmp_w2", "nsa_w_out",
        "ffn_w_gate", "ffn_w_up", "ffn_w_down"]


def kernel(**inputs):
    import concourse.bacc as _bacc
    from concourse.bass_utils import run_bass_kernel_spmd as _run

    nc = _bacc.Bacc("TRN2", target_bir_lowering=False, num_devices=1)
    arrays, args = {}, []
    for name in _INS:
        a = np.ascontiguousarray(inputs[name])
        arrays[f"in_{name}"] = a
        args.append(nc.dram_tensor(f"in_{name}", a.shape, mybir.dt.from_np(a.dtype), kind="ExternalInput").ap())
    args.append(nc.dram_tensor("out_x", (1, SEQ, DM), F32, kind="ExternalOutput").ap())
    trunk(nc, *args)
    return _run(nc, [arrays], core_ids=[0]).results[0]["out_x"]
```

```python
import math
from contextlib import ExitStack

import concourse.bass as bass
import numpy as np
from concourse import mybir

F32 = mybir.dt.float32
F32R = mybir.dt.float32r
I32 = mybir.dt.int32
ALU = mybir.AluOpType
ACT = mybir.ActivationFunctionType
AX = mybir.AxisListType

P = 128
SEQ = 1024
DM = 1024
TT = SEQ // P
KD = DM // P
HD = 64
HA = HD + 2
EPS = 1e-6
NEG = -1e30
BANK = 512

A_WIDTH = DM // 2
A_HEADS = 4
B_HEADS = 8
EVEN_IN = 4 * A_WIDTH + 3 * (DM - A_WIDTH)

C_HEADS = 16
KV_HEADS = 4
GROUP = C_HEADS // KV_HEADS
KV_W = KV_HEADS * HD
ODD_IN = DM + 6 * KV_W + 3 * C_HEADS
CMP_LEN, CMP_STRIDE, CMP_HIDDEN = 32, 16, 2 * HD
N_CMP = (SEQ - CMP_LEN) // CMP_STRIDE + 1
CMP_PAD = 64
SLC = 64
N_SLC = SEQ // SLC
TOPN = 8
WIN = 512
D_FF = -(-8 * DM // (3 * 256)) * 256


class Stage:

    def __init__(self, nc, name):
        self.nc, self.name, self.ctx, self.sems = nc, name, ExitStack(), []

    def __enter__(self):
        self.ctx.__enter__()
        return self

    def __exit__(self, *e):
        done = self.ctx.__exit__(*e)
        if e[0] is None:
            self.nc.clear_and_free_semaphores(self.sems)
            self.nc.all_engine_barrier()
        return done

    def sb(self, name, shape, dt=F32):
        return self.ctx.enter_context(self.nc.sbuf_tensor(f"{self.name}_{name}", shape, dt))

    def ps(self, name, shape, dt=F32):
        return self.ctx.enter_context(self.nc.psum_tensor(f"{self.name}_{name}", shape, dt))

    def sem(self, name):
        self.sems.append(self.nc.alloc_semaphore(f"{self.name}_{name}"))
        return self.sems[-1]

    def block(self):
        return self.ctx.enter_context(self.nc.Block())


def bcast(ap, n):
    return ap.to_broadcast(list(ap.shape[:-1]) + [n])



def load_stage(nc, x, x_sb, ident):
    with Stage(nc, "load") as st:
        x_in, zeroed = st.sem("x_in"), st.sem("zeroed")
        block = st.block()

        @block.sync
        def _(sp):
            sp.dma_start(x_sb[:], x.rearrange("o (t p) d -> p (o t) d", p=P)).then_inc(x_in, 16)
            sp.wait_ge(x_in, 16)

        @block.gpsimd
        def _(pool):
            nc.gpsimd.memset(ident[:], 0.0).then_inc(zeroed, 1)
            pool.wait_ge(zeroed, 1)
            nc.gpsimd.affine_select(out=ident[:], in_=ident[:], compare_op=ALU.not_equal, fill=1.0, base=0,
                                    pattern=[[-1, P]], channel_multiplier=1)


def transpose_stage(nc, name, src, dst, gains, ident, norm):
    dst_hi, dst_lo = dst
    scaled = norm or gains
    with Stage(nc, name) as st:
        gain = st.sb("gain", [P, DM]) if gains else None
        sq = st.sb("sq", [P, 2, DM]) if norm else None
        h = st.sb("h", [P, 2, DM]) if scaled else None
        ss = st.sb("ss", [P, TT])
        ms = st.sb("ms", [P, TT])
        root = st.sb("root", [P, TT])
        rstd = st.sb("rstd", [P, TT])
        tr = st.ps("tr", [P, 4, BANK])
        gain_in, gain_set = st.sem("gain_in"), st.sem("gain_set")
        ss_done, ms_done, root_done, rstd_done = (st.sem(n) for n in ("ss_done", "ms_done", "root_done", "rstd_done"))
        h_done, tr_done, hi_done, lo_done = (st.sem(n) for n in ("h_done", "tr_done", "hi_done", "lo_done"))
        block = st.block()

        @block.sync
        def _(sp):
            if gains:
                sp.wait_ge(gain_set, 1)
                for g, lo, hi in gains:
                    row = g.rearrange("(o d) -> o d", o=1)
                    sp.dma_start(gain[:, lo:hi], row.to_broadcast([P, hi - lo])).then_inc(gain_in, 16)

        @block.gpsimd
        def _(pool):
            if gains:
                nc.gpsimd.memset(gain[:], 1.0).then_inc(gain_set, 1)

        @block.scalar
        def _(act):
            if norm:
                for t in range(TT):
                    if t >= 2:
                        act.wait_ge(ss_done, t - 1)
                    nc.scalar.activation(sq[:, t % 2, :], src[:, t, :], ACT.Square,
                                         accum_out=ss[:, t:t + 1]).then_inc(ss_done, 1)
                act.wait_ge(ms_done, 1)
                nc.scalar.activation(root[:], ms[:], ACT.Sqrt).then_inc(root_done, 1)
            for m in range(2 * TT):
                t, k0 = m // 2, (m % 2) * 4
                act.wait_ge(tr_done, m + 1)
                nc.scalar.activation(dst_hi[:, k0:k0 + 4, t * P:(t + 1) * P],
                                     tr[:, m % 4, :].rearrange("p (k c) -> p k c", c=P), ACT.Copy).then_inc(hi_done, 1)

        @block.vector
        def _(dve):
            if norm:
                dve.wait_ge(ss_done, TT)
                nc.vector.tensor_scalar(ms[:], ss[:], 1.0 / DM, EPS, ALU.mult, ALU.add).then_inc(ms_done, 1)
                dve.wait_ge(root_done, 1)
                nc.vector.reciprocal(rstd[:], root[:]).then_inc(rstd_done, 1)
                dve.wait_ge(rstd_done, 1)
            if gains:
                dve.wait_ge(gain_in, 16 * len(gains))
            for t in range(TT + 1):
                if t < TT and scaled:
                    if t >= 2:
                        dve.wait_ge(tr_done, 2 * (t - 1))
                    if norm:
                        nc.vector.scalar_tensor_tensor(h[:, t % 2, :], src[:, t, :], rstd[:, t:t + 1], gain[:], ALU.mult,
                                                       ALU.mult).then_inc(h_done, 1)
                    else:
                        nc.vector.tensor_tensor(h[:, t % 2, :], src[:, t, :], gain[:], ALU.mult).then_inc(h_done, 1)
                for half in range(2 if t else 0):
                    m = 2 * (t - 1) + half
                    k0 = half * 4
                    dve.wait_ge(hi_done, m + 1)
                    nc.vector.tensor_tensor(dst_lo[:, k0:k0 + 4, (t - 1) * P:t * P],
                                            tr[:, m % 4, :].rearrange("p (k c) -> p k c", c=P),
                                            dst_hi[:, k0:k0 + 4, (t - 1) * P:t * P].bitcast(F32), ALU.subtract).then_inc(lo_done, 1)

        @block.tensor
        def _(pe):
            for t in range(TT):
                if scaled:
                    pe.wait_ge(h_done, t + 1)
                for half in range(2):
                    m = 2 * t + half
                    if m >= 4:
                        pe.wait_ge(lo_done, m - 3)
                    for k in range(4):
                        kk = half * 4 + k
                        rows = h[:, t % 2, :] if scaled else src[:, t, :]
                        ins = nc.tensor.transpose(tr[:, m % 4, k * P:(k + 1) * P], rows[:, kk * P:(kk + 1) * P],
                                                  ident[:])
                    ins.then_inc(tr_done, 1)




def linear_stage(nc, name, lhsT, w, groups, width, dst_dram=None, add_to=None):
    kt, NG, G = sum(groups), len(groups), max(groups)
    cols = w.shape[1]
    n_chunks = cols // width
    start = [sum(groups[:g]) for g in range(NG)]
    to_dram = dst_dram is not None
    with Stage(nc, name) as st:
        raw = st.sb("raw", [P, 2, G, width])
        w_hi = st.sb("w_hi", [P, 2, G, width], F32R)
        w_lo = st.sb("w_lo", [P, 2, G, width], F32R)
        out = st.sb("out", [P, TT, width]) if to_dram else None
        acc = st.ps("acc", [P, TT, BANK])
        w_in = [st.sem(f"w_in{s}") for s in range(2)]
        hi_done, lo_done, used, acc_done, acc_free, y_out = (
            st.sem(n) for n in ("hi_done", "lo_done", "used", "acc_done", "acc_free", "y_out"))
        wc = w.rearrange("(k p) (c n) -> p k c n", p=P, n=width)
        if to_dram:
            dc = dst_dram.rearrange("(t p) (c n) -> p t c n", p=P, n=width)
        else:
            xc = add_to[:, :, :].rearrange("p t (c n) -> p t c n", n=width)
        block = st.block()

        def all_chunks(eng, step):
            step(0, True, n_chunks == 1)
            if n_chunks > 2:
                with eng.Fori(1, n_chunks - 1) as c:
                    step(c, False, False)
            if n_chunks > 1:
                step(n_chunks - 1, False, True)

        def order(c, last):
            return [(c, g) for g in range(1, NG)] + ([] if last else [(c + 1, 0)])

        @block.sync
        def _(sp):
            def load(c, g, ahead=0):
                k0 = start[g]
                chunk = wc[:, k0:k0 + groups[g], ahead:, :][:, :, bass.ds(c, 1), :]
                sp.dma_start(raw[:, g % 2, 0:groups[g], :], chunk.rearrange("p k o n -> p k (o n)"))\
                    .then_inc(w_in[g % 2], 16)

            load(0, 0)
            load(0, 1)

            def chunk(c, first, last):
                for g in range(NG):
                    n = g + 2
                    if n >= NG and last:
                        break
                    sp.wait_ge(hi_done, c * NG + g + 1)
                    sp.wait_ge(lo_done, c * NG + g + 1)
                    load(c, n % NG, n // NG)

            all_chunks(sp, chunk)

        @block.scalar
        def _(act):
            def split(c, g, first):
                act.wait_ge(w_in[g % 2], c * (16 * (NG // 2)) + 16 * (g // 2 + 1))
                if g >= 2:
                    act.wait_ge(used, c * (NG - 1) + g - 1)
                elif not first and g == 1:
                    act.wait_ge(acc_done, c * TT)
                elif not first:
                    act.wait_ge(used, c * (NG - 1))
                nc.scalar.activation(w_hi[:, g % 2, 0:groups[g], :], raw[:, g % 2, 0:groups[g], :], ACT.Copy)\
                    .then_inc(hi_done, 1)

            def chunk(c, first, last):
                for cc, g in order(c, last):
                    split(cc, g, first and g > 0)
                if to_dram:
                    if not first:
                        act.wait_ge(y_out, c * 16)
                    for t in range(TT):
                        act.wait_ge(acc_done, c * TT + t + 1)
                        nc.scalar.activation(out[:, t, :], acc[:, t, 0:width], ACT.Copy).then_inc(acc_free, 1)

            split(0, 0, True)
            all_chunks(act, chunk)

        @block.vector
        def _(dve):
            def split(c, g):
                dve.wait_ge(hi_done, c * NG + g + 1)
                nc.vector.tensor_tensor(w_lo[:, g % 2, 0:groups[g], :], raw[:, g % 2, 0:groups[g], :],
                                        w_hi[:, g % 2, 0:groups[g], :].bitcast(F32), ALU.subtract).then_inc(lo_done, 1)

            def chunk(c, first, last):
                for cc, g in order(c, last):
                    split(cc, g)
                if not to_dram:
                    for t in range(TT):
                        dve.wait_ge(acc_done, c * TT + t + 1)
                        xs = xc[:, t, bass.ds(c, 1), :].rearrange("p o n -> p (o n)")
                        nc.vector.tensor_tensor(xs, acc[:, t, 0:width], xs, ALU.add).then_inc(acc_free, 1)

            split(0, 0)
            all_chunks(dve, chunk)

        @block.tensor
        def _(pe):
            def chunk(c, first, last):
                for g in range(NG):
                    pe.wait_ge(lo_done, c * NG + g + 1)
                    for k in range(start[g], start[g] + groups[g]):
                        for t in range(TT):
                            if k == 0 and not first:
                                pe.wait_ge(acc_free, c * TT + t + 1 - TT)
                            x_hi, x_lo = (x[:, k, t * P:(t + 1) * P] for x in lhsT)
                            r_hi, r_lo = (x[:, g % 2, k - start[g], :] for x in (w_hi, w_lo))
                            nc.tensor.matmul(acc[:, t, 0:width], x_hi, r_hi, start=k == 0, stop=False)
                            nc.tensor.matmul(acc[:, t, 0:width], x_hi, r_lo, start=False, stop=False)
                            ins = nc.tensor.matmul(acc[:, t, 0:width], x_lo, r_hi, start=False, stop=k == kt - 1)
                            if k == kt - 1:
                                ins.then_inc(acc_done, 1)
                    if g < NG - 1:
                        ins.then_inc(used, 1)

            all_chunks(pe, chunk)

        @block.gpsimd
        def _(pool):
            def store(c, first, last):
                pool.wait_ge(acc_free, (c + 1) * TT)
                pool.dma_start(dc[:, :, bass.ds(c, 1), :].rearrange("p t o n -> p t (o n)"), out[:]).then_inc(y_out, 16)

            if to_dram:
                all_chunks(pool, store)
                pool.wait_ge(y_out, 16 * n_chunks)


def ffn_stage(nc, name, hT, w_gate, w_up, actT):
    NF = w_gate.shape[1] // P
    HALF = SEQ // 2
    with Stage(nc, name) as st:
        raw = st.sb("raw", [P, 2, KD, P])
        w_hi = st.sb("w_hi", [P, 2, KD, P], F32R)
        w_lo = st.sb("w_lo", [P, 2, KD, P], F32R)
        sg = st.sb("sg", [P, 2, HALF])
        acc = st.ps("acc", [P, 2, 2, BANK])
        w_in = [st.sem("gate_in"), st.sem("up_in")]
        split_hi = [st.sem("gate_hi"), st.sem("up_hi")]
        split_lo = [st.sem("gate_lo"), st.sem("up_lo")]
        acc_done = [st.sem("gate_done"), st.sem("up_done")]
        silu_done, prod_done, act_hi, act_lo = (st.sem(n) for n in ("silu_done", "prod_done", "act_hi", "act_lo"))
        views = [w.rearrange("(k p) (c n) -> p k c n", p=P, n=P) for w in (w_gate, w_up)]
        a_hi, a_lo = actT
        block = st.block()

        def at(a, f, half):
            return a[:, bass.ds(f, 1), half * HALF:(half + 1) * HALF].rearrange("p o n -> p (o n)")

        @block.sync
        def _(sp):
            def load(f, m, ahead=0):
                sp.dma_start(raw[:, m, :, :], views[m][:, :, ahead:, :][:, :, bass.ds(f, 1), :]
                             .rearrange("p k o n -> p k (o n)")).then_inc(w_in[m], 16)

            for m in range(2):
                load(0, m)
            with sp.Fori(0, NF - 1) as f:
                for m in range(2):
                    sp.wait_ge(split_hi[m], f + 1)
                    sp.wait_ge(split_lo[m], f + 1)
                    load(f, m, 1)

        @block.tensor
        def _(pe):
            def tile(f, first):
                for m in range(2):
                    pe.wait_ge(split_lo[m], f + 1)
                    if not first:
                        pe.wait_ge((silu_done, prod_done)[m], f * 2)
                    for k in range(KD):
                        for w, h in ((w_hi, hT[0]), (w_hi, hT[1]), (w_lo, hT[0])):
                            for half in range(2):
                                end = k == KD - 1 and w is w_lo
                                ins = nc.tensor.matmul(acc[:, m, half, :], w[:, m, k, :],
                                                       h[:, k, half * HALF:(half + 1) * HALF],
                                                       start=k == 0 and w is w_hi and h is hT[0], stop=end)
                                if end:
                                    ins.then_inc(acc_done[m], 1)

            tile(0, True)
            with pe.Fori(1, NF) as f:
                tile(f, False)

        @block.scalar
        def _(act):
            def split(f, m, first=False):
                act.wait_ge(w_in[m], f * 16 + 16)
                if not first:
                    act.wait_ge(acc_done[m], f * 2)
                nc.scalar.activation(w_hi[:, m, :, :], raw[:, m, :, :], ACT.Copy).then_inc(split_hi[m], 1)

            def tile(f, first, last):
                if not last:
                    split(f + 1, 0)
                for half in range(2):
                    act.wait_ge(acc_done[0], f * 2 + half + 1)
                    if not first:
                        act.wait_ge(act_lo, f * 2 + half - 1)
                    nc.scalar.activation(sg[:, half, :], acc[:, 0, half, :], ACT.Silu).then_inc(silu_done, 1)
                if not last:
                    split(f + 1, 1)
                for half in range(2):
                    act.wait_ge(prod_done, f * 2 + half + 1)
                    nc.scalar.activation(at(a_hi, f, half), sg[:, half, :], ACT.Copy).then_inc(act_hi, 1)

            split(0, 0, True)
            split(0, 1, True)
            tile(0, True, False)
            with act.Fori(1, NF - 1) as f:
                tile(f, False, False)
            tile(NF - 1, False, True)

        @block.vector
        def _(dve):
            def split(f, m):
                dve.wait_ge(split_hi[m], f + 1)
                nc.vector.tensor_tensor(w_lo[:, m, :, :], raw[:, m, :, :], w_hi[:, m, :, :].bitcast(F32),
                                        ALU.subtract).then_inc(split_lo[m], 1)

            def tile(f, last):
                if not last:
                    split(f + 1, 0)
                    split(f + 1, 1)
                for half in range(2):
                    dve.wait_ge(acc_done[1], f * 2 + half + 1)
                    dve.wait_ge(silu_done, f * 2 + half + 1)
                    nc.vector.tensor_tensor(sg[:, half, :], acc[:, 1, half, :], sg[:, half, :], ALU.mult).then_inc(prod_done, 1)
                for half in range(2):
                    dve.wait_ge(act_hi, f * 2 + half + 1)
                    nc.vector.tensor_tensor(at(a_lo, f, half), sg[:, half, :], at(a_hi, f, half).bitcast(F32),
                                            ALU.subtract).then_inc(act_lo, 1)

            split(0, 0)
            split(0, 1)
            with dve.Fori(0, NF - 1) as f:
                tile(f, False)
            tile(NF - 1, True)



def hgrn_stage(nc, proj, lb_logits, mixed, ident):
    HEADS, V, D8 = A_HEADS, A_WIDTH // A_HEADS, 8
    LEVELS = (64, 32, 16, 8)
    NL = len(LEVELS)
    BLK = SEQ // D8
    CB = P // D8
    width = [D8 - s for s in range(D8)]
    off = [BLK * sum(width[:s]) for s in range(D8 + 1)]
    TINY = 2.0 ** -64
    with Stage(nc, "hg") as st:
        qf = st.sb("qf", [P, 2, 2, TT, P])
        v = st.sb("v", [P, 2, TT, V])
        lb0 = st.sb("lb0", [P, HEADS])
        lbs = st.sb("lbs", [P, 6, HEADS])
        f = st.sb("f", [P, SEQ])
        q = st.sb("q", [P, SEQ])
        k = st.sb("k", [P, SEQ])
        b = st.sb("b", [P, SEQ])
        reset = st.sb("reset", [P, SEQ])
        qb2 = st.sb("qb", [P, 2, SEQ])
        decay2 = st.sb("decay", [P, 2, TT])
        kl2 = st.sb("kl", [P, 2, SEQ])
        lev2 = st.sb("lev", [P, 2, NL, SEQ])
        near2 = st.sb("near", [P, 2, off[D8]])
        pick = st.sb("pick", [P, D8, P])
        m_lev = st.sb("m_lev", [P, NL, P])
        m_near = st.sb("m_near", [P, P])
        sm = st.sb("sm", [P, 2, NL + 1, P])
        kt = st.sb("kt", [P, 2, P])
        state = st.sb("state", [P, 2, V])
        ps_tr = st.ps("ps_tr", [P, 2, BANK])
        ps_l = st.ps("ps_l", [P, 2, BANK])
        ps_n = st.ps("ps_n", [P, 1, BANK])
        ps_kb = st.ps("ps_k", [P, 1, BANK])
        ps_ub = st.ps("ps_u", [P, 1, BANK])
        ps_o = st.ps("ps_o", [P, 1, BANK])
        ps_k, ps_u = ps_kb[:, 0, 0:P], ps_ub[:, 0, 0:V]
        qf_in = [st.sem(f"qf_in{x}") for x in range(2)]
        v_in = [st.sem(f"v_in{x}") for x in range(2)]
        lb_in, lb_exp, lb_step, setup = st.sem("lb_in"), st.sem("lb_exp"), st.sem("lb_step"), st.sem("setup")
        tr_done, sig_done, f_done, q_done, k_done, lf_done, b_done = (
            st.sem(n) for n in ("tr_done", "sig_done", "f_done", "q_done", "k_done", "lf_done", "b_done"))
        diff_done, exp_done, g_done, near_k = st.sem("diff_done"), st.sem("exp_done"), st.sem("g_done"), st.sem("near_k")
        a_done, m_done, kt_done, o_done, u_done, state_done, o_taken = (
            st.sem(n) for n in ("a_done", "m_done", "kt_done", "o_done", "u_done", "state_done", "o_taken"))
        cols = lambda c0: proj[:, c0:c0 + A_WIDTH].rearrange("(t p) (i x v) -> p t i x v", p=P, x=2, v=V)
        q_cols, f_cols, v_cols = cols(0), cols(A_WIDTH), cols(2 * A_WIDTH)
        DIFFS = 1 + NL + 1
        EXPS = 1 + DIFFS
        PRODUCTS = 2 + NL + 1
        block = st.block()

        def halves(ap, h):
            w = ap.rearrange("p (n x h) -> p n x h", x=2, h=h)
            return w[:, :, 0, :], w[:, :, 1, :]

        def near_of(ap, s):
            w = ap.rearrange("p (n c) -> p n c", c=D8)
            return w[:, :, s:], w[:, :, s:s + 1].to_broadcast([P, BLK, width[s]])

        @block.sync
        def _(sp):
            with nc.allow_non_contiguous_dma(reason="a bound per partition"):
                sp.dma_start(lb0[:], lb_logits.rearrange("o (h k) -> k (o h)", k=P)).then_inc(lb_in, 16)

            def load_qf(it, x):
                for n, src in enumerate((f_cols, q_cols)):
                    sp.dma_start(qf[:, x, n, :, :], src[:, :, bass.ds(it, 1), x, :].rearrange("p t o v -> p t (o v)")).then_inc(qf_in[x], 16)

            def load_v(it, x):
                sp.dma_start(v[:, x, :, :], v_cols[:, :, bass.ds(it, 1), x, :].rearrange("p t o v -> p t (o v)")).then_inc(v_in[x], 16)

            for x in range(2):
                load_qf(0, x)
                load_v(0, x)
            with sp.Fori(1, HEADS // 2) as it:
                for x in range(2):
                    sp.wait_ge(tr_done, it * 4 + 2 * x - 2)
                    load_qf(it, x)
                    sp.wait_ge(u_done, it * (2 * TT) + (x + 1) * TT - 2 * TT)
                    load_v(it, x)

        @block.gpsimd
        def _(pool):
            nc.gpsimd.memset(reset[:], 1.0).then_inc(setup, 1)
            nc.gpsimd.memset(pick[:], 0.0).then_inc(setup, 1)
            nc.gpsimd.memset(m_lev[:], 0.0).then_inc(setup, 1)
            nc.gpsimd.memset(m_near[:], 1.0).then_inc(setup, 1)
            pool.wait_ge(setup, 4)
            nc.gpsimd.memset(reset[:].rearrange("p (c t) -> p c t", t=P)[:, :, 0], 0.0)
            for s in range(D8):
                nc.gpsimd.memset(pick[:, s, :].rearrange("p (n c) -> p n c", c=D8)[:, :, s], 1.0)
            for n, h in enumerate(LEVELS):
                nc.gpsimd.memset(halves(m_lev[:, n, :], h)[1], 1.0)
            ins = nc.gpsimd.memset(state[:], 0.0)
            ins.then_inc(setup, 1)
            pool.wait_ge(setup, 5)
            for n, h in enumerate(LEVELS):
                right = halves(m_lev[:, n, :], h)[1]
                nc.gpsimd.affine_select(out=right, in_=right, compare_op=ALU.is_ge, fill=0.0, base=0,
                                        pattern=[[-2 * h, P // (2 * h)], [0, h]], channel_multiplier=1).then_inc(setup, 1)
            near_m = m_near[:].rearrange("p (n c) -> p n c", c=D8)
            nc.gpsimd.affine_select(out=near_m, in_=near_m, compare_op=ALU.is_ge, fill=0.0, base=0,
                                    pattern=[[-D8, CB], [0, D8]], channel_multiplier=1).then_inc(setup, 1)
            pool.wait_ge(setup, 6 + NL)
            for n, h in enumerate(LEVELS):
                right = halves(m_lev[:, n, :], h)[1]
                nc.gpsimd.affine_select(out=right, in_=right, compare_op=ALU.is_ge, fill=0.0, base=h - 1,
                                        pattern=[[2 * h, P // (2 * h)], [0, h]], channel_multiplier=-1).then_inc(setup, 1)
            nc.gpsimd.affine_select(out=near_m, in_=near_m, compare_op=ALU.is_ge, fill=0.0, base=D8 - 1,
                                    pattern=[[D8, CB], [0, D8]], channel_multiplier=-1).then_inc(setup, 1)

        def heads(eng, prepare, chunk, tail):
            for part in range(TT):
                prepare(0, 0, part)

            def body(it, last):
                for x in range(2):
                    for c in range(TT):
                        chunk(it, x, c)
                        if x == 0:
                            prepare(it, 1, c)
                        elif not last:
                            prepare(it + 1, 0, c)
                    tail(it, x)

            with eng.Fori(0, HEADS // 2 - 1) as it:
                body(it, False)
            body(HEADS // 2 - 1, True)

        flat = ps_tr[:, :, :].rearrange("p a b -> p (a b)")

        @block.tensor
        def _(pe):
            def prepare(it, x, part):
                if part > 1:
                    return
                head = it * 2 + x
                if part == 0:
                    pe.wait_ge(qf_in[x], (it + 1) * 32)
                else:
                    pe.wait_ge(sig_done, head * 2 + 1)
                for t in range(TT):
                    ins = nc.tensor.transpose(ps_tr[:, t // 4, (t % 4) * P:(t % 4 + 1) * P], qf[:, x, part, t, :], ident[:])
                ins.then_inc(tr_done, 1)

            def scores(it, x, c):
                head = it * 2 + x
                if c >= 2:
                    pe.wait_ge(m_done, head * TT + c - 1)
                for n in range(NL):
                    g = lev2[:, x, n, c * P:(c + 1) * P]
                    nc.tensor.matmul(ps_l[:, c % 2, n * P:(n + 1) * P], g, g, start=True, stop=True)
                if c:
                    pe.wait_ge(m_done, head * TT + c)
                for s in range(D8):
                    pairs = near2[:, x, off[s]:off[s + 1]].rearrange("p (n c) -> p n c", c=width[s])[:, c * CB:(c + 1) * CB, :]
                    nc.tensor.matmul(ps_n[:, 0, 0:P].rearrange("p (n c) -> p n c", c=D8)[:, :, s:], pick[:, s, :], pairs,
                                     start=s == 0, stop=s == D8 - 1, skip_group_check=True)
                if c:
                    pe.wait_ge(kt_done, head * TT + c)
                nc.tensor.transpose(ps_k, kl2[:, x, c * P:(c + 1) * P], ident[:]).then_inc(a_done, 1)

            def outputs(it, x, c):
                head = it * 2 + x
                pe.wait_ge(m_done, head * TT + c + 1)
                if c:
                    pe.wait_ge(o_taken, head * TT + c)
                    pe.wait_ge(state_done, head * (TT - 1) + c)
                for n in range(NL + 1):
                    ins = nc.tensor.matmul(ps_o[:, 0, 0:V], sm[:, c % 2, n, :], v[:, x, c, :], start=n == 0,
                                           stop=c == 0 and n == NL)
                if c:
                    ins = nc.tensor.matmul(ps_o[:, 0, 0:V], qb2[:, x, c * P:(c + 1) * P], state[:, c % 2, :], start=False, stop=True)
                ins.then_inc(o_done, 1)
                pe.wait_ge(kt_done, head * TT + c + 1)
                nc.tensor.matmul(ps_u, kt[:, c % 2, :], v[:, x, c, :], start=True, stop=True).then_inc(u_done, 1)

            def chunk(it, x, c):
                if c == 0:
                    pe.wait_ge(v_in[x], (it + 1) * 16)
                    pe.wait_ge(setup, 7 + 2 * NL)
                    pe.wait_ge(g_done, (it * 2 + x + 1) * PRODUCTS)
                    scores(it, x, 0)
                if c + 1 < TT:
                    scores(it, x, c + 1)
                outputs(it, x, c)

            heads(pe, prepare, chunk, lambda it, x: None)

        @block.scalar
        def _(act):
            act.wait_ge(lb_step, 1)
            nc.scalar.activation(lbs[:, 1, :], lbs[:, 0, :], ACT.Exp).then_inc(lb_exp, 1)

            def prepare(it, x, part):
                head = it * 2 + x

                def exp_of(ap, n):
                    act.wait_ge(diff_done, head * DIFFS + 1 + n)
                    nc.scalar.activation(ap, ap, ACT.Exp).then_inc(exp_done, 1)

                if part == 0:
                    act.wait_ge(tr_done, head * 2 + 1)
                    nc.scalar.activation(f[:], flat, ACT.Sigmoid).then_inc(sig_done, 1)
                elif part == 1:
                    act.wait_ge(tr_done, head * 2 + 2)
                    nc.scalar.activation(q[:], flat, ACT.Sigmoid).then_inc(sig_done, 1)
                    act.wait_ge(f_done, head * 2 + 2)
                    nc.scalar.activation(f[:], f[:], ACT.Ln).then_inc(lf_done, 1)
                elif part == 2:
                    act.wait_ge(b_done, head + 1)
                    nc.scalar.activation(decay2[:, x, :], b[:].rearrange("p (c t) -> p c t", t=P)[:, :, P - 1], ACT.Exp)
                    nc.scalar.activation(qb2[:, x, :], b[:], ACT.Exp).then_inc(exp_done, 1)
                elif part == 3:
                    exp_of(kl2[:, x, :], 0)
                    for n in range(NL // 2):
                        exp_of(lev2[:, x, n, :], 1 + n)
                elif part == 4:
                    for n in range(NL // 2, NL):
                        exp_of(lev2[:, x, n, :], 1 + n)
                elif part == 5:
                    exp_of(near2[:, x, :], 1 + NL)

            def take(it, x, c):
                dst = mixed[:, :, 0:A_WIDTH].rearrange("p t (i x v) -> p t i x v", x=2, v=V)
                act.wait_ge(o_done, (it * 2 + x) * TT + c + 1)
                nc.scalar.activation(dst[:, c, bass.ds(it, 1), x, :].rearrange("p o v -> p (o v)"),
                                     ps_o[:, 0, 0:V], ACT.Copy).then_inc(o_taken, 1)

            def chunk(it, x, c):
                head = it * 2 + x
                act.wait_ge(a_done, head * TT + c + 1)
                if c >= 2:
                    act.wait_ge(u_done, head * TT + c - 1)
                nc.scalar.activation(kt[:, c % 2, :], ps_k, ACT.Copy).then_inc(kt_done, 1)
                if c:
                    take(it, x, c - 1)

            heads(act, prepare, chunk, lambda it, x: take(it, x, TT - 1))

        @block.vector
        def _(dve):
            dve.wait_ge(lb_in, 16)
            nc.vector.tensor_tensor(lbs[:, 0, :], lb0[:], lb0[:], ALU.subtract).then_inc(lb_step, 1)
            dve.wait_ge(lb_exp, 1)
            nc.vector.reciprocal(lbs[:, 2, :], lbs[:, 1, :]).then_inc(lb_step, 1)
            dve.wait_ge(lb_step, 2)
            nc.vector.tensor_tensor(lbs[:, 3, :], lbs[:, 1, :], lbs[:, 2, :], ALU.mult).then_inc(lb_step, 1)
            dve.wait_ge(lb_step, 3)
            nc.vector.tensor_tensor(lbs[:, 4, :], lbs[:, 3, :], lbs[:, 3, :], ALU.subtract).then_inc(lb_step, 1)
            dve.wait_ge(lb_step, 4)
            nc.vector.tensor_scalar(lbs[:, 5, :], lbs[:, 4, :], -1.0, 1.0, ALU.mult, ALU.add).then_inc(lb_step, 1)
            dve.wait_ge(lb_step, 5)
            dve.wait_ge(setup, 7 + 2 * NL)

            def prepare(it, x, part):
                head = it * 2 + x
                lb = lbs[:, 4, :].rearrange("p (i x) -> p i x", x=2)[:, bass.ds(it, 1), x]
                one_lb = lbs[:, 5, :].rearrange("p (i x) -> p i x", x=2)[:, bass.ds(it, 1), x]
                qb, kl, near = qb2[:, x, :], kl2[:, x, :], near2[:, x, :]

                def near_s(s):
                    return near[:, off[s]:off[s + 1]].rearrange("p (n c) -> p n c", c=width[s])

                def level_products(n):
                    h = LEVELS[n]
                    to_left, to_right = halves(lev2[:, x, n, :], h)
                    dve.wait_ge(exp_done, head * EXPS + 3 + n)
                    nc.vector.tensor_tensor(to_left, to_left, halves(k[:], h)[0], ALU.mult)
                    nc.vector.tensor_tensor(to_right, to_right, halves(q[:], h)[1], ALU.mult).then_inc(g_done, 1)

                if part == 0:
                    dve.wait_ge(sig_done, head * 2 + 1)
                    nc.vector.tensor_scalar(f[:], f[:], one_lb, lb, ALU.mult, ALU.add).then_inc(f_done, 1)
                    dve.wait_ge(f_done, head * 2 + 1)
                    nc.vector.tensor_scalar(k[:], f[:], -1.0, 1.0, ALU.mult, ALU.add).then_inc(k_done, 1)
                    dve.wait_ge(k_done, head + 1)
                    nc.vector.tensor_scalar(f[:], f[:], TINY, None, ALU.max).then_inc(f_done, 1)
                elif part == 1:
                    dve.wait_ge(sig_done, head * 2 + 2)
                    nc.vector.tensor_tensor(q[:], flat, q[:], ALU.mult).then_inc(q_done, 1)
                elif part == 2:
                    dve.wait_ge(lf_done, head + 1)
                    nc.vector.tensor_tensor_scan(b[:], reset[:], f[:], 0.0, ALU.mult, ALU.add).then_inc(b_done, 1)
                    dve.wait_ge(b_done, head + 1)
                    b3 = b[:].rearrange("p (c t) -> p c t", t=P)
                    nc.vector.tensor_tensor(kl.rearrange("p (c t) -> p c t", t=P), b3[:, :, P - 1:P].to_broadcast([P, TT, P]), b3,
                                            ALU.subtract).then_inc(diff_done, 1)
                    for n, h in enumerate(LEVELS):
                        left, right = halves(b[:], h)
                        to_left, to_right = halves(lev2[:, x, n, :], h)
                        middle = left[:, :, h - 1:h].to_broadcast([P, SEQ // (2 * h), h])
                        nc.vector.tensor_tensor(to_left, middle, left, ALU.subtract)
                        nc.vector.tensor_tensor(to_right, right, middle, ALU.subtract).then_inc(diff_done, 1)
                elif part == 3:
                    for s in range(D8):
                        behind, key = near_of(b[:], s)
                        ins = nc.vector.tensor_tensor(near_s(s), behind, key, ALU.subtract)
                    ins.then_inc(diff_done, 1)
                    dve.wait_ge(exp_done, head * EXPS + 1)
                    nc.vector.tensor_tensor(qb, qb, q[:], ALU.mult).then_inc(g_done, 1)
                elif part == 4:
                    dve.wait_ge(exp_done, head * EXPS + 2)
                    nc.vector.tensor_tensor(kl, kl, k[:], ALU.mult).then_inc(g_done, 1)
                    for n in range(NL // 2):
                        level_products(n)
                elif part == 5:
                    for n in range(NL // 2, NL):
                        level_products(n)
                elif part == 6:
                    dve.wait_ge(exp_done, head * EXPS + EXPS)
                    for s in range(D8):
                        ins = nc.vector.tensor_tensor(near_s(s), near_s(s), near_of(k[:], s)[1], ALU.mult)
                    ins.then_inc(near_k, 1)
                elif part == 7:
                    dve.wait_ge(near_k, head + 1)
                    for s in range(D8):
                        ins = nc.vector.tensor_tensor(near_s(s), near_s(s), near_of(q[:], s)[0], ALU.mult)
                    ins.then_inc(g_done, 1)

            def masks(it, x, c):
                head = it * 2 + x
                dve.wait_ge(a_done, head * TT + c + 1)
                if c >= 2:
                    dve.wait_ge(o_done, head * TT + c - 1)
                nc.vector.tensor_tensor(sm[:, c % 2, 0:NL, :], ps_l[:, c % 2, :].rearrange("p (n t) -> p n t", t=P),
                                        m_lev[:], ALU.mult)
                nc.vector.tensor_tensor(sm[:, c % 2, NL, :], ps_n[:, 0, 0:P], m_near[:], ALU.mult).then_inc(m_done, 1)

            def chunk(it, x, c):
                head = it * 2 + x
                if c == 0:
                    masks(it, x, 0)
                if c + 1 == TT:
                    return
                masks(it, x, c + 1)
                dve.wait_ge(u_done, head * TT + c + 1)
                if c == 0:
                    nc.vector.tensor_copy(state[:, 1, :], ps_u).then_inc(state_done, 1)
                else:
                    dve.wait_ge(state_done, head * (TT - 1) + c)
                    nc.vector.scalar_tensor_tensor(state[:, (c + 1) % 2, :], state[:, c % 2, :], decay2[:, x, c:c + 1], ps_u,
                                                   ALU.mult, ALU.add).then_inc(state_done, 1)

            heads(dve, prepare, chunk, lambda it, x: None)
    hgrn_out_stage(nc, proj, mixed)


def hgrn_out_stage(nc, proj, mixed):
    HEADS, V = A_HEADS, A_WIDTH // A_HEADS
    with Stage(nc, "hgo") as st:
        g = st.sb("g", [P, TT, A_WIDTH])
        sg = st.sb("sg", [P, TT, A_WIDTH])
        sq = st.sb("sq", [P, TT, A_WIDTH])
        ss = st.sb("ss", [P, TT, HEADS])
        ms = st.sb("ms", [P, TT, HEADS])
        root = st.sb("root", [P, TT, HEADS])
        rstd = st.sb("rstd", [P, TT, HEADS])
        g_in, sg_done, sq_done, norm, silu_done = (st.sem(n) for n in ("g_in", "sg_done", "sq_done", "norm", "silu_done"))
        block = st.block()
        o = mixed[:, :, 0:A_WIDTH]

        @block.sync
        def _(sp):
            sp.dma_start(g[:], proj[:, 3 * A_WIDTH:4 * A_WIDTH].rearrange("(t p) n -> p t n", p=P)).then_inc(g_in, 16)

        @block.scalar
        def _(act):
            nc.scalar.activation(sq[:], o, ACT.Square).then_inc(sq_done, 1)
            act.wait_ge(g_in, 16)
            nc.scalar.activation(sg[:], g[:], ACT.Sigmoid).then_inc(sg_done, 1)
            act.wait_ge(norm, 2)
            nc.scalar.activation(root[:], ms[:], ACT.Sqrt).then_inc(norm, 1)

        @block.vector
        def _(dve):
            dve.wait_ge(sq_done, 1)
            nc.vector.tensor_reduce(ss[:].rearrange("p t h -> p (t h)"), sq[:].rearrange("p t (h v) -> p (t h) v", v=V), AX.X, ALU.add)\
                .then_inc(norm, 1)
            dve.wait_ge(norm, 1)
            nc.vector.tensor_scalar(ms[:], ss[:], 1.0 / V, EPS, ALU.mult, ALU.add).then_inc(norm, 1)
            dve.wait_ge(sg_done, 1)
            nc.vector.tensor_tensor(sg[:], sg[:], g[:], ALU.mult).then_inc(silu_done, 1)
            dve.wait_ge(norm, 3)
            nc.vector.reciprocal(rstd[:], root[:]).then_inc(norm, 1)
            dve.wait_ge(norm, 4)
            o4 = o.rearrange("p t (h v) -> p t h v", v=V)
            nc.vector.tensor_tensor(o4, o4, rstd[:].rearrange("p t (h x) -> p t h x", x=1).to_broadcast([P, TT, HEADS, V]), ALU.mult)\
                .then_inc(norm, 1)
            dve.wait_ge(norm, 5)
            dve.wait_ge(silu_done, 1)
            nc.vector.tensor_tensor(o, o, sg[:], ALU.mult)



def heads_stage(nc, name, src, quads, ident):
    Q = 4
    whole = [n for n, q in enumerate(quads) if q[1] is not None]
    in_parts = [n for n, q in enumerate(quads) if q[2] is not None]
    with Stage(nc, name) as st:
        raw = st.sb("raw", [P, 2, TT, Q, HD])
        sq = st.sb("sq", [P, TT, Q, HD])
        tok = st.sb("tok", [P, 2, TT, Q, HA])
        outT = st.sb("outT", [HA, 2, Q, SEQ])
        out_hi, out_lo = (st.sb(n, [HA, Q, SEQ], F32R) for n in ("out_hi", "out_lo"))
        ss = st.sb("ss", [P, TT * Q])
        ms = st.sb("ms", [P, TT * Q])
        root = st.sb("root", [P, TT * Q])
        rstd = st.sb("rstd", [P, TT * Q])
        pos_i = st.sb("pos_i", [P, TT], I32)
        pos = st.sb("pos", [P, TT])
        gains = st.sb("gains", [HA, len(quads)])
        gsc = st.sb("gsc", [HA, len(quads)])
        tr = st.ps("tr", [HA, TT, BANK])
        raw_in = [st.sem(f"raw_in{s}") for s in range(2)]
        outT_out = [st.sem(f"outT_out{s}") for s in range(2)]
        hi_done, lo_done, parts_out = st.sem("hi_done"), st.sem("lo_done"), st.sem("parts_out")
        gain_in, setup, gsc_done = st.sem("gain_in"), st.sem("setup"), st.sem("gsc_done")
        sq_done, ss_done, ms_done, root_done, rstd_done = (
            st.sem(n) for n in ("sq_done", "ss_done", "ms_done", "root_done", "rstd_done"))
        aug_done, tok_done, tr_done = st.sem("aug_done"), st.sem("tok_done"), st.sem("tr_done")
        taken = [st.sem("taken_act"), st.sem("taken_dve")]
        normed = [n for n, q in enumerate(quads) if q[3] is not None]
        sv = src.rearrange("(t p) n -> p t n", p=P)
        block = st.block()

        @block.sync
        def _(sp):
            sp.wait_ge(setup, 1)
            with nc.allow_non_contiguous_dma(reason="a gain per partition"):
                for n in normed:
                    sp.dma_start(gains[0:HD, n:n + 1], quads[n][3].rearrange("(d o) -> d o", o=1)).then_inc(gain_in, 16)
            for n, (col, *_) in enumerate(quads):
                if n >= 2:
                    sp.wait_ge(tok_done, n - 1)
                sp.dma_start(raw[:, n % 2, :, :, :],
                             sv[:, :, col:col + Q * HD].rearrange("p t (h d) -> p t h d", d=HD)).then_inc(raw_in[n % 2], 16)

        @block.gpsimd
        def _(pool):
            nc.gpsimd.memset(gains[:], 1.0).then_inc(setup, 1)
            nc.gpsimd.iota(pos_i[:], pattern=[[P, TT]], base=0, channel_multiplier=1).then_inc(setup, 1)
            pool.wait_ge(setup, 2)
            nc.gpsimd.tensor_copy(pos[:], pos_i[:]).then_inc(setup, 1)
            pool.wait_ge(setup, 3)

            def aug(n):
                slopes, s = quads[n][5], n % 2
                if n >= 2:
                    pool.wait_ge(tr_done, (n - 1) * TT)
                for h in range(Q):
                    for r, ap in ((HD, tok[:, s, :, h, HD:HD + 1]), (HD + 1, tok[:, s, :, h, HD + 1:HA])):
                        ap = ap.rearrange("p t o -> p (t o)")
                        if slopes is not None and r == HD:
                            ins = nc.gpsimd.memset(ap, slopes[h])
                        elif slopes is not None:
                            ins = nc.gpsimd.tensor_scalar(ap, pos[:], -slopes[h], 1.0, ALU.mult, ALU.mult)
                        elif r == HD:
                            ins = nc.gpsimd.tensor_copy(ap, pos[:])
                        else:
                            ins = nc.gpsimd.memset(ap, 1.0)
                ins.then_inc(aug_done, 1)

            def store(n):
                dst, parts = quads[n][1:3]
                for who in range(2):
                    pool.wait_ge(taken[who], (n + 1) * (TT // 2))
                if dst is not None:
                    pool.dma_start(dst.rearrange("h r t -> r h t"), outT[:, n % 2, :, :]).then_inc(outT_out[n % 2], 16)
                if parts is not None:
                    pool.wait_ge(lo_done, in_parts.index(n) + 1)
                    for to, of in zip(parts, (out_hi, out_lo)):
                        pool.dma_start(to.rearrange("h r t -> r h t"), of[:].bitcast(F32)).then_inc(parts_out, 16)

            for n in range(len(quads) + 1):
                if n < len(quads):
                    aug(n)
                if n:
                    store(n - 1)
            for s in range(2):
                if any(n % 2 == s for n in whole):
                    pool.wait_ge(outT_out[s], 16 * sum(n % 2 == s for n in whole))
            if in_parts:
                pool.wait_ge(parts_out, 32 * len(in_parts))

        def take(eng, who, n):
            if n - 2 in whole:
                eng.wait_ge(outT_out[n % 2], 16 * sum(x % 2 == n % 2 for x in whole if x < n))
            if n - 2 in in_parts:
                eng.wait_ge(lo_done, in_parts.index(n - 2) + 1)
            if n == 0:
                eng.wait_ge(gsc_done, 1)
            for t in range(who, TT, 2):
                eng.wait_ge(tr_done, n * TT + t + 1)
                to, of = outT[:, n % 2, :, t * P:(t + 1) * P], tr[:, t, :].rearrange("r (h c) -> r h c", c=P)
                if who == 0:
                    nc.scalar.activation(to, of, ACT.Copy, scale=gsc[:, n:n + 1]).then_inc(taken[0], 1)
                else:
                    nc.vector.tensor_scalar(to, of, gsc[:, n:n + 1], None, ALU.mult).then_inc(taken[1], 1)

        @block.scalar
        def _(act):
            for n in range(len(quads) + 1):
                if n < len(quads) and n in normed:
                    i = normed.index(n)
                    act.wait_ge(raw_in[n % 2], 16 * (n // 2 + 1))
                    if i:
                        act.wait_ge(ss_done, i)
                    nc.scalar.activation(sq[:], raw[:, n % 2, :, :, :], ACT.Square).then_inc(sq_done, 1)
                    act.wait_ge(ms_done, i + 1)
                    nc.scalar.activation(root[:], ms[:], ACT.Sqrt).then_inc(root_done, 1)
                if n:
                    take(act, 0, n - 1)
                if n - 1 in in_parts:
                    i = in_parts.index(n - 1)
                    act.wait_ge(taken[0], n * (TT // 2))
                    act.wait_ge(taken[1], n * (TT // 2))
                    if i:
                        act.wait_ge(parts_out, 32 * i)
                    nc.scalar.activation(out_hi[:], outT[:, (n - 1) % 2, :, :], ACT.Copy).then_inc(hi_done, 1)

        @block.vector
        def _(dve):
            dve.wait_ge(gain_in, 16 * len(normed))
            for n, q in enumerate(quads):
                ins = nc.vector.tensor_scalar(gsc[0:HD, n:n + 1], gains[0:HD, n:n + 1], q[4], None, ALU.mult)
            nc.vector.tensor_copy(gsc[HD:HA, :], gains[HD:HA, :]).then_inc(gsc_done, 1)
            for n in range(len(quads) + 1):
                if n < len(quads):
                    s = n % 2
                    dve.wait_ge(raw_in[s], 16 * (n // 2 + 1))
                    if n in normed:
                        i = normed.index(n)
                        dve.wait_ge(sq_done, i + 1)
                        nc.vector.tensor_reduce(ss[:], sq[:].rearrange("p t h d -> p (t h) d"), AX.X, ALU.add)\
                            .then_inc(ss_done, 1)
                        dve.wait_ge(ss_done, i + 1)
                        nc.vector.tensor_scalar(ms[:], ss[:], 1.0 / HD, EPS, ALU.mult, ALU.add).then_inc(ms_done, 1)
                        dve.wait_ge(root_done, i + 1)
                        nc.vector.reciprocal(rstd[:], root[:]).then_inc(rstd_done, 1)
                        dve.wait_ge(rstd_done, i + 1)
                    if n >= 2:
                        dve.wait_ge(tr_done, (n - 1) * TT)
                    if n in normed:
                        nc.vector.tensor_tensor(
                            tok[:, s, :, :, 0:HD].rearrange("p t h d -> p (t h) d"),
                            raw[:, s, :, :, :].rearrange("p t h d -> p (t h) d"),
                            bcast(rstd[:].rearrange("p (a o) -> p a o", o=1), HD), ALU.mult).then_inc(tok_done, 1)
                    else:
                        nc.vector.tensor_copy(tok[:, s, :, :, 0:HD].rearrange("p t h d -> p (t h) d"),
                                              raw[:, s, :, :, :].rearrange("p t h d -> p (t h) d")).then_inc(tok_done, 1)
                if n:
                    take(dve, 1, n - 1)
                if n - 1 in in_parts:
                    dve.wait_ge(hi_done, in_parts.index(n - 1) + 1)
                    nc.vector.tensor_tensor(out_lo[:], outT[:, (n - 1) % 2, :, :], out_hi[:].bitcast(F32), ALU.subtract)\
                        .then_inc(lo_done, 1)

        @block.tensor
        def _(pe):
            for n in range(len(quads)):
                pe.wait_ge(tok_done, n + 1)
                pe.wait_ge(aug_done, n + 1)
                for t in range(TT):
                    if n:
                        pe.wait_ge(taken[t % 2], (n - 1) * (TT // 2) + t // 2 + 1)
                    for h in range(Q):
                        ins = nc.tensor.transpose(tr[:, t, h * P:(h + 1) * P], tok[:, n % 2, t, h, :], ident[:])
                    ins.then_inc(tr_done, 1)


def bias_parts_stage(nc, name, bias, rows, cols, ident):
    with Stage(nc, name) as st:
        tr = st.ps("tr", [P, 2, BANK])
        tr_done, hi_done = st.sem("tr_done"), st.sem("hi_done")
        block = st.block()
        hi, lo = cols

        @block.tensor
        def _(pe):
            for d in range(TT):
                at = SEQ - (d + 1) * P
                nc.tensor.transpose(tr[:, d // 4, (d % 4) * P:(d % 4 + 1) * P], bias[:, at:at + P], ident[:]).then_inc(tr_done, 1)

        @block.scalar
        def _(act):
            nc.scalar.activation(rows[:], bias[:], ACT.Copy)
            act.wait_ge(tr_done, TT)
            nc.scalar.activation(hi[:], tr[:, :, :].rearrange("p a b -> p (a b)"), ACT.Copy).then_inc(hi_done, 1)

        @block.vector
        def _(dve):
            if lo is not None:
                dve.wait_ge(hi_done, 1)
                nc.vector.tensor_tensor(lo[:], tr[:, :, :].rearrange("p a b -> p (a b)"), hi[:].bitcast(F32), ALU.subtract)


class Branch:

    def __init__(self, kT, v, group, rows, cols, at, span, gate0=0, selected=False):
        self.kT, self.v, self.group, self.rows, self.cols, self.at = kT, v, group, rows, [c for c in cols if c is not None], at
        self.span, self.gate0, self.selected = span, gate0, selected

    def runs(self, dists):
        out = []
        for pos, d in enumerate(dists):
            if d in self.at:
                if out and out[-1][0] + out[-1][1] == pos:
                    out[-1][1] += 1
                else:
                    out.append([pos, 1])
        return out


def attention_stage(nc, name, n_heads, qT, branches, mixed, col0, ident, gates=None, selT=None):
    NB = len(branches)
    S = 4
    W = S * P
    V1 = HD + 1
    SEL0 = 96
    SETS = 2
    per_head = branches[0].group == 1
    H = 2 if per_head else GROUP
    ROUNDS = n_heads // H
    units = [(hh if per_head else br, hh, br, strip) for br in range(NB) for hh in range(H) for strip in range(TT // S)]
    U = len(units)
    chunks, of_unit = [], []
    for u, (_, _, br, strip) in enumerate(units):
        own = range(strip * S, strip * S + S)
        keys = [own[0]] + [j for j in range(own[-1] + 1) if j != own[0] and j + branches[br].span > own[0]]
        of_unit.append(range(len(chunks), len(chunks) + len(keys)))
        chunks += [(u, j, max(j, own[0]), min(own[-1], j + branches[br].span - 1)) for j in keys]
    C = len(chunks)
    pieces, pieces_of = [], []
    for u, (_, _, br, strip) in enumerate(units):
        n0 = len(pieces)
        for x in range(S):
            i = strip * S + x
            k0 = max(0, i + 1 - branches[br].span)
            pieces += [(u, x, j, min(S, i + 1 - j), h) for h, j in enumerate(range(k0, i + 1, S))]
        pieces_of.append(range(n0, len(pieces)))
    M = len(pieces)
    last_of_set = [max(c for c in range(C) if units[chunks[c][0]][0] == s) + 1 for s in range(SETS)]
    last_of_head = [max(c for c in range(C) if units[chunks[c][0]][1] == h) + 1 for h in range(H)]
    AHEAD, EARLY = (4, 0) if branches[0].group == 1 else (5, 2)
    R = 6
    RB = 3
    n_q, n_k = 4 + (selT is not None), 7
    links = 1 if gates is None else 2
    with Stage(nc, name) as st:
        qa, qb = (st.sb(n, [P, H, SEQ], F32R) for n in ("qa", "qb"))
        ka, kb, kc = (st.sb(n, [P, SETS, SEQ], F32R) for n in ("ka", "kb", "kc"))
        v_raw = st.sb("v_raw", [P, SETS, TT, HD])
        v_hi, v_lo = (st.sb(n, [P, SETS, TT, V1], F32R) for n in ("v_hi", "v_lo"))
        base = st.sb("base", [P, SEQ])
        ident_r, minus_one = (st.sb(n, [P, P], F32R) for n in ("ident_r", "minus_one"))
        shift = st.sb("shift", [P, 2, W], F32R)
        top = st.sb("top", [P, U, 2, S])
        pr = st.sb("pr", [P, R, W])
        p_hi, p_lo = (st.sb(n, [P, R, W], F32R) for n in ("p_hi", "p_lo"))
        oT = st.sb("oT", [V1, 2, W])
        rl = st.sb("rl", [P, U, S])
        sc = st.sb("sc", [P, U, S])
        o_sb = st.sb("o", [P, S, HD])
        ps_m = st.ps("ps_m", [P, 2, BANK])
        ps_s = st.ps("ps_s", [P, RB, BANK])
        ps_o = st.ps("ps_o", [V1, 2, BANK])
        ps_t = st.ps("ps_t", [P, 1, BANK])
        q_in = [st.sem(f"q_in{h}") for h in range(H)]
        k_in = [st.sem(f"k_in{s}") for s in range(SETS)]
        v_in = [st.sem(f"v_in{s}") for s in range(SETS)]
        block_row, setup, m_done, piece_done, top_done, shift_done, s_done, p_done, hi_done, lo_done, pv_done, v_hi_done = (
            st.sem(n) for n in ("block_row", "setup", "m_done", "piece_done", "top_done", "shift_done", "s_done", "p_done", "hi_done",
                                "lo_done", "pv_done", "v_hi_done"))
        v_lo_done, oT_done, t_done, step, o_free = (st.sem(n) for n in ("v_lo_done", "oT_done", "t_done", "step", "o_free"))
        block = st.block()

        maxima_at = {step: [] for step in range(-C, C)}
        for u in range(U):
            before = of_unit[u - 1]
            room = before[:len(before) - len(before) // 4]
            for x, m in enumerate(pieces_of[u]):
                early = room[x * len(room) // len(pieces_of[u])] - AHEAD - EARLY
                if u == 0 or (per_head and units[u][3] == 0):
                    early = of_unit[u][0] - AHEAD - S + x * (S - 1) // S
                maxima_at[early].append(m)
        ends = {of_unit[u][-1]: u for u in range(U)}
        split_at = {min(of_unit[u][0] for u in range(U) if units[u][0] == s) - 3: s for s in range(SETS)}
        first_of_set = {min(of_unit[u][0] for u in range(U) if units[u][0] == s): s for s in range(SETS)}

        def kv_of(it, s):
            b = branches[0 if per_head else s]
            vv = b.v.rearrange("(t p) (g d) -> p t g d", p=P, d=HD)
            if per_head:
                keys = [part.rearrange("(i s) r t -> i s r t", s=2)[bass.ds(it, 1), s, :, :] for part in b.kT]
                vs = vv.rearrange("p t (i s) d -> p t i s d", s=2)[:, :, bass.ds(it, 1), s, :]
            else:
                g = it
                keys = [part[bass.ds(g, 1), :, :] for part in b.kT]
                vs = vv[:, :, bass.ds(g, 1), :]
            return [x.rearrange("o r t -> (o r) t") for x in keys], vs.rearrange("p t o d -> p t (o d)")

        def events(at, it, c, last):
            return [(it, x) for x in at.get(c, [])] + ([] if last else [(it + 1, x) for x in at.get(c - C, [])])

        def ahead(it, c, last):
            return [(it, c)] if c < C else [] if last else [(it + 1, c - C)]

        def ended(it, c, first):
            if c >= 0:
                return [(it, ends[c])] if c in ends else []
            return [(it - 1, ends[c + C])] if not first and c + C in ends else []

        def rounds(eng, body):
            body(0, True, False)
            with eng.Fori(1, ROUNDS - 1) as it:
                body(it, False, False)
            body(ROUNDS - 1, False, True)

        def cold(it, n, depth):
            return isinstance(it, int) and it == 0 and n < depth

        split_events = {c: [s] for c, s in split_at.items()}

        @block.sync
        def _(sp):
            def load_q(it, s):
                qv = [part.rearrange("(i s) r t -> i s r t", s=H)[bass.ds(it, 1), s, :, :].rearrange("o r t -> (o r) t")
                      for part in qT]
                for to, of in ((qa[0:HA, s, :], qv[0]), (qa[HA:HA + 2, s, :], qv[1][HD:HA, :]),
                               (qb[0:HD, s, :], qv[0][0:HD, :]), (qb[HD:P, s, :], qv[1][0:HD, :])):
                    sp.dma_start(to.bitcast(F32), of).then_inc(q_in[s], 16)
                if selT is not None:
                    blocks = selT[bass.ds(it, 1), :, :].rearrange("o r t -> (o r) t")
                    sp.dma_start(qa[SEL0:SEL0 + N_SLC, s, :].bitcast(F32), blocks).then_inc(q_in[s], 16)

            def load_k(it, s):
                hi, lo = kv_of(it, s)[0]
                for to, of in ((kc[0:HA, s, :], hi), (kc[HA:HA + 2, s, :], hi[HD:HA, :]),
                               (ka[0:HD, s, :], lo[0:HD, :]), (ka[HD:HA, s, :], hi[HD:HA, :]), (ka[HA:HA + 2, s, :], hi[HD:HA, :]),
                               (kb[0:HD, s, :], hi[0:HD, :]), (kb[HD:P, s, :], hi[0:HD, :])):
                    sp.dma_start(to.bitcast(F32), of).then_inc(k_in[s], 16)

            def load_v(it, s):
                sp.dma_start(v_raw[:, s, :, :], kv_of(it, s)[1]).then_inc(v_in[s], 16)

            sp.wait_ge(setup, 7)
            for s in range(H):
                load_q(0, s)
                if s < SETS:
                    load_k(0, s)
                    load_v(0, s)
            reload = sorted([(last_of_set[s], load, s) for s in range(SETS) for load in (load_k, load_v)] +
                            [(last_of_head[h], load_q, h) for h in range(H)], key=lambda r: r[0])
            with sp.Fori(1, ROUNDS) as it:
                for done, load, s in reload:
                    sp.wait_ge(pv_done, it * C + done - C)
                    load(it, s)

        @block.gpsimd
        def _(pool):
            nc.gpsimd.memset(base[:], 1.0).then_inc(block_row, 1)
            pool.wait_ge(block_row, 1)
            nc.gpsimd.affine_select(out=base[:], in_=base[:], compare_op=ALU.is_ge, fill=0.0, base=SLC * SEL0,
                                    pattern=[[1, SEQ]], channel_multiplier=-SLC).then_inc(block_row, 1)
            pool.wait_ge(block_row, 2)
            nc.gpsimd.affine_select(out=base[:], in_=base[:], compare_op=ALU.is_ge, fill=0.0, base=SLC - 1 - SLC * SEL0,
                                    pattern=[[-1, SEQ]], channel_multiplier=SLC).then_inc(block_row, 1)
            ident4 = ident[:].rearrange("p (o c) -> p o c", o=1).to_broadcast([P, S, P])

            with pool.Fori(0, ROUNDS) as it:
                for u in range(U):
                    pool.wait_ge(top_done, it * U + u + 1)
                    pool.nop(nofuse=True)
                    nc.gpsimd.tensor_tensor(shift[:, u % 2, :].rearrange("p (n c) -> p n c", c=P), ident4,
                                            bcast(top[:, u, 0, :].rearrange("p (n o) -> p n o", o=1), P), ALU.mult)\
                        .then_inc(shift_done, 1)

        @block.tensor
        def _(pe):
            pe.wait_ge(setup, 7)
            def maxima(it, m):
                u, x, j, w, _ = pieces[m]
                s, hh, br, strip = units[u]
                i = strip * S + x
                if m == pieces_of[u][0] and strip == 0:
                    pe.wait_ge(q_in[hh], (it + 1) * (16 * n_q))
                    pe.wait_ge(k_in[s], (it + 1) * (16 * n_k))
                if not cold(it, m, 2):
                    pe.wait_ge(piece_done, it * M + m - 1)
                parts = [(qa[:, hh, i * P:(i + 1) * P], kc[:, s, j * P:(j + w) * P], 0, w)]
                for pos, n in branches[br].runs([i - j - x for x in range(w)]):
                    at = SEQ - (i - j - pos + 1) * P
                    parts.append((ident_r[:], branches[br].rows[:, at:at + n * P], pos, n))
                for x, (lhsT, rhs, pos, n) in enumerate(parts):
                    ins = nc.tensor.matmul(ps_m[:, m % 2, pos * P:(pos + n) * P], lhsT, rhs, start=x == 0,
                                           stop=x == len(parts) - 1, skip_group_check=True)
                ins.then_inc(m_done, 1)

            def scores(it, c):
                u, j, i0, i1 = chunks[c]
                s, hh, br, strip = units[u]
                w = i1 - i0 + 1
                if c == of_unit[u][0]:
                    pe.wait_ge(shift_done, it * U + u + 1)
                if not cold(it, c, RB):
                    pe.wait_ge(p_done, it * C + c - RB + 1)
                tok, key = slice(i0 * P, (i1 + 1) * P), slice(j * P, (j + 1) * P)
                t0 = i0 - strip * S
                parts = [(kb[:, s, key], qb[:, hh, tok], 0, w), (ka[:, s, key], qa[:, hh, tok], 0, w),
                         (minus_one[:], shift[:, u % 2, t0 * P:(t0 + w) * P], 0, w)]
                for pos, n in branches[br].runs([i - j for i in range(i0, i1 + 1)]):
                    at = (i0 + pos - j) * P
                    parts += [(ident_r[:], x[:, at:at + n * P], pos, n) for x in branches[br].cols]
                for x, (lhsT, rhs, pos, n) in enumerate(parts):
                    ins = nc.tensor.matmul(ps_s[:, c % RB, pos * P:(pos + n) * P], lhsT, rhs, start=x == 0,
                                           stop=x == len(parts) - 1, skip_group_check=True)
                ins.then_inc(s_done, 1)

            def values(it, c):
                u, j, i0, i1 = chunks[c]
                s, hh, br, strip = units[u]
                w = (i1 - i0 + 1) * P
                t0 = (i0 - strip * S) * P
                if c in first_of_set:
                    pe.wait_ge(v_lo_done, it * SETS + s + 1)
                if c == of_unit[u][0] and not cold(it, u, 2):
                    pe.wait_ge(oT_done, it * U + u - 1)
                pe.wait_ge(lo_done, it * C + c + 1)
                for x, (vx, px) in enumerate(((v_hi, p_hi), (v_lo, p_hi), (v_hi, p_lo))):
                    ins = nc.tensor.matmul(ps_o[:, u % 2, t0:t0 + w], vx[:, s, j, :], px[:, c % R, 0:w],
                                           start=x == 0 and c == of_unit[u][0], stop=x == 2 and c == of_unit[u][-1],
                                           skip_group_check=True)
                ins.then_inc(pv_done, 1)

            def back(it, u):
                pe.wait_ge(oT_done, it * U + u + 1)
                pe.wait_ge(o_free, it * U + u + 1)
                for n in range(S):
                    ins = nc.tensor.transpose(ps_t[:, 0, n * V1:(n + 1) * V1], oT[:, u % 2, n * P:(n + 1) * P],
                                              ident[0:V1, 0:V1])
                ins.then_inc(t_done, 1)

            for c in range(-C, 0):
                for m in maxima_at[c]:
                    maxima(0, m)
                if c + AHEAD >= 0:
                    scores(0, c + AHEAD)

            def body(it, first, last):
                for c in range(C):
                    todo = events(maxima_at, it, c, last)
                    half = (len(todo) + 1) // 2
                    for i, m in todo[:half]:
                        maxima(i, m)
                    for i, n in ahead(it, c + AHEAD, last):
                        scores(i, n)
                    for i, m in todo[half:]:
                        maxima(i, m)
                    values(it, c)
                    for i, u in ended(it, c - 2, first):
                        back(i, u)
                if last:
                    back(it, U - 1)

            rounds(pe, body)

        @block.scalar
        def _(act):
            nc.scalar.activation(ident_r[:], ident[:], ACT.Copy).then_inc(setup, 1)
            act.wait_ge(block_row, 3)
            for s in range(SETS):
                for to in (ka, kc):
                    zero = 1.0 if branches[0 if per_head else s].selected else 0.0
                    nc.scalar.activation(to[HD:P, s, :], base[HD:P, :], ACT.Copy, scale=zero).then_inc(setup, 1)
            def exps(it, c):
                w = (chunks[c][3] - chunks[c][2] + 1) * P
                act.wait_ge(s_done, it * C + c + 1)
                if not cold(it, c, R):
                    act.wait_ge(lo_done, it * C + c - R + 1)
                nc.scalar.activation(pr[:, c % R, 0:w], ps_s[:, c % RB, 0:w], ACT.Exp).then_inc(p_done, 1)

            def high(it, c):
                w = (chunks[c][3] - chunks[c][2] + 1) * P
                act.wait_ge(p_done, it * C + c + 1)
                if not cold(it, c, R):
                    act.wait_ge(pv_done, it * C + c - R + 1)
                nc.scalar.activation(p_hi[:, c % R, 0:w], pr[:, c % R, 0:w], ACT.Copy).then_inc(hi_done, 1)

            def evacuate(it, u):
                act.wait_ge(pv_done, it * C + of_unit[u][-1] + 1)
                if not cold(it, u, 2):
                    act.wait_ge(t_done, it * U + u - 1)
                nc.scalar.activation(oT[:, u % 2, :], ps_o[:, u % 2, :], ACT.Copy).then_inc(oT_done, 1)

            def split(it, s):
                act.wait_ge(v_in[s], it * 16 + 16)
                nc.scalar.activation(v_hi[:, s, :, 0:HD], v_raw[:, s, :, :], ACT.Copy).then_inc(v_hi_done, 1)

            split(0, 0)
            for c in range(3):
                exps(0, c)
            high(0, 0)

            def body(it, first, last):
                for c in range(C):
                    for i, s in events(split_events, it, c, last):
                        split(i, s)
                    for i, n in ahead(it, c + 3, last):
                        exps(i, n)
                    for i, n in ahead(it, c + 1, last):
                        high(i, n)
                    for i, u in ended(it, c - 1, first):
                        evacuate(i, u)
                if last:
                    evacuate(it, U - 1)

            rounds(act, body)

        @block.vector
        def _(dve):
            nc.vector.memset(minus_one[:].bitcast(F32), -1.0).then_inc(setup, 1)
            for to, value in ((v_hi, 1.0), (v_lo, 0.0)):
                nc.vector.memset(to[:, :, :, HD:V1].bitcast(F32), value)
            nc.vector.memset(qa[HD:P, :, :].bitcast(F32), 0.0).then_inc(setup, 1)
            nc.vector.memset(o_sb[:], 0.0).then_inc(o_free, 1)
            def maximum(it, m):
                u, x, _, w, half = pieces[m]
                dve.wait_ge(m_done, it * M + m + 1)
                ins = nc.vector.tensor_reduce(top[:, u, half, x:x + 1], ps_m[:, m % 2, 0:w * P], AX.X, ALU.max)
                ins.then_inc(piece_done, 1)
                if m == pieces_of[u][-1]:
                    dve.wait_ge(piece_done, it * M + m + 1)
                    ins = nc.vector.tensor_tensor(top[:, u, 0, :], top[:, u, 0, :], top[:, u, half, :], ALU.max)
                    ins.then_inc(top_done, 1)

            def low(it, c):
                w = (chunks[c][3] - chunks[c][2] + 1) * P
                dve.wait_ge(hi_done, it * C + c + 1)
                nc.vector.tensor_tensor(p_lo[:, c % R, 0:w], pr[:, c % R, 0:w], p_hi[:, c % R, 0:w].bitcast(F32),
                                        ALU.subtract).then_inc(lo_done, 1)

            def output(it, u):
                _, hh, br, strip = units[u]
                done = (it * U + u) * links
                tiles = mixed[:, strip * S:(strip + 1) * S, col0:col0 + n_heads * HD]
                dst = tiles.rearrange("p t (i s d) -> p t i s d", s=H, d=HD)[:, :, bass.ds(it, 1), hh, :]
                dst = dst.rearrange("p t o d -> p t (o d)")
                bank = ps_t[:, 0, 0:S * V1].rearrange("p (t d) -> p t d", d=V1)
                dve.wait_ge(t_done, it * U + u + 1)
                nc.vector.reciprocal(rl[:, u, :], bank[:, :, HD]).then_inc(step, 1)
                dve.wait_ge(step, done + 1)
                if gates is None:
                    nc.vector.tensor_tensor(dst, bank[:, :, 0:HD], bcast(rl[:, u, :].rearrange("p (t o) -> p t o", o=1), HD),
                                            ALU.mult).then_inc(o_free, 1)
                    return
                g = gates[:, strip * S:(strip + 1) * S, branches[br].gate0:branches[br].gate0 + n_heads]
                g = g.rearrange("p t (i s) -> p t i s", s=H)[:, :, bass.ds(it, 1), hh].rearrange("p t o -> p (t o)")
                nc.vector.tensor_tensor(sc[:, u, :], rl[:, u, :], g, ALU.mult).then_inc(step, 1)
                dve.wait_ge(step, done + 2)
                nc.vector.tensor_tensor(o_sb[:], bank[:, :, 0:HD], bcast(sc[:, u, :].rearrange("p (t o) -> p t o", o=1), HD),
                                        ALU.mult).then_inc(o_free, 1)
                dve.wait_ge(o_free, it * U + u + 2)
                nc.vector.tensor_tensor(dst, o_sb[:], dst, ALU.add)

            def split(it, s):
                dve.wait_ge(v_hi_done, it * SETS + s + 1)
                nc.vector.tensor_tensor(v_lo[:, s, :, 0:HD], v_raw[:, s, :, :], v_hi[:, s, :, 0:HD].bitcast(F32),
                                        ALU.subtract).then_inc(v_lo_done, 1)

            for c in range(-C, 0):
                for m in maxima_at[c]:
                    maximum(0, m)
            split(0, 0)
            low(0, 0)

            def body(it, first, last):
                for c in range(C):
                    for i, s in events(split_events, it, c, last):
                        split(i, s)
                    for i, n in ahead(it, c + 1, last):
                        low(i, n)
                    for i, m in events(maxima_at, it, c, last):
                        maximum(i, m)
                    for i, u in ended(it, c - 3, first):
                        output(i, u)
                if last:
                    output(it, U - 1)

            rounds(dve, body)



def compress_stage(nc, kvT, pe, w1, w2, k_gain, gate_cols, kcT, vc, gates, ident):
    G = KV_HEADS
    NW = N_CMP
    with Stage(nc, "cmp") as st:
        t_in = st.sb("t_in", [HD, 2, G, SEQ])
        w1s = st.sb("w1s", [HD, 2, CMP_LEN, CMP_HIDDEN])
        w2s = st.sb("w2s", [CMP_HIDDEN, 2, HD])
        pes = st.sb("pes", [2 * CMP_LEN, HD])
        peT = st.sb("peT", [HD, 2 * CMP_LEN])
        gain = st.sb("gain", [HA, 1])
        g_raw = st.sb("g_raw", [P, TT, 3 * C_HEADS])
        pb = st.sb("pb", [CMP_HIDDEN, 2])
        hid = st.sb("hid", [CMP_HIDDEN, 2, G * NW])
        sq = st.sb("sq", [NW, G, HD])
        ss = st.sb("ss", [NW, G])
        ms = st.sb("ms", [NW, G])
        root = st.sb("root", [NW, G])
        rstd = st.sb("rstd", [NW, G])
        pos_i = st.sb("pos_i", [CMP_PAD, 1], I32)
        ktok = st.sb("ktok", [CMP_PAD, G, HA])
        ps_h = st.ps("ps_h", [CMP_HIDDEN, 2, BANK])
        ps_b = st.ps("ps_b", [CMP_HIDDEN, 2, BANK])
        ps_c = st.ps("ps_c", [CMP_PAD, 2, BANK])
        ps_t = st.ps("ps_t", [P, 1, BANK])
        pe_in, in_sem, g_in, gain_in = st.sem("pe_in"), st.sem("in"), st.sem("g_in"), st.sem("gain_in")
        peT_ready, peT_done, bias_ready, pb_done, hid_ready, hid_done, c_ready = (
            st.sem(x) for x in ("peT_ready", "peT_done", "bias_ready", "pb_done", "hid_ready", "hid_done", "c_ready"))
        norm, sq_done, ktok_set, ktok_done, tr_ready, gain_set = (
            st.sem(x) for x in ("norm", "sq_done", "ktok_set", "ktok_done", "tr_ready", "gain_set"))
        block = st.block()

        @block.sync
        def _(sp):
            sp.dma_start(pes[:], pe.rearrange("v l d -> (v l) d")).then_inc(pe_in, 16)
            for v in range(2):
                sp.dma_start(w1s[:, v, :, :], w1[v, :, :].rearrange("(l d) h -> d l h", d=HD)).then_inc(in_sem, 16)
                sp.dma_start(w2s[:, v, :], w2[v, :, :]).then_inc(in_sem, 16)
                sp.dma_start(t_in[:, v, :, :], kvT[v * G:(v + 1) * G, 0:HD, :].rearrange("g r t -> r g t")).then_inc(in_sem, 16)
            sp.dma_start(g_raw[:], gate_cols.rearrange("(t p) n -> p t n", p=P)).then_inc(g_in, 16)
            sp.wait_ge(gain_set, 1)
            with nc.allow_non_contiguous_dma(reason="a gain per partition"):
                sp.dma_start(gain[0:HD, :], k_gain.rearrange("(d o) -> d o", o=1)).then_inc(gain_in, 16)

        @block.gpsimd
        def _(pool):
            nc.gpsimd.memset(gain[:], 1.0).then_inc(gain_set, 1)
            nc.gpsimd.iota(pos_i[:], pattern=[[0, 1]], base=CMP_LEN - 1, channel_multiplier=CMP_STRIDE).then_inc(ktok_set, 1)
            nc.gpsimd.memset(ktok[:], 0.0).then_inc(ktok_set, 1)
            nc.gpsimd.memset(vc[:], 0.0).then_inc(ktok_set, 1)
            pool.wait_ge(ktok_set, 3)
            for g in range(G):
                nc.gpsimd.tensor_copy(ktok[:, g, HD:HD + 1], pos_i[:])
                ins = nc.gpsimd.memset(ktok[:, g, HD + 1:HA], 1.0)
            ins.then_inc(ktok_set, 1)

        @block.tensor
        def _(te):
            te.wait_ge(pe_in, 16)
            nc.tensor.transpose(ps_t[0:HD, 0, 0:2 * CMP_LEN], pes[:], ident[0:2 * CMP_LEN, 0:2 * CMP_LEN]).then_inc(peT_ready, 1)
            te.wait_ge(in_sem, 16 * 6)
            te.wait_ge(peT_done, 1)
            for v in range(2):
                for l in range(CMP_LEN):
                    ins = nc.tensor.matmul(ps_b[:, v, 0:1], w1s[:, v, l, :], peT[:, v * CMP_LEN + l:v * CMP_LEN + l + 1],
                                           start=l == 0, stop=l == CMP_LEN - 1)
                ins.then_inc(bias_ready, 1)
            for v in range(2):
                for l in range(CMP_LEN):
                    windows = t_in[:, v, :, l:l + CMP_STRIDE * (NW - 1) + 1:CMP_STRIDE]
                    ins = nc.tensor.matmul(ps_h[:, v, 0:G * NW].rearrange("p (g n) -> p g n", n=NW), w1s[:, v, l, :],
                                           windows, start=l == 0, stop=l == CMP_LEN - 1)
                ins.then_inc(hid_ready, 1)
            for v in range(2):
                te.wait_ge(hid_done, v + 1)
                for g in range(G):
                    ins = nc.tensor.matmul(ps_c[0:NW, v, g * HD:(g + 1) * HD], hid[:, v, g * NW:(g + 1) * NW], w2s[:, v, :],
                                           start=True, stop=True)
                ins.then_inc(c_ready, 1)
            te.wait_ge(ktok_done, 1)
            for g in range(G):
                ins = nc.tensor.transpose(ps_t[0:HA, 0, g * CMP_PAD:(g + 1) * CMP_PAD], ktok[:, g, :], ident[0:CMP_PAD, 0:CMP_PAD])
            ins.then_inc(tr_ready, 1)

        @block.scalar
        def _(act):
            act.wait_ge(bias_ready, 2)
            nc.scalar.activation(pb[:], ps_b[:, :, 0:1].rearrange("p v o -> p (v o)"), ACT.Copy).then_inc(pb_done, 1)
            act.wait_ge(pb_done, 1)
            for v in range(2):
                act.wait_ge(hid_ready, v + 1)
                nc.scalar.activation(hid[:, v, :], ps_h[:, v, 0:G * NW], ACT.Silu, bias=pb[:, v:v + 1]).then_inc(hid_done, 1)
            act.wait_ge(c_ready, 1)
            nc.scalar.activation(sq[:], ps_c[0:NW, 0, 0:G * HD].rearrange("p (g d) -> p g d", d=HD), ACT.Square)\
                .then_inc(sq_done, 1)
            act.wait_ge(norm, 2)
            nc.scalar.activation(root[:], ms[:], ACT.Sqrt).then_inc(norm, 1)
            act.wait_ge(g_in, 16)
            nc.scalar.activation(gates[:], g_raw[:], ACT.Sigmoid)

        @block.vector
        def _(dve):
            dve.wait_ge(peT_ready, 1)
            nc.vector.tensor_copy(peT[:], ps_t[0:HD, 0, 0:2 * CMP_LEN]).then_inc(peT_done, 1)
            dve.wait_ge(sq_done, 1)
            nc.vector.tensor_reduce(ss[:], sq[:], AX.X, ALU.add).then_inc(norm, 1)
            dve.wait_ge(norm, 1)
            nc.vector.tensor_scalar(ms[:], ss[:], 1.0 / HD, EPS, ALU.mult, ALU.add).then_inc(norm, 1)
            dve.wait_ge(norm, 3)
            nc.vector.reciprocal(rstd[:], root[:]).then_inc(norm, 1)
            dve.wait_ge(norm, 4)
            dve.wait_ge(ktok_set, 4)
            nc.vector.tensor_tensor(ktok[0:NW, :, 0:HD], ps_c[0:NW, 0, 0:G * HD].rearrange("p (g d) -> p g d", d=HD),
                                    bcast(rstd[:].rearrange("p (g o) -> p g o", o=1), HD), ALU.mult).then_inc(ktok_done, 1)
            dve.wait_ge(c_ready, 2)
            nc.vector.tensor_copy(vc[0:NW, :, :], ps_c[0:NW, 1, 0:G * HD].rearrange("p (g d) -> p g d", d=HD))
            dve.wait_ge(tr_ready, 1)
            dve.wait_ge(gain_in, 16)
            nc.vector.tensor_scalar(kcT[:], ps_t[0:HA, 0, 0:G * CMP_PAD].rearrange("p (g n) -> p g n", n=CMP_PAD),
                                    gain[:, 0:1], None, ALU.mult)


def select_stage(nc, qT, kcT, vc, gates, sel, mixed, ident):
    J = GROUP
    N = 2 * TT
    ROUNDS = KV_HEADS // 2
    FIRST = TOPN * SLC // P
    PICKED = 3e38
    FORCED = 1e30
    with Stage(nc, "sel") as st:
        q = st.sb("q", [HA, 2, J, SEQ])
        cmask = st.sb("cmask", [P, TT, CMP_PAD])
        force = st.sb("force", [P, TT, N_SLC])
        alive = st.sb("alive", [P, TT])
        s = st.sb("s", [P, 2, J, CMP_PAD])
        e = st.sb("e", [P, 2, J, CMP_PAD])
        pn = st.sb("pn", [P, 2, J, CMP_PAD])
        pt = st.sb("pt", [CMP_PAD, 2, J, P])
        nm = st.sb("nm", [P, 2, J])
        rowsum = st.sb("rowsum", [P, 2, J])
        rl = st.sb("rl", [P, 2, J])
        rla = st.sb("rla", [P, 2, J])
        both = st.sb("both", [P, 1 + CMP_PAD])
        quad = st.sb("quad", [P, N_SLC])
        imp = st.sb("imp", [P, N_SLC])
        score = st.sb("score", [P, N_SLC])
        top = st.sb("top", [P, 8])
        marked = st.sb("marked", [P, N_SLC])
        ps_s = st.ps("ps_s", [P, 2, BANK])
        ps_t = st.ps("ps_t", [CMP_PAD, 2, BANK])
        ps_o = st.ps("ps_o", [P, 2, BANK])
        in_sem = [st.sem(f"in{x}") for x in range(2)]
        setup, s_done, neg_done, e_done, pn_done, t_done, pt_done, o_done, o_taken, link, sel_link = (
            st.sem(x) for x in ("setup", "s_done", "neg_done", "e_done", "pn_done", "t_done", "pt_done", "o_done",
                                "o_taken", "link", "sel_link"))
        masked, force_set = st.sem("masked"), st.sem("force_set")
        picks = [n for n in range(N) if n % TT >= FIRST]
        qv = qT.rearrange("(i s j) r t -> i s r j t", s=2, j=J)
        block = st.block()

        @block.sync
        def _(sp):
            def load(it, x):
                for j in range(J):
                    sp.dma_start(q[:, x, j, :], qv[bass.ds(it, 1), x, :, j, :].rearrange("o r t -> (o r) t")).then_inc(in_sem[x], 16)

            for x in range(2):
                load(0, x)
            with sp.Fori(1, ROUNDS) as it:
                for x in range(2):
                    sp.wait_ge(s_done, it * N + (x + 1) * TT - N)
                    load(it, x)

        @block.gpsimd
        def _(pool):
            nc.gpsimd.memset(cmask[:], 0.0).then_inc(setup, 1)
            nc.gpsimd.memset(alive[:], 1.0).then_inc(setup, 1)
            nc.gpsimd.memset(both[:], 0.0).then_inc(setup, 1)
            nc.gpsimd.memset(sel[:], 0.0).then_inc(setup, 1)
            pool.wait_ge(setup, 4)
            nc.gpsimd.affine_select(out=cmask[:], in_=cmask[:], compare_op=ALU.is_ge, fill=NEG, base=-(CMP_LEN - 1),
                                    pattern=[[P, TT], [-CMP_STRIDE, CMP_PAD]], channel_multiplier=1).then_inc(setup, 1)
            nc.gpsimd.affine_select(out=alive[:], in_=alive[:], compare_op=ALU.is_ge, fill=0.0, base=-(CMP_LEN - 1),
                                    pattern=[[P, TT]], channel_multiplier=1).then_inc(setup, 1)

        @block.tensor
        def _(pe):
            with pe.Fori(0, ROUNDS) as it:
                def scores(n):
                    x, i = divmod(n, TT)
                    if i == 0:
                        pe.wait_ge(in_sem[x], (it + 1) * (16 * J))
                    if n >= 2:
                        pe.wait_ge(masked, it * N + n - 1)
                    for j in range(J):
                        ins = nc.tensor.matmul(ps_s[:, n % 2, j * CMP_PAD:(j + 1) * CMP_PAD], q[:, x, j, i * P:(i + 1) * P],
                                               kview(it, x), start=True, stop=True)
                    ins.then_inc(s_done, 1)

                def transposes(n):
                    pe.wait_ge(pn_done, it * N + n + 1)
                    if n >= 2:
                        pe.wait_ge(pt_done, it * N + n - 1)
                    pe.nop(nofuse=True)
                    for j in range(J):
                        ins = nc.tensor.transpose(ps_t[:, n % 2, j * P:(j + 1) * P], pn[:, n % 2, j, :], ident[:])
                    ins.then_inc(t_done, 1)

                def values(n):
                    x, i = divmod(n, TT)
                    pe.wait_ge(pt_done, it * N + n + 1)
                    if n >= 2:
                        pe.wait_ge(o_taken, it * N + n - 1)
                    pe.nop(nofuse=True)
                    for j in range(J):
                        ins = nc.tensor.matmul(ps_o[:, n % 2, j * HD:(j + 1) * HD], pt[:, n % 2, j, :], vview(it, x),
                                               start=True, stop=True)
                    ins.then_inc(o_done, 1)

                def kview(it, x):
                    return kcT[:, :, :].rearrange("p (i s) n -> p i s n", s=2)[:, bass.ds(it, 1), x, :].rearrange("p o n -> p (o n)")

                def vview(it, x):
                    return vc[:, :, :].rearrange("p (i s) n -> p i s n", s=2)[:, bass.ds(it, 1), x, :].rearrange("p o n -> p (o n)")

                scores(0)
                scores(1)
                for n in range(N):
                    transposes(n)
                    if n:
                        values(n - 1)
                    if n + 2 < N:
                        scores(n + 2)
                values(N - 1)

        @block.scalar
        def _(act):
            with act.Fori(0, ROUNDS) as it:
                for n in range(N + 1):
                    if n < N:
                        act.wait_ge(neg_done, it * N + n + 1)
                        for j in range(J):
                            ins = nc.scalar.activation(e[:, n % 2, j, :], s[:, n % 2, j, :], ACT.Exp,
                                                       bias=nm[:, n % 2, j:j + 1], accum_out=rowsum[:, n % 2, j:j + 1])
                        ins.then_inc(e_done, 1)
                    if n:
                        m = n - 1
                        act.wait_ge(t_done, it * N + m + 1)
                        if m >= 2:
                            act.wait_ge(o_done, it * N + m - 1)
                        nc.scalar.activation(pt[:, m % 2, :, :], ps_t[:, m % 2, :].rearrange("p (j c) -> p j c", c=P), ACT.Copy)\
                            .then_inc(pt_done, 1)

        @block.vector
        def _(dve):
            nc.vector.memset(force[:], 0.0).then_inc(force_set, 1)
            dve.wait_ge(force_set, 1)
            for i in range(FIRST, TT):
                for half in range(2):
                    cur = 2 * i + half
                    rows = slice(half * SLC, (half + 1) * SLC)
                    nc.vector.memset(force[rows, i, 0:1], FORCED)
                    ins = nc.vector.memset(force[rows, i, cur - 1:cur + 1], FORCED)
                    if cur + 1 < N_SLC:
                        ins = nc.vector.memset(force[rows, i, cur + 1:N_SLC], NEG)
            ins.then_inc(force_set, 1)
            dve.wait_ge(force_set, 2)
            dve.wait_ge(setup, 6)
            with dve.Fori(0, ROUNDS) as it:
                def negate(n):
                    i = n % TT
                    dve.wait_ge(s_done, it * N + n + 1)
                    nc.vector.tensor_tensor(s[:, n % 2, :, :], ps_s[:, n % 2, 0:J * CMP_PAD].rearrange("p (j c) -> p j c", c=CMP_PAD),
                                            cmask[:, i:i + 1, :].to_broadcast([P, J, CMP_PAD]), ALU.add).then_inc(masked, 1)
                    dve.wait_ge(masked, it * N + n + 1)
                    nc.vector.tensor_reduce(nm[:, n % 2, :], s[:, n % 2, :, :], AX.X, ALU.max, negate=True).then_inc(neg_done, 1)

                def normalize(n):
                    i = n % TT
                    dve.wait_ge(e_done, it * N + n + 1)
                    nc.vector.reciprocal(rl[:, n % 2, :], rowsum[:, n % 2, :]).then_inc(link, 1)
                    dve.wait_ge(link, it * (2 * N) + 2 * n + 1)
                    nc.vector.tensor_scalar(rla[:, n % 2, :], rl[:, n % 2, :], alive[:, i:i + 1], None, ALU.mult).then_inc(link, 1)
                    dve.wait_ge(link, it * (2 * N) + 2 * n + 2)
                    if n >= 2:
                        dve.wait_ge(t_done, it * N + n - 1)
                    nc.vector.tensor_tensor(pn[:, n % 2, :, :], e[:, n % 2, :, :],
                                            bcast(rla[:, n % 2, :].rearrange("p (j o) -> p j o", o=1), CMP_PAD),
                                            ALU.mult).then_inc(pn_done, 1)

                def pick(n):
                    i = n % TT
                    m = picks.index(n)
                    at = it * (7 * len(picks)) + 7 * m
                    dve.wait_ge(pn_done, it * N + n + 1)
                    nc.vector.tensor_reduce(both[:, 1:], pn[:, n % 2, :, :].rearrange("p j n -> p n j"), AX.X, ALU.add).then_inc(sel_link, 1)
                    dve.wait_ge(sel_link, at + 1)
                    nc.vector.tensor_reduce(quad[:], both[:, 1:].rearrange("p (m w) -> p m w", w=SLC // CMP_STRIDE), AX.X, ALU.add)\
                        .then_inc(sel_link, 1)
                    dve.wait_ge(sel_link, at + 2)
                    nc.vector.tensor_tensor(imp[:], quad[:], both[:, 0:CMP_PAD:SLC // CMP_STRIDE], ALU.add).then_inc(sel_link, 1)
                    dve.wait_ge(sel_link, at + 3)
                    nc.vector.tensor_tensor(score[:], imp[:], force[:, i, :], ALU.add).then_inc(sel_link, 1)
                    dve.wait_ge(sel_link, at + 4)
                    nc.vector.nop(nofuse=True)
                    nc.vector.max(top[:], score[:]).then_inc(sel_link, 1)
                    dve.wait_ge(sel_link, at + 5)
                    nc.vector.nop(nofuse=True)
                    nc.vector.match_replace(marked[:], top[:], score[:], PICKED).then_inc(sel_link, 1)
                    dve.wait_ge(sel_link, at + 6)
                    nc.vector.tensor_scalar(sel[:, :, i, :].rearrange("p (i s) n -> p i s n", s=2)[:, bass.ds(it, 1), n // TT, :]
                                            .rearrange("p o n -> p (o n)"), marked[:], PICKED, NEG, ALU.not_equal, ALU.mult)\
                        .then_inc(sel_link, 1)

                def output(n):
                    x, i = divmod(n, TT)
                    dve.wait_ge(o_done, it * N + n + 1)
                    dst = mixed[:, i, :].rearrange("p (i s j d) -> p i s j d", s=2, j=J, d=HD)[:, bass.ds(it, 1), x, :, :]
                    g = gates[:, i, 0:C_HEADS].rearrange("p (i s j) -> p i s j", s=2, j=J)[:, bass.ds(it, 1), x, :]
                    nc.vector.tensor_tensor(dst.rearrange("p o j d -> p (o j) d"),
                                            ps_o[:, n % 2, 0:J * HD].rearrange("p (j d) -> p j d", d=HD),
                                            bcast(g.rearrange("p o (j x) -> p (o j) x", x=1), HD), ALU.mult).then_inc(o_taken, 1)

                negate(0)
                negate(1)
                for n in range(N):
                    normalize(n)
                    if n in picks:
                        pick(n)
                    if n:
                        output(n - 1)
                    if n + 2 < N:
                        negate(n + 2)
                output(N - 1)


def dilated_bias_stage(nc, bias):
    reach = ((128, 1), (512, 4), (2048, 16))
    with Stage(nc, "dil") as st:
        d = st.sb("d", [P, SEQ], I32)
        r = st.sb("r", [P, SEQ], I32)
        df = st.sb("df", [P, SEQ])
        a = st.sb("a", [P, SEQ])
        b = st.sb("b", [P, SEQ])
        c = st.sb("c", [P, SEQ])
        step, iota_done = st.sem("step"), st.sem("iota_done")
        block = st.block()

        @block.gpsimd
        def _(pool):
            nc.gpsimd.iota(d[:], pattern=[[-1, SEQ]], base=SEQ - P, channel_multiplier=1).then_inc(iota_done, 1)
            pool.wait_ge(step, 15)
            nc.gpsimd.affine_select(out=bias[:], in_=a[:], compare_op=ALU.is_ge, fill=NEG, base=SEQ - P,
                                    pattern=[[-1, SEQ]], channel_multiplier=1)

        @block.vector
        def _(dve):
            dve.wait_ge(iota_done, 1)
            nc.vector.tensor_copy(df[:], d[:]).then_inc(step, 1)
            dve.wait_ge(step, 1)
            nc.vector.tensor_scalar(c[:], df[:], float(reach[0][0]), None, ALU.is_le).then_inc(step, 1)
            for n, (window, dilation) in enumerate(reach[1:]):
                at = 2 + 4 * n
                nc.vector.tensor_scalar(r[:], d[:], dilation - 1, None, ALU.bitwise_and).then_inc(step, 1)
                dve.wait_ge(step, at + 1)
                nc.vector.tensor_scalar(a[:], r[:], 0.0, None, ALU.is_equal).then_inc(step, 1)
                dve.wait_ge(step, at + 2)
                nc.vector.scalar_tensor_tensor(b[:], df[:], float(window), a[:], ALU.is_le, ALU.mult).then_inc(step, 1)
                dve.wait_ge(step, at + 3)
                nc.vector.tensor_tensor(c[:], c[:], b[:], ALU.add).then_inc(step, 1)
                dve.wait_ge(step, at + 4)
            nc.vector.tensor_scalar(a[:], c[:], 0.0, NEG, ALU.is_equal, ALU.mult).then_inc(step, 1)
            for n, count in enumerate((2, 3)):
                at = 11 + 2 * n
                nc.vector.tensor_scalar(b[:], c[:], float(count), math.log(count), ALU.is_equal, ALU.mult).then_inc(step, 1)
                dve.wait_ge(step, at + 1)
                nc.vector.tensor_tensor(a[:], a[:], b[:], ALU.add).then_inc(step, 1)
                dve.wait_ge(step, at + 2)


def distance_bias_stage(nc, causal, window):
    with Stage(nc, "dist") as st:
        step = st.sem("step")
        block = st.block()

        @block.gpsimd
        def _(pool):
            nc.gpsimd.memset(causal[:], 0.0).then_inc(step, 1)
            pool.wait_ge(step, 1)
            nc.gpsimd.affine_select(out=causal[:], in_=causal[:], compare_op=ALU.is_ge, fill=NEG, base=SEQ - P,
                                    pattern=[[-1, SEQ]], channel_multiplier=1).then_inc(step, 1)
            pool.wait_ge(step, 2)
            nc.gpsimd.affine_select(out=window[:], in_=causal[:], compare_op=ALU.is_ge, fill=NEG, base=WIN - 1 - (SEQ - P),
                                    pattern=[[1, SEQ]], channel_multiplier=-1)


def transposed_selection_stage(nc, sel, selT, ident):
    with Stage(nc, "selT") as st:
        blocks = st.sb("blocks", [N_SLC, KV_HEADS, SEQ], F32R)
        tr = st.ps("tr", [N_SLC, KV_HEADS, 2 * BANK])
        tr_done, taken, stored = st.sem("tr_done"), st.sem("taken"), st.sem("stored")
        block = st.block()

        @block.tensor
        def _(pe):
            for g in range(KV_HEADS):
                for t in range(TT):
                    ins = nc.tensor.transpose(tr[:, g, t * P:(t + 1) * P], sel[:, g, t, :], ident[:])
                ins.then_inc(tr_done, 1)

        @block.scalar
        def _(act):
            for g in range(KV_HEADS):
                act.wait_ge(tr_done, g + 1)
                nc.scalar.activation(blocks[:, g, :], tr[:, g, :], ACT.Copy).then_inc(taken, 1)

        @block.gpsimd
        def _(pool):
            pool.wait_ge(taken, KV_HEADS)
            pool.dma_start(selT.rearrange("g b t -> b g t"), blocks[:].bitcast(F32)).then_inc(stored, 16)
            pool.wait_ge(stored, 16)


def store_stage(nc, x_sb, out):
    with Stage(nc, "store") as st:
        x_out = st.sem("x_out")
        block = st.block()

        @block.sync
        def _(sp):
            sp.dma_start(out.rearrange("o (t p) d -> p (o t) d", p=P), x_sb[:]).then_inc(x_out, 16)
            sp.wait_ge(x_out, 16)


def trunk(nc, x, attn_norm, ffn_norm, hy_w_in, hy_lb_logits, hy_o_gain, hy_q_gain, hy_k_gain, hy_w_out, nsa_w_in,
          nsa_q_gain, nsa_k_gain, nsa_cmp_pe, nsa_cmp_w1, nsa_cmp_w2, nsa_w_out, ffn_w_gate, ffn_w_up, ffn_w_down, out):
    def slopes(n, first, count):
        return [2.0 ** (-8.0 * (h + 1) / n) for h in range(first, first + count)]

    def dram(name, shape):
        return nc.dram_tensor(name, shape, F32).ap()

    def dram_parts(name, shape):
        return [dram(f"{name}_{part}", shape) for part in ("hi", "lo")]

    def some(parts, first, count=4):
        return [part[first:first + count, :, :] for part in parts]

    proj0 = dram("proj0", (SEQ, EVEN_IN))
    q0T, k0T = dram_parts("q0T", (B_HEADS, HA, SEQ)), dram_parts("k0T", (B_HEADS, HA, SEQ))
    proj1 = dram("proj1", (SEQ, ODD_IN))
    q1T = dram("q1T", (C_HEADS, HA, SEQ))
    q1T_parts = dram_parts("q1T", (C_HEADS, HA, SEQ))
    kvT = dram("kvT", (2 * KV_HEADS, HA, SEQ))
    k1T = dram_parts("k1T", (2 * KV_HEADS, HA, SEQ))
    selT = dram("selT", (KV_HEADS, N_SLC, SEQ))
    Q = 4 * HD

    with ExitStack() as whole:
        def sb(ctx, name, shape, dt=F32):
            return ctx.enter_context(nc.sbuf_tensor(name, shape, dt))

        def parts(ctx, name, shape):
            return [ctx.enter_context(nc.sbuf_tensor(f"{name}_{part}", shape, F32R)) for part in ("hi", "lo")]

        x_sb = sb(whole, "x_sb", [P, TT, DM])
        ident = sb(whole, "ident", [P, P])
        load_stage(nc, x, x_sb, ident)

        def ffn(layer):
            with ExitStack() as c:
                hT = parts(c, f"ffn_hT{layer}", [P, KD, SEQ])
                transpose_stage(nc, f"fn{layer}", x_sb, hT, [(ffn_norm[layer, :], 0, DM)], ident, True)
                for n, (f0, groups) in enumerate(((0, (2, 2, 2, 2)), (8, (2, 2, 2, 2)), (16, (3, 3)))):
                    lo, hi = f0 * P, (f0 + sum(groups)) * P
                    with ExitStack() as c2:
                        actT = parts(c2, f"actT{layer}_{n}", [P, sum(groups), SEQ])
                        ffn_stage(nc, f"up{layer}_{n}", hT, ffn_w_gate[layer, :, lo:hi], ffn_w_up[layer, :, lo:hi], actT)
                        linear_stage(nc, f"down{layer}_{n}", actT, ffn_w_down[layer, lo:hi, :], groups, BANK, add_to=x_sb)

        with ExitStack() as c:
            hT = parts(c, "hT0", [P, KD, SEQ])
            transpose_stage(nc, "an0", x_sb, hT, [(attn_norm[0, :], 0, DM)], ident, True)
            linear_stage(nc, "in0", hT, hy_w_in[0, :, :], (4, 4), BANK, dst_dram=proj0)
        with ExitStack() as c:
            mixed = sb(c, "mixed0", [P, TT, DM])
            hgrn_stage(nc, proj0, hy_lb_logits, mixed, ident)
            with ExitStack() as c2:
                rows, cols = sb(c2, "dil_rows", [P, SEQ], F32R), parts(c2, "dil_cols", [P, SEQ])
                with ExitStack() as c3:
                    bias = sb(c3, "dil_bias", [P, SEQ])
                    dilated_bias_stage(nc, bias)
                    bias_parts_stage(nc, "dil_parts", bias, rows, cols, ident)
                at = 4 * A_WIDTH
                quads = [(at + Q * n, None, some(q0T, 4 * n), hy_q_gain[0, :], HD ** -0.5, slopes(B_HEADS, 4 * n, 4))
                         for n in range(2)]
                at += B_HEADS * HD
                quads += [(at + Q * n, None, some(k0T, 4 * n), hy_k_gain[0, :], 1.0, None) for n in range(2)]
                heads_stage(nc, "heads0", proj0, quads, ident)
                at += B_HEADS * HD
                dilated = Branch(k0T, proj0[:, at:at + B_HEADS * HD], 1, rows, cols, range(TT), TT)
                attention_stage(nc, "at0", B_HEADS, q0T, [dilated], mixed, A_WIDTH, ident)
            mT = parts(c, "mT0", [P, KD, SEQ])
            transpose_stage(nc, "mt0", mixed, mT, [(hy_o_gain[0, :], 0, A_WIDTH)], ident, False)
            linear_stage(nc, "out0", mT, hy_w_out[0, :, :], (4, 4), BANK, add_to=x_sb)
        ffn(0)

        with ExitStack() as c:
            hT = parts(c, "hT1", [P, KD, SEQ])
            transpose_stage(nc, "an1", x_sb, hT, [(attn_norm[1, :], 0, DM)], ident, True)
            linear_stage(nc, "in1", hT, nsa_w_in[0, :, :], (4, 4), ODD_IN // 8, dst_dram=proj1)
        main = DM + 6 * KV_W
        with ExitStack() as c:
            mixed = sb(c, "mixed1", [P, TT, DM])
            with ExitStack() as c2:
                gates = sb(c2, "gates", [P, TT, 3 * C_HEADS])
                kcT = sb(c2, "kcT", [HA, KV_HEADS, CMP_PAD])
                vc = sb(c2, "vc", [CMP_PAD, KV_HEADS, HD])
                sel = sb(c2, "sel", [P, KV_HEADS, TT, N_SLC])
                masks = []
                for mask in ("causal", "window"):
                    masks.append((sb(c2, f"{mask}_rows", [P, SEQ], F32R), [sb(c2, f"{mask}_cols", [P, SEQ], F32R), None]))
                with ExitStack() as c3:
                    causal, window = sb(c3, "causal", [P, SEQ]), sb(c3, "window", [P, SEQ])
                    distance_bias_stage(nc, causal, window)
                    bias_parts_stage(nc, "causal_parts", causal, *masks[0], ident)
                    bias_parts_stage(nc, "window_parts", window, *masks[1], ident)
                quads = [(Q * n, q1T[4 * n:4 * n + 4, :, :], some(q1T_parts, 4 * n), nsa_q_gain[0, :],
                          HD ** -0.5, slopes(C_HEADS, 4 * n, 4)) for n in range(4)]
                quads += [(DM, kvT[0:4, :, :], None, None, 1.0, None), (DM + KV_W, kvT[4:8, :, :], None, None, 1.0, None),
                          (DM + 2 * KV_W, None, some(k1T, 0), nsa_k_gain[0, 1, :], 1.0, None),
                          (DM + 4 * KV_W, None, some(k1T, 4), nsa_k_gain[0, 2, :], 1.0, None)]
                heads_stage(nc, "heads1", proj1, quads, ident)
                compress_stage(nc, kvT, nsa_cmp_pe[0, :, :, :], nsa_cmp_w1[0, :, :, :], nsa_cmp_w2[0, :, :, :],
                               nsa_k_gain[0, 0, :], proj1[:, main:ODD_IN], kcT, vc, gates, ident)
                select_stage(nc, q1T, kcT, vc, gates, sel, mixed, ident)
                vs, vw = DM + 3 * KV_W, DM + 5 * KV_W
                transposed_selection_stage(nc, sel, selT, ident)
                picked = Branch(some(k1T, 0), proj1[:, vs:vs + KV_W], GROUP, *masks[0], (0,), TT, C_HEADS, True)
                near = Branch(some(k1T, 4), proj1[:, vw:vw + KV_W], GROUP, *masks[1], (0, WIN // P), WIN // P + 1, 2 * C_HEADS)
                attention_stage(nc, "at1", C_HEADS, q1T_parts, [picked, near], mixed, 0, ident, gates=gates, selT=selT)
            mT = parts(c, "mT1", [P, KD, SEQ])
            transpose_stage(nc, "mt1", mixed, mT, [], ident, False)
            linear_stage(nc, "out1", mT, nsa_w_out[0, :, :], (4, 4), BANK, add_to=x_sb)
        ffn(1)
        store_stage(nc, x_sb, out)


_INS = ["x", "attn_norm", "ffn_norm", "hy_w_in", "hy_lb_logits", "hy_o_gain", "hy_q_gain", "hy_k_gain", "hy_w_out",
        "nsa_w_in", "nsa_q_gain", "nsa_k_gain", "nsa_cmp_pe", "nsa_cmp_w1", "nsa_cmp_w2", "nsa_w_out",
        "ffn_w_gate", "ffn_w_up", "ffn_w_down"]


def kernel(**inputs):
    import concourse.bacc as _bacc
    from concourse.bass_utils import run_bass_kernel_spmd as _run

    nc = _bacc.Bacc("TRN2", target_bir_lowering=False, num_devices=1)
    arrays, args = {}, []
    for name in _INS:
        a = np.ascontiguousarray(inputs[name])
        arrays[f"in_{name}"] = a
        args.append(nc.dram_tensor(f"in_{name}", a.shape, mybir.dt.from_np(a.dtype), kind="ExternalInput").ap())
    args.append(nc.dram_tensor("out_x", (1, SEQ, DM), F32, kind="ExternalOutput").ap())
    trunk(nc, *args)
    return _run(nc, [arrays], core_ids=[0]).results[0]["out_x"]
```
